# Optimizing a Trainium2 kernel written in Bass

```python
import math
import jax, jax.numpy as jnp
from jax import lax
import numpy as np

D_MODEL = 1024
BATCH = 1
SEQ = 256
DEPTH = 1

HEAD_DIM = 64
BLK = 128
A_GROUPS = ((128, 1), (512, 4), (2048, 16))
A_HEADS = 4
B_Q_HEADS = 8
B_KV_HEADS = 2
B_WINDOW = 128
C_HEADS = 4
N_BRANCH = 3
NUM_BUCKETS = 32
MAX_DISTANCE = max(w for w, _ in A_GROUPS)
D_FF = 4 * D_MODEL
CONV_WIDTH = 3
EPS = 1e-6

A_WIDTH = A_HEADS * HEAD_DIM
B_WIDTH = B_Q_HEADS * HEAD_DIM
C_WIDTH = C_HEADS * HEAD_DIM
B_GROUP = B_Q_HEADS // B_KV_HEADS
N_A_GROUP_HEADS = len(A_GROUPS) * A_HEADS
N_BIAS_HEADS = N_A_GROUP_HEADS + B_Q_HEADS
A_QKV_COLS = 3 * N_A_GROUP_HEADS * HEAD_DIM
B_Q_COLS = B_WIDTH
B_KV_COLS = 2 * B_KV_HEADS * HEAD_DIM
C_QKV_COLS = 3 * C_WIDTH
GATE_COLS = N_BRANCH * D_MODEL
OFF_B_Q = A_QKV_COLS
OFF_B_KV = OFF_B_Q + B_Q_COLS
OFF_C = OFF_B_KV + B_KV_COLS
OFF_GATE = OFF_C + C_QKV_COLS
IN_COLS = OFF_GATE + GATE_COLS
SCALE = HEAD_DIM ** -0.5


def rms_norm(x, g):
    xf = x.astype(jnp.float32)
    y = xf * lax.rsqrt(jnp.mean(xf * xf, axis=-1, keepdims=True) + EPS)
    return (y * g.astype(jnp.float32)).astype(x.dtype)

def t5_bucket(dist):
    max_exact = NUM_BUCKETS // 2
    nf = jnp.maximum(dist, 1).astype(jnp.float32)
    large = max_exact + (jnp.log(nf / max_exact) / math.log(MAX_DISTANCE / max_exact)
                         * (NUM_BUCKETS - max_exact)).astype(jnp.int32)
    large = jnp.minimum(large, NUM_BUCKETS - 1)
    return jnp.where(dist < max_exact, dist, large)

def band_layout(n_blocks, max_dist):
    a = jnp.arange(BLK)[:, None]
    b = jnp.arange(2 * BLK)[None, :]
    dist = a + BLK - b
    in_band = (dist >= 0) & (dist <= max_dist)
    key_exists = (jnp.arange(n_blocks)[:, None] > 0) | (jnp.arange(2 * BLK)[None, :] >= BLK)
    mask = in_band[None] & key_exists[:, None, :]
    return jnp.maximum(dist, 0), mask

def band_bias(table, dist):
    return jnp.transpose(table[t5_bucket(dist)], (2, 0, 1)).astype(jnp.float32)

def banded_attention(q, k, v, bias, mask):
    n, hkv, g, L, dh = q.shape
    nb = L // BLK
    qb = q.reshape(n, hkv, g, nb, BLK, dh)

    def two_blocks(t):
        tb = t.reshape(n, hkv, nb, BLK, dh)
        prev = jnp.pad(tb, ((0, 0), (0, 0), (1, 0), (0, 0), (0, 0)))[:, :, :nb]
        return jnp.concatenate([prev, tb], axis=3)

    kw, vw = two_blocks(k), two_blocks(v)
    logits = jnp.einsum('nkgbqd,nkbsd->nkgbqs', qb, kw, preferred_element_type=jnp.float32) * SCALE
    logits = jnp.where(mask, logits + bias[:, :, None], -jnp.inf)
    m = jnp.max(logits, axis=-1)
    p = jnp.exp(logits - m[..., None])
    l = jnp.sum(p, axis=-1)
    num = jnp.einsum('nkgbqs,nkbsd->nkgbqd', p, vw.astype(jnp.float32))
    return num.reshape(n, hkv, g, L, dh), m.reshape(n, hkv, g, L), l.reshape(n, hkv, g, L)

def to_sub(t, d, lp):
    b, s, h, dh = t.shape
    L = s // d
    t = t.reshape(b, L, d, h, dh).transpose(0, 2, 3, 1, 4).reshape(b * d, h, L, dh)
    return jnp.pad(t, ((0, 0), (0, 0), (0, lp - L), (0, 0)))

def dilated_attention(q, k, v, table_a):
    b, s = q.shape[:2]
    nums, ms, ls = [], [], []
    for gi, (window, d) in enumerate(A_GROUPS):
        L = s // d
        lp = -(-L // BLK) * BLK
        dist, mask = band_layout(lp // BLK, window // d)
        bias = band_bias(table_a[:, gi], dist * d)[:, None]
        num, m, l = banded_attention(to_sub(q[:, :, gi], d, lp)[:, :, None],
                                     to_sub(k[:, :, gi], d, lp), to_sub(v[:, :, gi], d, lp), bias, mask)
        num = num[:, :, 0, :L].reshape(b, d, A_HEADS, L, HEAD_DIM).transpose(0, 3, 1, 2, 4)
        nums.append(num.reshape(b, s, A_HEADS, HEAD_DIM))
        ms.append(m[:, :, 0, :L].reshape(b, d, A_HEADS, L).transpose(0, 3, 1, 2).reshape(b, s, A_HEADS))
        ls.append(l[:, :, 0, :L].reshape(b, d, A_HEADS, L).transpose(0, 3, 1, 2).reshape(b, s, A_HEADS))
    nums = jnp.stack(nums, axis=2)
    ms = jnp.stack(ms, axis=2)
    ls = jnp.stack(ls, axis=2)
    c = jnp.exp(ms - jnp.max(ms, axis=2, keepdims=True))
    out = jnp.sum(c[..., None] * nums, axis=2) / jnp.sum(c * ls, axis=2)[..., None]
    return out.reshape(b, s, A_WIDTH).astype(q.dtype)

def sliding_window_gqa(q, k, v, sinks, table_b):
    b, s = q.shape[:2]
    dist, mask = band_layout(s // BLK, B_WINDOW - 1)
    bias = band_bias(table_b, dist).reshape(B_KV_HEADS, B_GROUP, BLK, 2 * BLK)
    qh = q.reshape(b, s, B_KV_HEADS, B_GROUP, HEAD_DIM).transpose(0, 2, 3, 1, 4)
    num, m, l = banded_attention(qh, k.transpose(0, 2, 1, 3), v.transpose(0, 2, 1, 3), bias, mask)
    sink = sinks.reshape(B_KV_HEADS, B_GROUP)[None, :, :, None].astype(jnp.float32)
    mx = jnp.maximum(m, sink)
    c = jnp.exp(m - mx)
    out = num * (c / (l * c + jnp.exp(sink - mx)))[..., None]
    return out.transpose(0, 3, 1, 2, 4).reshape(b, s, B_WIDTH).astype(q.dtype)

def stick_breaking_attention(q, k, v):
    b, s = q.shape[:2]
    qh, kh, vh = (t.transpose(0, 2, 1, 3) for t in (q, k, v))
    outs = []
    for i in range(s // BLK):
        lo, hi = i * BLK, (i + 1) * BLK
        z = jnp.einsum('bhqd,bhsd->bhqs', qh[:, :, lo:hi], kh[:, :, :hi],
                       preferred_element_type=jnp.float32) * SCALE
        before = jnp.arange(hi)[None, :] < jnp.arange(lo, hi)[:, None]
        log_keep = jnp.where(before, jax.nn.log_sigmoid(-z), 0.0)
        log_rest = lax.cumsum(log_keep, axis=3, reverse=True) - log_keep
        wts = jnp.where(before, jnp.exp(jax.nn.log_sigmoid(z) + log_rest), 0.0)
        outs.append(jnp.einsum('bhqs,bhsd->bhqd', wts, vh[:, :, :hi].astype(jnp.float32)))
    out = jnp.concatenate(outs, axis=2).transpose(0, 2, 1, 3)
    return out.reshape(b, s, C_WIDTH).astype(q.dtype)

def hybrid_mixer(h, rel_bias, w_in, b_gate, sinks, w_br_a, w_br_b, w_br_c, w_out):
    b, s, _ = h.shape
    proj = h @ w_in
    a_qkv, b_q, b_kv, c_qkv, gates = jnp.split(proj, [OFF_B_Q, OFF_B_KV, OFF_C, OFF_GATE], axis=-1)
    a_qkv = a_qkv.reshape(b, s, 3, len(A_GROUPS), A_HEADS, HEAD_DIM)
    table_a = rel_bias[:, :N_A_GROUP_HEADS].reshape(NUM_BUCKETS, len(A_GROUPS), A_HEADS)
    o_a = dilated_attention(a_qkv[:, :, 0], a_qkv[:, :, 1], a_qkv[:, :, 2], table_a)
    b_kv = b_kv.reshape(b, s, 2, B_KV_HEADS, HEAD_DIM)
    o_b = sliding_window_gqa(b_q.reshape(b, s, B_Q_HEADS, HEAD_DIM), b_kv[:, :, 0], b_kv[:, :, 1],
                             sinks, rel_bias[:, N_A_GROUP_HEADS:])
    c_qkv = c_qkv.reshape(b, s, 3, C_HEADS, HEAD_DIM)
    o_c = stick_breaking_attention(c_qkv[:, :, 0], c_qkv[:, :, 1], c_qkv[:, :, 2])
    g = jax.nn.sigmoid(gates.reshape(b, s, N_BRANCH, D_MODEL) + b_gate)
    merged = g[:, :, 0] * (o_a @ w_br_a) + g[:, :, 1] * (o_b @ w_br_b) + g[:, :, 2] * (o_c @ w_br_c)
    return merged @ w_out

def conv_ffn(h, w_up, conv_w, conv_b, w_down):
    u = h @ w_up
    u = lax.conv_general_dilated(u, conv_w[:, None, :], window_strides=(1,),
                                 padding=[(CONV_WIDTH - 1, 0)],
                                 dimension_numbers=('NWC', 'WIO', 'NWC'),
                                 feature_group_count=u.shape[-1]) + conv_b
    gate, val = jnp.split(u, 2, axis=-1)
    return (jax.nn.gelu(gate, approximate=True) * val) @ w_down

def first_inputs(seed: int = 0) -> dict:
    key = jax.random.key(seed)
    ks = jax.random.split(key, 17)

    def nrm(k, shape, scale):
        return jax.random.normal(k, shape, jnp.float32) * scale

    def gain(k):
        return 1.0 + nrm(k, (DEPTH, D_MODEL), 0.1)

    return {
        'x': nrm(ks[0], (BATCH, SEQ, D_MODEL), 1.0),
        'rel_bias': nrm(ks[1], (NUM_BUCKETS, N_BIAS_HEADS), 0.5),
        'attn_pre_norm': gain(ks[2]),
        'w_in': nrm(ks[3], (DEPTH, D_MODEL, IN_COLS), D_MODEL ** -0.5),
        'b_gate': nrm(ks[4], (DEPTH, N_BRANCH, D_MODEL), 0.1),
        'sinks': nrm(ks[5], (DEPTH, B_Q_HEADS), 0.5),
        'w_br_a': nrm(ks[6], (DEPTH, A_WIDTH, D_MODEL), A_WIDTH ** -0.5),
        'w_br_b': nrm(ks[7], (DEPTH, B_WIDTH, D_MODEL), B_WIDTH ** -0.5),
        'w_br_c': nrm(ks[8], (DEPTH, C_WIDTH, D_MODEL), C_WIDTH ** -0.5),
        'w_out': nrm(ks[9], (DEPTH, D_MODEL, D_MODEL), D_MODEL ** -0.5),
        'attn_post_norm': gain(ks[10]),
        'ffn_pre_norm': gain(ks[11]),
        'w_up': nrm(ks[12], (DEPTH, D_MODEL, 2 * D_FF), D_MODEL ** -0.5),
        'conv_w': nrm(ks[13], (DEPTH, CONV_WIDTH, 2 * D_FF), CONV_WIDTH ** -0.5),
        'conv_b': nrm(ks[14], (DEPTH, 2 * D_FF), 0.02),
        'w_down': nrm(ks[15], (DEPTH, D_FF, D_MODEL), D_FF ** -0.5),
        'ffn_post_norm': gain(ks[16]),
    }

def first_block(x, rel_bias, attn_pre_norm, w_in, b_gate, sinks, w_br_a, w_br_b, w_br_c, w_out,
              attn_post_norm, ffn_pre_norm, w_up, conv_w, conv_b, w_down, ffn_post_norm):
    for layer in range(DEPTH):
        h = rms_norm(x, attn_pre_norm[layer])
        h = hybrid_mixer(h, rel_bias, w_in[layer], b_gate[layer], sinks[layer],
                         w_br_a[layer], w_br_b[layer], w_br_c[layer], w_out[layer])
        x = x + rms_norm(h, attn_post_norm[layer])
        h = rms_norm(x, ffn_pre_norm[layer])
        h = conv_ffn(h, w_up[layer], conv_w[layer], conv_b[layer], w_down[layer])
        x = x + rms_norm(h, ffn_post_norm[layer])
    return x


DEPTH_2 = 2

GRID_W = 64
CTX_LEN = 256

ATT_HEADS = 8
ATT_HEAD_DIM = 64
ATT_QK_DIM = ATT_HEADS * 2 * ATT_HEAD_DIM
ATT_V_DIM = ATT_HEADS * 2 * ATT_HEAD_DIM
Q_BLOCK = 128
ROPE_BASE = 10000.0
ROPE_PAIRS = ATT_HEAD_DIM // 4

SSD_D_INNER = 2 * D_MODEL
SSD_HEAD_DIM = 64
SSD_HEADS = SSD_D_INNER // SSD_HEAD_DIM
SSD_GROUPS = 8
SSD_STATE = 128
SSD_CONV = 5
SSD_CHUNK = 128
SSD_CONV_DIM = SSD_D_INNER + 2 * SSD_GROUPS * SSD_STATE

D_FF_2 = 4 * D_MODEL

N_BRANCH_2 = 2
N_MOD = 6
IN_DIM = 2 * ATT_QK_DIM + ATT_V_DIM + SSD_D_INNER + SSD_CONV_DIM + 2 * SSD_HEADS + N_BRANCH_2 * D_MODEL


def rmsnorm(x, g, eps=1e-6):
    xf = x.astype(jnp.float32)
    y = xf * lax.rsqrt(jnp.mean(xf * xf, axis=-1, keepdims=True) + eps)
    return (y * g.astype(jnp.float32)).astype(x.dtype)

def modulate(x, g, shift, scale):
    return rmsnorm(x, g) * (1 + scale) + shift

def in_proj_split(t):
    sizes = (ATT_QK_DIM, ATT_QK_DIM, ATT_V_DIM, SSD_D_INNER, SSD_CONV_DIM,
             SSD_HEADS, SSD_HEADS, D_MODEL, D_MODEL)
    idx, acc = [], 0
    for s in sizes[:-1]:
        acc += s
        idx.append(acc)
    return jnp.split(t, idx, axis=-1)

def axial_rope(n_tok):
    rows = n_tok // GRID_W
    row = jnp.broadcast_to(jnp.arange(rows)[:, None], (rows, GRID_W)).reshape(-1).astype(jnp.float32)
    col = jnp.broadcast_to(jnp.arange(GRID_W)[None, :], (rows, GRID_W)).reshape(-1).astype(jnp.float32)
    inv = jnp.float32(ROPE_BASE) ** (-jnp.arange(ROPE_PAIRS, dtype=jnp.float32) / ROPE_PAIRS)
    ang = jnp.concatenate([row[:, None] * inv, col[:, None] * inv], axis=-1)
    return jnp.cos(ang), jnp.sin(ang)

def apply_rope(x, cos, sin):
    half = x.shape[-1] // 2
    x1 = x[..., :half].astype(jnp.float32)
    x2 = x[..., half:].astype(jnp.float32)
    c = cos[:, None, None, :]
    s = sin[:, None, None, :]
    return jnp.concatenate([x1 * c - x2 * s, x1 * s + x2 * c], axis=-1).astype(x.dtype)

def diff_attend(q, k, v, lam):
    s = jnp.einsum('bqhcd,bkhcd->bchqk', q, k).astype(jnp.float32) * (ATT_HEAD_DIM ** -0.5)
    p = jax.nn.softmax(s, axis=-1)
    a = p[:, 0] - lam * p[:, 1]
    return jnp.einsum('bhqk,bkhe->bqhe', a.astype(v.dtype), v)

def diff_attention(q_l, k_l, v_l, q_c, k_c, v_c, lam, lam_init, subln_g, with_ctx_out):
    b, n, h = q_l.shape[:3]
    k_all = jnp.concatenate([k_l, k_c], axis=1)
    v_all = jnp.concatenate([v_l, v_c], axis=1)
    nb = n // Q_BLOCK
    qb = jnp.moveaxis(q_l.reshape(b, nb, Q_BLOCK, h, 2, ATT_HEAD_DIM), 1, 0)
    o_l = lax.map(lambda qq: diff_attend(qq, k_all, v_all, lam), qb)
    o_l = jnp.moveaxis(o_l, 0, 1).reshape(b, n, h, 2 * ATT_HEAD_DIM)

    def post(o):
        return (rmsnorm(o, subln_g) * (1.0 - lam_init)).reshape(o.shape[0], o.shape[1], ATT_V_DIM)

    o_c = post(diff_attend(q_c, k_c, v_c, lam)) if with_ctx_out else None
    return post(o_l), o_c

def dwconv_silu(x, w, bias):
    kw = w.shape[0]
    y = lax.conv_general_dilated(x, w.astype(x.dtype)[:, None, :], window_strides=(1,),
                                 padding=[(kw // 2, kw // 2)],
                                 dimension_numbers=('NWC', 'WIO', 'NWC'),
                                 feature_group_count=x.shape[-1])
    return jax.nn.silu(y + bias)

def ssd_chunked(x, dt, a, bm, cm, h0, need_y):
    f32 = jnp.float32
    out_dtype = x.dtype
    b, n, h, p = x.shape
    g, ns = bm.shape[2], bm.shape[3]
    r = h // g
    nc = n // SSD_CHUNK
    dt = dt.astype(f32)
    xc = (x.astype(f32) * dt[..., None]).reshape(b, nc, SSD_CHUNK, g, r, p)
    cs = jnp.cumsum((dt * a.astype(f32)).reshape(b, nc, SSD_CHUNK, g, r), axis=2)
    bc = bm.astype(f32).reshape(b, nc, SSD_CHUNK, g, ns)
    cc = cm.astype(f32).reshape(b, nc, SSD_CHUNK, g, ns)
    decay_to_end = jnp.exp(cs[:, :, -1:] - cs)
    chunk_states = jnp.einsum('bclgn,bclgr,bclgrp->bcgrpn', bc, decay_to_end, xc)
    chunk_decay = jnp.exp(cs[:, :, -1])

    def step(hc, inp):
        st, dec = inp
        return hc * dec[..., None, None] + st, hc

    h_last, h_in = lax.scan(step, h0.astype(f32),
                            (jnp.moveaxis(chunk_states, 1, 0), jnp.moveaxis(chunk_decay, 1, 0)))
    if not need_y:
        return None, h_last
    h_in = jnp.moveaxis(h_in, 0, 1)
    seg = cs[:, :, :, None] - cs[:, :, None, :]
    lower = jnp.tril(jnp.ones((SSD_CHUNK, SSD_CHUNK), dtype=bool))[:, :, None, None]
    lmat = jnp.exp(jnp.where(lower, seg, -jnp.inf))
    cb = jnp.einsum('bclgn,bcsgn->bclsg', cc, bc)
    y = (jnp.einsum('bclsg,bclsgr,bcsgrp->bclgrp', cb, lmat, xc)
         + jnp.einsum('bclgn,bcgrpn,bclgr->bclgrp', cc, h_in, jnp.exp(cs)))
    return y.reshape(b, n, h, p).astype(out_dtype), h_last

def ssd_inputs(xbc_raw, dtf_raw, dtb_raw, conv_w, conv_b, dt_bias_f, dt_bias_b):
    xbc = dwconv_silu(xbc_raw, conv_w, conv_b)
    xs, bm, cm = jnp.split(xbc, [SSD_D_INNER, SSD_D_INNER + SSD_GROUPS * SSD_STATE], axis=-1)
    b, n = xs.shape[:2]
    xs = xs.reshape(b, n, SSD_HEADS, SSD_HEAD_DIM)
    bm = bm.reshape(b, n, SSD_GROUPS, SSD_STATE)
    cm = cm.reshape(b, n, SSD_GROUPS, SSD_STATE)
    dt_f = jax.nn.softplus((dtf_raw + dt_bias_f).astype(jnp.float32))
    dt_b = jax.nn.softplus((dtb_raw + dt_bias_b).astype(jnp.float32))
    return xs, bm, cm, dt_f, dt_b

def ssd_output(yf, yb, xs, z, ssd_d, ssd_norm_g, w_ssd_o):
    b, n = xs.shape[:2]
    y = (yf + yb + ssd_d[:, None] * xs).reshape(b, n, SSD_D_INNER)
    return rmsnorm(y * jax.nn.silu(z), ssd_norm_g) @ w_ssd_o

def hybrid_mixer_2(h_l, h_c, cos, sin, w_in, conv_w, conv_b, dt_bias_f, dt_bias_b, a_log_f, a_log_b,
                 ssd_d, ssd_norm_g, lam, lam_init, subln_g, w_attn_o, w_ssd_o, w_out, with_ctx_out):
    ql, kl, vl, zl, xbcl, dtfl, dtbl, gal, gsl = in_proj_split(h_l @ w_in)
    qc, kc, vc, zc, xbcc, dtfc, dtbc, gac, gsc = in_proj_split(h_c @ w_in)

    def qk(t):
        return t.reshape(t.shape[0], t.shape[1], ATT_HEADS, 2, ATT_HEAD_DIM)

    def vv(t):
        return t.reshape(t.shape[0], t.shape[1], ATT_HEADS, 2 * ATT_HEAD_DIM)

    att_l, att_c = diff_attention(apply_rope(qk(ql), cos, sin), apply_rope(qk(kl), cos, sin), vv(vl),
                                  qk(qc), qk(kc), vv(vc), lam, lam_init, subln_g, with_ctx_out)

    a_f = -jnp.exp(a_log_f.astype(jnp.float32))
    a_b = -jnp.exp(a_log_b.astype(jnp.float32))
    rev = lambda t: jnp.flip(t, axis=1)
    xs_c, bm_c, cm_c, dtf_c, dtb_c = ssd_inputs(xbcc, dtfc, dtbc, conv_w, conv_b, dt_bias_f, dt_bias_b)
    xs_l, bm_l, cm_l, dtf_l, dtb_l = ssd_inputs(xbcl, dtfl, dtbl, conv_w, conv_b, dt_bias_f, dt_bias_b)
    b = h_l.shape[0]
    h0 = jnp.zeros((b, SSD_GROUPS, SSD_HEADS // SSD_GROUPS, SSD_HEAD_DIM, SSD_STATE), jnp.float32)
    yc_f, st_f = ssd_chunked(xs_c, dtf_c, a_f, bm_c, cm_c, h0, with_ctx_out)
    yc_b, st_b = ssd_chunked(rev(xs_c), rev(dtb_c), a_b, rev(bm_c), rev(cm_c), h0, with_ctx_out)
    yl_f, _ = ssd_chunked(xs_l, dtf_l, a_f, bm_l, cm_l, st_f, True)
    yl_b, _ = ssd_chunked(rev(xs_l), rev(dtb_l), a_b, rev(bm_l), rev(cm_l), st_b, True)
    ssd_l = ssd_output(yl_f, rev(yl_b), xs_l, zl, ssd_d, ssd_norm_g, w_ssd_o)

    def merge(att, ssd, ga, gs):
        return (jax.nn.sigmoid(ga) * (att @ w_attn_o) + jax.nn.sigmoid(gs) * ssd) @ w_out

    o_l = merge(att_l, ssd_l, gal, gsl)
    o_c = None
    if with_ctx_out:
        ssd_c = ssd_output(yc_f, rev(yc_b), xs_c, zc, ssd_d, ssd_norm_g, w_ssd_o)
        o_c = merge(att_c, ssd_c, gac, gsc)
    return o_l, o_c

def sq_relu_mlp(h, w1, w2):
    return jnp.square(jax.nn.relu(h @ w1)) @ w2

def second_inputs(seed: int = 0) -> dict:
    key = jax.random.key(seed)
    ks = jax.random.split(key, 32)
    f32 = jnp.float32

    def nrm(k, shape, scale):
        return jax.random.normal(k, shape, f32) * scale

    def gain(k, shape):
        return 1.0 + 0.05 * jax.random.normal(k, shape, f32)

    dt = jnp.exp(jax.random.uniform(ks[10], (DEPTH_2, 2, SSD_HEADS), f32,
                                    math.log(1e-3), math.log(1e-1)))
    dt_bias = dt + jnp.log(-jnp.expm1(-dt))
    a_log = jnp.log(jax.random.uniform(ks[11], (DEPTH_2, 2, SSD_HEADS), f32, 1.0, 16.0))
    return {
        'x': nrm(ks[0], (BATCH, SEQ, D_MODEL), 1.0),
        'c': nrm(ks[1], (BATCH, D_MODEL), 1.0),
        'ctx': nrm(ks[2], (BATCH, CTX_LEN, D_MODEL), 1.0),
        'c_ctx': nrm(ks[3], (D_MODEL,), 1.0),
        'ada_w': nrm(ks[4], (DEPTH_2, D_MODEL, N_MOD * D_MODEL), 0.5 * D_MODEL ** -0.5),
        'ada_b': nrm(ks[5], (DEPTH_2, N_MOD * D_MODEL), 0.02),
        'norm_mix_g': gain(ks[6], (DEPTH_2, D_MODEL)),
        'w_in': nrm(ks[7], (DEPTH_2, D_MODEL, IN_DIM), D_MODEL ** -0.5),
        'conv_w': nrm(ks[8], (DEPTH_2, SSD_CONV, SSD_CONV_DIM), SSD_CONV ** -0.5),
        'conv_b': nrm(ks[9], (DEPTH_2, SSD_CONV_DIM), 0.02),
        'dt_bias_f': dt_bias[:, 0],
        'dt_bias_b': dt_bias[:, 1],
        'a_log_f': a_log[:, 0],
        'a_log_b': a_log[:, 1],
        'ssd_d': gain(ks[12], (DEPTH_2, SSD_HEADS)),
        'ssd_norm_g': gain(ks[13], (DEPTH_2, SSD_D_INNER)),
        'lambda_q1': nrm(ks[14], (DEPTH_2, ATT_HEAD_DIM), 0.1),
        'lambda_k1': nrm(ks[15], (DEPTH_2, ATT_HEAD_DIM), 0.1),
        'lambda_q2': nrm(ks[16], (DEPTH_2, ATT_HEAD_DIM), 0.1),
        'lambda_k2': nrm(ks[17], (DEPTH_2, ATT_HEAD_DIM), 0.1),
        'attn_subln_g': gain(ks[18], (DEPTH_2, 2 * ATT_HEAD_DIM)),
        'w_attn_o': nrm(ks[19], (DEPTH_2, ATT_V_DIM, D_MODEL), ATT_V_DIM ** -0.5),
        'w_ssd_o': nrm(ks[20], (DEPTH_2, SSD_D_INNER, D_MODEL), SSD_D_INNER ** -0.5),
        'w_out': nrm(ks[21], (DEPTH_2, D_MODEL, D_MODEL), D_MODEL ** -0.5),
        'norm_mlp_g': gain(ks[22], (DEPTH_2, D_MODEL)),
        'w_mlp1': nrm(ks[23], (DEPTH_2, D_MODEL, D_FF_2), D_MODEL ** -0.5),
        'w_mlp2': nrm(ks[24], (DEPTH_2, D_FF_2, D_MODEL), D_FF_2 ** -0.5),
        'final_norm_g': gain(ks[25], (D_MODEL,)),
    }

def second_block(x, c, ctx, c_ctx, ada_w, ada_b, norm_mix_g, w_in, conv_w, conv_b, dt_bias_f, dt_bias_b,
              a_log_f, a_log_b, ssd_d, ssd_norm_g, lambda_q1, lambda_k1, lambda_q2, lambda_k2,
              attn_subln_g, w_attn_o, w_ssd_o, w_out, norm_mlp_g, w_mlp1, w_mlp2, final_norm_g):
    n_lat = x.shape[1]
    cos, sin = axial_rope(n_lat)
    c_act = jax.nn.silu(c)
    cc_act = jax.nn.silu(c_ctx)
    xl, xc = x, ctx
    for l in range(DEPTH_2):
        last = l == DEPTH_2 - 1
        mod_l = [m[:, None, :] for m in jnp.split(c_act @ ada_w[l] + ada_b[l], N_MOD, axis=-1)]
        mod_c = jnp.split(cc_act @ ada_w[l] + ada_b[l], N_MOD, axis=-1)
        lam_init = 0.8 - 0.6 * math.exp(-0.3 * l)
        lam = (jnp.exp(jnp.sum(lambda_q1[l].astype(jnp.float32) * lambda_k1[l].astype(jnp.float32)))
               - jnp.exp(jnp.sum(lambda_q2[l].astype(jnp.float32) * lambda_k2[l].astype(jnp.float32)))
               + lam_init)
        h_l = modulate(xl, norm_mix_g[l], mod_l[0], mod_l[1])
        h_c = modulate(xc, norm_mix_g[l], mod_c[0], mod_c[1])
        o_l, o_c = hybrid_mixer_2(h_l, h_c, cos, sin, w_in[l], conv_w[l], conv_b[l], dt_bias_f[l], dt_bias_b[l],
                                a_log_f[l], a_log_b[l], ssd_d[l], ssd_norm_g[l], lam, lam_init,
                                attn_subln_g[l], w_attn_o[l], w_ssd_o[l], w_out[l], not last)
        xl = xl + mod_l[2] * o_l
        xl = xl + mod_l[5] * sq_relu_mlp(modulate(xl, norm_mlp_g[l], mod_l[3], mod_l[4]), w_mlp1[l], w_mlp2[l])
        if not last:
            xc = xc + mod_c[2] * o_c
            xc = xc + mod_c[5] * sq_relu_mlp(modulate(xc, norm_mlp_g[l], mod_c[3], mod_c[4]), w_mlp1[l], w_mlp2[l])
    return rmsnorm(xl, final_norm_g)


def setup_inputs(seed=0):
    out = dict(first_inputs(seed))
    for name, value in second_inputs(seed + 1).items():
        if name != "x":
            out[name + "_2"] = value
    return out


def reference(
    x, rel_bias, attn_pre_norm, w_in, b_gate, sinks, w_br_a, w_br_b, w_br_c, w_out,
    attn_post_norm, ffn_pre_norm, w_up, conv_w, conv_b, w_down, ffn_post_norm, c_2, ctx_2,
    c_ctx_2, ada_w_2, ada_b_2, norm_mix_g_2, w_in_2, conv_w_2, conv_b_2, dt_bias_f_2,
    dt_bias_b_2, a_log_f_2, a_log_b_2, ssd_d_2, ssd_norm_g_2, lambda_q1_2, lambda_k1_2,
    lambda_q2_2, lambda_k2_2, attn_subln_g_2, w_attn_o_2, w_ssd_o_2, w_out_2, norm_mlp_g_2,
    w_mlp1_2, w_mlp2_2, final_norm_g_2,
):
    x = first_block(
        x, rel_bias, attn_pre_norm, w_in, b_gate, sinks, w_br_a, w_br_b, w_br_c, w_out,
        attn_post_norm, ffn_pre_norm, w_up, conv_w, conv_b, w_down, ffn_post_norm,
    )
    return second_block(
        x, c_2, ctx_2, c_ctx_2, ada_w_2, ada_b_2, norm_mix_g_2, w_in_2, conv_w_2, conv_b_2,
        dt_bias_f_2, dt_bias_b_2, a_log_f_2, a_log_b_2, ssd_d_2, ssd_norm_g_2, lambda_q1_2,
        lambda_k1_2, lambda_q2_2, lambda_k2_2, attn_subln_g_2, w_attn_o_2, w_ssd_o_2, w_out_2,
        norm_mlp_g_2, w_mlp1_2, w_mlp2_2, final_norm_g_2,
    )


_drawn_inputs = setup_inputs


def setup_inputs(seed=0):
    import zlib

    import numpy as np

    out = dict(_drawn_inputs(seed))
    spreads = {}
    factors = {'sinks': 5.001,
     'conv_b': 3.421,
     'norm_mix_g_2': 5.02,
     'conv_b_2': 8.0,
     'ssd_d_2': 8.0,
     'ssd_norm_g_2': 8.0,
     'lambda_q1_2': 5.196,
     'lambda_k1_2': 8.0,
     'lambda_q2_2': 8.0,
     'lambda_k2_2': 8.0,
     'attn_subln_g_2': 8.0,
     'norm_mlp_g_2': 2.881}
    for name, (base, spread) in spreads.items():
        noise = np.random.default_rng([zlib.crc32(name.encode()), seed]).standard_normal(out[name].shape)
        drawn = base * np.exp(spread * noise) if base else spread * noise
        out[name] = __import__('jax').numpy.asarray(drawn.astype(out[name].dtype))
    for name, factor in factors.items():
        out[name] = (out[name] * factor).astype(out[name].dtype)
    return out
```

```python
import math
from contextlib import ExitStack

import numpy as np

import concourse.bass as bass
from concourse import mybir

P = 128
D = 1024
KT = D // P
T1 = 256
TT = 512
DEPTH_2 = 2
CHUNK = 256
SLOTS = 4
FF = 4 * D
NEG = -1.0e30
HD = 64
A_HEADS, A_GROUPS, B_HEADS, C_HEADS = 4, 3, 8, 4
SSD_HEADS, SSD_GROUPS, SSD_INNER = 32, 8, 2048
SCALE = HD ** -0.5
EPS = 1e-6
GRID_W = 64

ALU = mybir.AluOpType
ACT = mybir.ActivationFunctionType
AX = mybir.AxisListType
F32 = mybir.dt.float32


def columns_of(parts):
    at, out = 0, {}
    for name, n in parts:
        out[name] = (at, n)
        at += n
    return out, at


def param_parts():
    parts = [("pre_g", KT), ("post_g", KT), ("ffn_pre_g", KT), ("ffn_post_g", KT), ("b_gate", 3 * KT),
             ("conv_w", 3 * 2 * FF // P), ("conv_b", 2 * FF // P), ("final_g", KT), ("cvec", 2 * KT)]
    for la in range(DEPTH_2):
        parts += [(f"ada_b{la}", 6 * KT), (f"mix_g{la}", KT), (f"sconv_w{la}", 5 * 32), (f"sconv_b{la}", 32),
                  (f"subln_g{la}", 1), (f"ssd_g{la}", 16), (f"mlp_g{la}", KT)]
    return parts


def row_parts():
    parts = [("sinks", B_HEADS)]
    for la in range(DEPTH_2):
        parts += [(f"dt_bias{la}", 64), (f"a_log{la}", 64), (f"ssd_d{la}", SSD_HEADS),
                  (f"lam_q{la}", 128), (f"lam_k{la}", 128)]
    return parts


def const_parts():
    return [("ident", P), ("tri_le", P), ("tri_ge", P), ("rot", P), ("flip", P), ("cos", T1), ("sin", T1),
            ("c_before", 2 * P), ("c_after", 2 * P)]


PARAMS, N_PARAMS = columns_of(param_parts())
ROWS, N_ROWS = columns_of(row_parts())
CONSTS, N_CONSTS = columns_of(const_parts())
N_REV = 384
N_BIAS = A_GROUPS * A_HEADS + B_HEADS


def chunk_plan():
    sizes = [("a_qk", 6), ("a_v", 3), ("b_q", 2), ("b_kv", 1), ("c_qk", 2), ("c_v", 1), ("gates", 12),
             ("branches", 4), ("out", 4), ("up", 32), ("down", 16)]
    for la in range(DEPTH_2):
        sizes += [(f"ada{la}", 24), (f"q{la}", 4), (f"k{la}", 4), (f"v{la}", 4), (f"ga{la}", 4), (f"attn_o{la}", 4),
                  (f"ssd{la}", 16), (f"z{la}", 8), (f"ssd_o{la}", 8),
                  (f"gs{la}", 4), (f"out2{la}", 4), (f"mlp1{la}", 16), (f"mlp2{la}", 16)]
    at, plan = 0, {}
    for name, n in sizes:
        plan[name] = (at, n)
        at += n
    return plan, at


PLAN, N_CHUNKS = chunk_plan()


def group_plan():
    at, plan = 0, {}
    for name, (_, n) in PLAN.items():
        share = 4 if name == "down" or name.startswith("mlp2") else 2 if name.startswith("ssd_o") else 1
        plan[name] = at
        at += n // share
    return plan


GROUPS = group_plan()

B1_BIAS = 0
B1_QK = B1_BIAS + N_BIAS * 256
B1_V = B1_QK + 21 * 256
B1_GATE = B1_V + 2 * 1152
B1_O = B1_GATE + 24 * 256
B1_TMP = B1_O + 8 * 256
L_Q, L_K, L_V, L_TMP = 0, 4096, 8192, 16384
L_Y, L_MRG, L_SSD = 0, 8192, 12288
ARENA = 26624
ADA_WORDS = 6 * D


def program(nc, xT, stream, params, rows, consts, rel_bias, rev_hot, w_dt, scratch, out):
    ctx = ExitStack()
    with ctx:
        def sb(name, shape):
            return ctx.enter_context(nc.sbuf_tensor(name, shape, F32))

        made = {}

        def sem(name):
            if name not in made:
                made[name] = ctx.enter_context(nc.semaphore(name))
            return made[name]

        ring = sb("ring", [P, SLOTS, KT, CHUNK])
        X = sb("X", [P, KT, TT])
        H = sb("H", [P, KT, TT])
        par = sb("par", [P, N_PARAMS])
        row = sb("row", [P, N_ROWS])
        con = sb("con", [P, N_CONSTS])
        wdt = sb("wdt", [P, DEPTH_2, KT, 64])
        mod = sb("mod", [P, DEPTH_2, 6 * KT, 2])
        small = sb("small", [P, 512])
        work = sb("work", [P, ARENA])
        PB = ctx.enter_context(nc.psum_tensor("PB", [P, 2, 2, 512], F32))
        PA = [ctx.enter_context(nc.psum_tensor(f"PA{i}", [P, 512], F32))[:, :] for i in range(2)]
        PS = ctx.enter_context(nc.psum_tensor("PS", [P, 2, 512], F32))

        def area(at, *shape):
            n = int(np.prod(shape))
            assert at + n <= ARENA, (at, n)
            v = work[:, at:at + n]
            names = "abcd"[:len(shape)]
            if len(shape) == 1:
                return v
            return v.rearrange(f"p ({' '.join(names)}) -> p {' '.join(names)}",
                               **{k: s for k, s in zip(names, shape)})

        def p_(name, i=0, n=1):
            at, _ = PARAMS[name]
            return par[:, at + i:at + i + n]

        def r_(name, i=0, n=None):
            at, m = ROWS[name]
            return row[:, at + i:at + i + (m if n is None else n)]

        def c_(name, i=0, n=None):
            at, m = CONSTS[name]
            return con[:, at + i:at + i + (m if n is None else n)]

        ident = c_("ident")
        ONE, ONE_D, ONE_H, ONE_I = (small[:, 0:1], small[:, 1:2], small[:, 2:3], small[:, 3:4])
        EPS_C = small[:, 4:5]
        LAM = small[:, 8:16]

        def full(col):
            return col.broadcast_to([P, P])

        landed = [sem(f"weights_landed{i}") for i in range(SLOTS)]
        chunk_done = sem("chunk_done")
        evacuated = [sem("evacuated0"), sem("evacuated1")]
        stage_end = sem("stage_end")
        loaded, rows_in = sem("loaded"), sem("rows_in")

        LAYER = {
            "mod_sum": 1, "rot_read": 16, "rot": 16, "rot_cos": 16, "w_exp": 64, "w_scores": 32,
            "w_probs": 32, "w_turned": 32, "w_turns": 32, "w_out_read": 32, "w_out": 32, "w_max": 32,
            "sub_sq": 8, "sub_root": 8, "sub_sum": 8, "sub_out": 8, "ga_v": 4, "dt_sum": 1,
            "dt_a": 1, "dt_cs": 1, "dt_abs": 1, "dt_exp": 1, "dt_one": 1, "dt_ln": 1,
            "dt_rest": 2, "dt_wd": 1, "s_conv": 32, "s_y": 16, "s_diff": 64, "s_turns": 24,
            "s_cb": 8, "s_turned": 24, "s_xd": 48, "s_delta": 48, "s_state": 48, "s_inter": 48,
            "s_inter_read": 48, "s_cbm": 16, "s_bc": 64, "s_exp": 64, "s_m": 64, "s_xc": 64,
            "s_within": 32, "s_mid": 32, "s_yi": 8, "yt_read": 16, "yt": 16, "z_used": 8,
            "z_sq": 4, "z_root": 1, "gs_v": 4, "gs_done": 1,
        }
        NORMS = ["n1", "n2", "n3", "n4", "m10", "m20", "m11", "m21", "final"]

        def past(tag):
            return {"m10": 0, "m20": 2 * KT, "m11": 4 * KT, "m21": 6 * KT}[tag]

        barriers = {}

        def barrier(eng, who):
            barriers[who] = barriers.get(who, 0) + 1
            eng.drain().then_inc(stage_end, 1)
            eng.wait_ge(stage_end, 4 * barriers[who])

        def repeat(eng, n, body, first=False):
            if first:
                body(0)
            if n == 1:
                body(0)
            else:
                with eng.Fori(1 if first else 0, n) as i:
                    body(i)

        def mod_(la, part, k, c):
            i = part * KT + k
            return mod[:, la, i:i + 1, c:c + 1].rearrange("p a b -> p (a b)")

        def span(base, step, it, size=1):
            if isinstance(it, int):
                return slice((base + step * it) * size, (base + step * it + 1) * size)
            return bass.ds(it * (step * size) + base * size, size)

        def span2(j, step, it):
            if isinstance(it, int):
                return slice(2 * (j + step * it), 2 * (j + step * it) + 2)
            return bass.ds(it * (2 * step) + 2 * j, 2)

        def one(buf, base, step, it):
            if isinstance(it, int):
                return buf[:, base + step * it, :]
            return buf[:, span(base, step, it), :].rearrange("p o n -> p (o n)")

        def take_chunk(pe, c, it, step):
            pe.wait_ge(landed[c % SLOTS], 16 * (c // SLOTS + 1) + 16 * (step // SLOTS) * it)

        def take_banks(pe, g, it, step):
            if g >= 2:
                pe.wait_ge(evacuated[g % 2], 2 * (g // 2) + step * it)

        def pe_features(pe, name, rhs, T, per=4):
            (c0, n), g0 = PLAN[name], GROUPS[name]
            per = min(per, n)
            loops = n // per if n % per == 0 and per % SLOTS == 0 else 1
            per = n // loops

            def body(it):
                for j in range(per):
                    c, g = c0 + j, g0 + j
                    take_chunk(pe, c, it, per)
                    take_banks(pe, g, it, per)
                    for t in range(2):
                        for k in range(KT):
                            mm = pe.matmul(PB[:, g % 2, t, 0:T], ring[:, c % SLOTS, k, t * P:(t + 1) * P],
                                           rhs(k), start=(k == 0), stop=(k == KT - 1))
                    mm.then_inc(chunk_done, 1)
            repeat(pe, loops, body)

        def pe_tokens(pe, name, lhs, n_tok, per=4):
            (c0, n), g0 = PLAN[name], GROUPS[name]
            loops = n // per if n % per == 0 else 1
            per = n // loops

            def body(it):
                for j in range(per):
                    c, g = c0 + j, g0 + j
                    take_chunk(pe, c, it, per)
                    take_banks(pe, g, it, per)
                    for t in range(n_tok):
                        half = t // (n_tok // 2)
                        col = CHUNK * (t % (n_tok // 2))
                        for k in range(KT):
                            mm = pe.matmul(PB[:, g % 2, half, col:col + CHUNK], lhs(k, t),
                                           ring[:, c % SLOTS, k, :], start=(k == 0), stop=(k == KT - 1))
                    mm.then_inc(chunk_done, 1)
            repeat(pe, loops, body)

        def pe_deep(pe, name, rhs, T, share):
            (c0, n), g0 = PLAN[name], GROUPS[name]
            per = 2 * share
            loops = n // per if per % SLOTS == 0 else 1
            per = n // loops

            def body(it):
                for j in range(per):
                    c, g, part = c0 + j, g0 + j // share, j % share
                    take_chunk(pe, c, it, per)
                    if part == 0:
                        take_banks(pe, g, it, per // share)
                    for t in range(2):
                        for k in range(KT):
                            mm = pe.matmul(PB[:, g % 2, t, 0:T], ring[:, c % SLOTS, k, t * P:(t + 1) * P],
                                           rhs(KT * part + k), start=(part == 0 and k == 0),
                                           stop=(part == share - 1 and k == KT - 1))
                    mm.then_inc(chunk_done, 1)
            repeat(pe, loops, body)

        def evac(eng, half, name, op, share=1, per=4):
            (c0, n), g0 = PLAN[name], GROUPS[name]
            groups = n // share
            per_g = min(per, groups) if share == 1 else 2
            if groups % per_g or (per_g * share) % SLOTS or per_g % 2:
                per_g = groups
            loops = groups // per_g

            def body(it):
                for j in range(per_g):
                    g = g0 + j
                    eng.wait_ge(chunk_done, c0 + share * (j + 1) + per_g * share * it)
                    op(PB[:, g % 2, half, :], j, it * per_g if loops > 1 else 0).then_inc(evacuated[g % 2], 1)
            repeat(eng, loops, body)

        def both(eng, name, op, share=1):
            (c0, n), g0 = PLAN[name], GROUPS[name]
            groups = n // share
            per_g = min(4, groups) if share == 1 else 2
            loops = groups // per_g

            def body(it):
                for j in range(per_g):
                    g = g0 + j
                    eng.wait_ge(chunk_done, c0 + share * (j + 1) + per_g * share * it)
                    for t in range(2):
                        op(PB[:, g % 2, t, :], t, j, it * per_g if loops > 1 else 0).then_inc(evacuated[g % 2], 1)
            repeat(eng, loops, body)

        SQ = area(ARENA - 4096, KT, TT)
        RSTD = sb("rstd", [P, TT])

        def norm_pe(pe, tag, T, ones, n=KT):
            for k in range(n):
                if k % 2 == 0:
                    pe.wait_ge(sem("norm_sq_v"), 4 * NORMS.index(tag) + k // 2 + 1)
                else:
                    pe.wait_ge(sem("norm_sq_a"), 4 * NORMS.index(tag) + k // 2 + 1)
                mm = pe.matmul(PA[0][:, 0:T], full(ones), SQ[:, k, 0:T], start=(k == 0), stop=(k == n - 1))
            mm.then_inc(sem("norm_sum"), 1)

        def norm_act(act, tag, src, T):
            for k in range(1, KT, 2):
                nc.scalar.activation(SQ[:, k, 0:T], src(k), ACT.Square).then_inc(sem("norm_sq_a"), 1)
            act.wait_ge(sem("norm_sum"), NORMS.index(tag) + 1)
            nc.scalar.activation(RSTD[:, 0:T], PA[0][:, 0:T], ACT.Sqrt, bias=EPS_C).then_inc(sem("norm_root"), 1)

        def norm_dve(v, tag, src, T):
            for k in range(0, KT, 2):
                nc.vector.tensor_tensor(SQ[:, k, 0:T], src(k), src(k), ALU.mult).then_inc(sem("norm_sq_v"), 1)
            v.wait_ge(sem("norm_root"), NORMS.index(tag) + 1)
            nc.vector.reciprocal(RSTD[:, 0:T], RSTD[:, 0:T]).then_inc(sem("norm_rstd"), 1)
            v.wait_ge(sem("norm_rstd"), NORMS.index(tag) + 1)

        A_QK = area(B1_QK, 21, T1)
        V1 = area(B1_V, 2, 1152)
        GATE = area(B1_GATE, 24, T1)
        O1 = area(B1_O, 8, T1)
        BIAS = area(B1_BIAS, N_BIAS, 256)
        BIAS_UP = area(B1_GATE, N_BIAS, 256)
        REL = area(B1_O, 32)
        HOT = area(B1_O + 32, N_REV)
        REV = area(B1_O + 512, N_REV)
        HO1 = area(B1_QK, 8, T1)
        HID1 = area(0, 32, T1)
        DN1 = area(B1_GATE, 8, T1)
        UP = area(B1_QK + 4096, 2, 2, 2 * T1)

        U_L = [area(B1_TMP + 768 * i, 768) for i in range(2)]
        U_P = [area(B1_TMP + 1536 + 768 * i, 768) for i in range(2)]
        U_T = area(B1_TMP + 3072, 6, P)
        U_R = area(B1_TMP + 3840, 260)
        U_K = area(B1_TMP + 4104, 256)
        STAT = small[:, 64:96]
        CACT = small[:, 16:32].rearrange("p (k c) -> p k c", c=2)
        NEG_SINK = small[:, 32:40]
        NEG_LAM = small[:, 40:42]
        LAMS = small[:, 48:56]

        LQ, LK, LV = area(L_Q, KT, TT), area(L_K, KT, TT), area(L_V, 4, D)
        MRG = area(L_MRG, KT, TT)
        AT_P = [area(L_TMP + 1024 * i, 2, TT) for i in range(2)]
        AT_T = [area(L_TMP + 2048 + 512 * i, 4, P) for i in range(2)]
        ADA = area(0, ADA_WORDS)
        ROT_T = [area(L_TMP + 4096 + 256 * i, T1) for i in range(2)]
        SUB_R = [area(L_TMP + 512 * i, TT) for i in range(2)]
        SUB_S = [area(L_TMP + 1024 + 512 * i, TT) for i in range(2)]

        Y = area(L_Y, 4, SSD_INNER)
        at = L_SSD
        CV = [area(at + 2048 * i, 4, TT) for i in range(2)]
        at += 4096
        XG = area(at, 4, 256)
        at += 1024
        BT = area(at, 4, P)
        at += 512
        CBM = area(at, 2, 4, P)
        at += 1024
        MB = [area(at + 1024 * i, 2, 4, P) for i in range(2)]
        at += 2048
        XC = [area(at + 512 * i, 2, 4, HD) for i in range(2)]
        at += 1024
        XD = [area(at + 256 * i, 256) for i in range(2)]
        at += 512
        HT = [area(at + 256 * i, 256) for i in range(2)]
        at += 512
        YI = area(at, 4, 256)
        at += 1024
        YT2 = [area(at + 256 * i, 256) for i in range(2)]
        at += 512
        DT, DTA, CS, ECS, WD, CHD = (area(at + 256 * i, 4, 64) for i in range(6))
        at += 1536
        assert at <= ARENA, at
        ZT = [area(L_SSD + 8192 + 1024 * i, 1024) for i in range(2)]
        YT = area(L_SSD, 16, TT)
        MIX = area(L_SSD + 8192, KT, TT)
        GS = area(L_Y, KT, TT)
        HID2 = area(0, 32, TT)
        HID1_PAIRS = area(0, 16, 2 * T1)

        units1 = [("a", h, qt) for h in range(A_HEADS) for qt in range(2)]
        units1 += [("b", h, qt) for h in range(B_HEADS) for qt in range(2)]
        units1 += [("c", h, qt) for h in range(C_HEADS) for qt in range(2)]
        N_AB = 2 * (A_HEADS + B_HEADS)

        def unit1(u):
            br, h, qt = units1[u]
            if br == "a":
                q, k = [2 * g + h // 2 for g in range(3)], [6 + 2 * g + h // 2 for g in range(3)]
                return br, h, qt, q, k, h % 2, h % 2, [(g * A_HEADS + h) * HD for g in range(3)], h // 2
            if br == "b":
                half = h // (B_HEADS // 2)
                return br, h, qt, [12 + h % 4], [16], half, half, [768 + half * HD], 2 + h % 4
            return br, h, qt, [17 + h // 2], [19 + h // 2], h % 2, h % 2, [896 + h * HD], 6 + h // 2

        def scores_bank(u):
            return PS if u % 2 == 0 else PB[:, 1]

        def units2(la):
            lat = [(h, qt, 0, TT) for h in range(8) for qt in range(2)]
            own = [(h, 2 + qt, T1, T1) for h in range(8) for qt in range(2)]
            return lat + (own if la == 0 else [])

        F_ORDER, B_ORDER = (2, 3, 0, 1), (3, 2, 1, 0)

        def channels(g, i):
            return (2 * g, 2 * g + 1, 16 + g, 24 + g)[i]

        def inter_count(la, g, i):
            a_group = 6 if la == 0 else 4
            return a_group * g + max(0, 2 * (i + 1) - (0 if la == 0 else 2))

        def live(la, tt):
            return la == 0 or tt < 2

        block = ctx.enter_context(nc.Block())

        @block.sync
        def _(sp):
            sp.dma_start(X[:, :, :], xT).then_inc(loaded, 16)
            sp.dma_start(par[:, :], params).then_inc(loaded, 16)
            sp.dma_start(con[:, :], consts).then_inc(loaded, 16)
            for c in range(SLOTS):
                sp.dma_start(ring[:, c, :, :], stream[c]).then_inc(landed[c], 16)
            with sp.Fori(1, N_CHUNKS // SLOTS) as it:
                for j in range(SLOTS):
                    sp.wait_ge(chunk_done, SLOTS * it + (j + 1 - SLOTS))
                    sp.dma_start(ring[:, j, :, :],
                                 stream[bass.ds(SLOTS * it + j, 1)].rearrange("o p k n -> (o p) k n"))\
                        .then_inc(landed[j], 16)
            for c in range(N_CHUNKS // SLOTS * SLOTS, N_CHUNKS):
                sp.wait_ge(chunk_done, c - SLOTS + 1)
                sp.dma_start(ring[:, c % SLOTS, :, :], stream[c]).then_inc(landed[c % SLOTS], 16)
            sp.wait_ge(sem("final_h"), KT)
            sp.dma_start(out, H[:, :, 0:T1]).then_inc(sem("stored"), 16)
            sp.wait_ge(sem("stored"), 16)

        @block.tensor
        def _(pe):
            def bar():
                barrier(pe, "pe")

            pe.wait_ge(loaded, 16 * 3)
            pe.wait_ge(rows_in, 16 * 2)
            pe.wait_ge(sem("consts"), 1)
            pe.wait_ge(sem("hot"), 32)
            pe.matmul(PA[1][0:N_BIAS, 0:N_REV], REL[0:36, 0:N_BIAS], HOT[0:36, :], start=True, stop=True)\
                .then_inc(sem("rev_sum"), 1)

            def x1(k):
                return X[:, k, 0:T1]

            def h1(k):
                return H[:, k, 0:T1]

            def h1_tok(k, t):
                return H[:, k, t * P:(t + 1) * P]

            norm_pe(pe, "n1", T1, ONE_D)
            pe.wait_ge(sem("n1_h"), KT)
            pe_features(pe, "a_qk", h1, T1)
            pe_tokens(pe, "a_v", h1_tok, 2)
            pe_features(pe, "b_q", h1, T1)
            c, g = PLAN["b_kv"][0], GROUPS["b_kv"]
            take_chunk(pe, c, 0, 0)
            take_banks(pe, g, 0, 0)
            for k in range(KT):
                pe.matmul(PB[:, g % 2, 0, 0:T1], ring[:, c % SLOTS, k, 0:P], h1(k),
                          start=(k == 0), stop=(k == KT - 1))
            for t in range(2):
                for k in range(KT):
                    mm = pe.matmul(PB[:, g % 2, 1, t * P:(t + 1) * P], h1_tok(k, t),
                                   ring[:, c % SLOTS, k, P:2 * P], start=(k == 0), stop=(k == KT - 1))
            mm.then_inc(chunk_done, 1)
            pe_features(pe, "c_qk", h1, T1)
            pe_tokens(pe, "c_v", h1_tok, 2)
            pe.wait_ge(sem("bias_in"), 16)
            for i in range(N_BIAS // 2):
                if i >= 2:
                    pe.wait_ge(sem("flip_read"), i - 1)
                pe.matmul(PS[:, i % 2, :], c_("flip"), BIAS_UP[:, 2 * i:2 * i + 2, :].rearrange("p a b -> p (a b)"),
                          start=True, stop=True).then_inc(sem("flip"), 1)
            pe_features(pe, "gates", h1, T1)
            bar()

            def scores1(u):
                br, h, qt, qi, ki, qh, kh, vi, o = unit1(u)
                nk = P * (qt + 1)
                if u >= 2:
                    if u - 2 < N_AB:
                        pe.wait_ge(sem("u_read_v"), u - 1)
                    else:
                        pe.wait_ge(sem("u_read_a"), u - 1 - N_AB)
                S = scores_bank(u)
                for i, (a, b) in enumerate(zip(qi, ki)):
                    r = slice(HD * qh, HD * qh + HD)
                    mm = pe.matmul(S[:, i // 2, (i % 2) * nk:(i % 2) * nk + nk], A_QK[r, a, qt * P:(qt + 1) * P],
                                   A_QK[r, b, 0:nk], start=True, stop=True)
                mm.then_inc(sem("u_scores"), 1)

            def values1(u):
                br, h, qt, qi, ki, qh, kh, vi, o = unit1(u)
                nk = P * (qt + 1)
                n = len(qi) * (qt + 1)
                pe.wait_ge(sem("u_probs"), u + 1)
                if u >= 1:
                    pe.wait_ge(sem("u_turned"), u)
                for i in range(n):
                    mm = pe.transpose(PA[i // 4][:, (i % 4) * P:(i % 4 + 1) * P],
                                      U_P[u % 2][:, i * P:(i + 1) * P], ident)
                mm.then_inc(sem("u_turns"), 1)
                pe.wait_ge(sem("u_turned"), u + 1)
                if u >= 2:
                    pe.wait_ge(sem("u_out_read"), u - 1)
                for i in range(n):
                    col = vi[i // (qt + 1)]
                    mm = pe.matmul(PB[HD * qh:HD * qh + HD, 0, u % 2, 0:P],
                                   V1[:, i % (qt + 1), col:col + HD], U_T[:, i, :],
                                   start=(i == 0), stop=(i == n - 1))
                mm.then_inc(sem("u_out"), 1)

            for u in range(len(units1) + 1):
                if u < len(units1):
                    scores1(u)
                if u >= 1:
                    values1(u - 1)
            bar()

            c0, g0 = PLAN["branches"][0], GROUPS["branches"]
            for j in range(4):
                c, g = c0 + j, g0 + j
                take_chunk(pe, c, 0, 0)
                take_banks(pe, g, 0, 0)
                for t in range(2):
                    for i, (k0, k1) in enumerate(((0, 2), (2, 6), (6, 8))):
                        dst = PS[:, g % 2, t * T1:(t + 1) * T1] if i == 2 \
                            else PB[:, g % 2, t, i * T1:(i + 1) * T1]
                        for k in range(k0, k1):
                            mm = pe.matmul(dst, ring[:, c % SLOTS, k, t * P:(t + 1) * P], O1[:, k, :],
                                           start=(k == k0), stop=(k == k1 - 1))
                mm.then_inc(chunk_done, 1)
            bar()
            pe_features(pe, "out", lambda k: GATE[:, k, :], T1)
            bar()
            norm_pe(pe, "n2", T1, ONE_D)
            bar()
            norm_pe(pe, "n3", T1, ONE_D)
            pe.wait_ge(sem("n3_h"), KT)
            pe_features(pe, "up", h1, T1)
            bar()
            pe_deep(pe, "down", lambda k: HID1[:, k, :], T1, 4)
            bar()
            norm_pe(pe, "n4", T1, ONE_D)
            bar()

            for la in range(DEPTH_2):
                T = TT if la == 0 else T1
                (c0, n), g0 = PLAN[f"ada{la}"], GROUPS[f"ada{la}"]

                def ada(it):
                    for j in range(4):
                        c, g = c0 + j, g0 + j
                        take_chunk(pe, c, it, 4)
                        take_banks(pe, g, it, 4)
                        for t in range(2):
                            for k in range(KT):
                                mm = pe.matmul(PB[0:2, g % 2, t, 0:P], CACT[:, k, :],
                                               ring[:, c % SLOTS, k, t * P:(t + 1) * P],
                                               start=(k == 0), stop=(k == KT - 1))
                        mm.then_inc(chunk_done, 1)
                repeat(pe, n // 4, ada)
                bar()
                for i in range(6 * KT):
                    mm = pe.transpose(PA[1][:, 2 * i:2 * i + 2], ADA[0:2, i * P:(i + 1) * P], ident[0:2, 0:2])
                mm.then_inc(sem("mod_sum"), 1)
                norm_pe(pe, f"m1{la}", TT, ONE_D)
                pe.wait_ge(sem("mod_shifted"), past(f"m1{la}") + 2 * KT)

                def hl(k):
                    return H[:, k, 0:T]

                def hall(k):
                    return H[:, k, :]

                pe_features(pe, f"q{la}", hl, T)
                pe_features(pe, f"k{la}", hall, TT)
                pe_tokens(pe, f"v{la}", lambda k, t: H[:, k, t * P:(t + 1) * P], 4)
                bar()
                for i in range(2 * KT):
                    if i >= 2:
                        pe.wait_ge(sem("rot_read"), LAYER["rot_read"] * la + i - 1)
                    pe.matmul(PS[:, i % 2, 0:T1], c_("rot"), (LQ if i < KT else LK)[:, i % KT, 0:T1],
                              start=True, stop=True).then_inc(sem("rot"), 1)
                bar()

                us = units2(la)

                def scores2(u):
                    h, qt, k0, nk = us[u]
                    if u >= 2:
                        pe.wait_ge(sem("w_exp"), LAYER["w_exp"] * la + 2 * (u - 1))
                    S = scores_bank(u)
                    for cc in range(2):
                        rows_ = slice(HD * cc, HD * cc + HD)
                        mm = pe.matmul(S[:, cc, 0:nk], LQ[rows_, h, qt * P:(qt + 1) * P],
                                       LK[rows_, h, k0:k0 + nk], start=True, stop=True)
                    mm.then_inc(sem("w_scores"), 1)

                def values2(u):
                    h, qt, k0, nk = us[u]
                    n = nk // P
                    pe.wait_ge(sem("w_probs"), LAYER["w_probs"] * la + u + 1)
                    if u >= 2:
                        pe.wait_ge(sem("w_turned"), LAYER["w_turned"] * la + u - 1)
                    for i in range(n):
                        mm = pe.transpose(PA[u % 2][:, i * P:(i + 1) * P],
                                          AT_P[u % 2][:, 0, i * P:(i + 1) * P], ident)
                    mm.then_inc(sem("w_turns"), 1)
                    pe.wait_ge(sem("w_turned"), LAYER["w_turned"] * la + u + 1)
                    if u >= 2:
                        pe.wait_ge(sem("w_out_read"), LAYER["w_out_read"] * la + u - 1)
                    for i in range(n):
                        mm = pe.matmul(PB[:, 0, u % 2, 0:P], LV[:, k0 // P + i, h * P:(h + 1) * P],
                                       AT_T[u % 2][:, i, :], start=(i == 0), stop=(i == n - 1))
                    mm.then_inc(sem("w_out"), 1)

                for u in range(len(us) + 1):
                    if u < len(us):
                        scores2(u)
                    if u >= 1:
                        values2(u - 1)
                bar()
                for h in range(8):
                    pe.wait_ge(sem("sub_sq"), LAYER["sub_sq"] * la + h + 1)
                    if h >= 2:
                        pe.wait_ge(sem("sub_root"), LAYER["sub_root"] * la + h - 1)
                    pe.matmul(PS[:, h % 2, 0:T], full(ONE_H), SUB_S[h % 2][:, 0:T], start=True, stop=True)\
                        .then_inc(sem("sub_sum"), 1)
                bar()
                pe_features(pe, f"ga{la}", hl, T)
                bar()
                pe_features(pe, f"attn_o{la}", lambda k: LQ[:, k, 0:T], T)
                bar()
                for t in range(4):
                    for k in range(KT):
                        mm = pe.matmul(PS[:, 0, 64 * t:64 * t + 64], H[:, k, t * P:(t + 1) * P],
                                       wdt[:, la, k, :], start=(k == 0), stop=(k == KT - 1))
                mm.then_inc(sem("dt_sum"), 1)
                pe.wait_ge(sem("dt_a"), LAYER["dt_a"] * la + 1)
                for t in range(4):
                    for d, tri in enumerate((c_("tri_le"), c_("tri_ge"))):
                        pe.matmul(PS[:, 1, 64 * t + 32 * d:64 * t + 32 * d + 32], tri,
                                  DTA[:, t, 32 * d:32 * d + 32], start=True, stop=True)
                pe.matmul(PS[:, 1, 256:512], full(ONE), DTA.rearrange("p a b -> p (a b)"),
                          start=True, stop=True).then_inc(sem("dt_cs"), 1)
                bar()

                (c0, _), g0 = PLAN[f"ssd{la}"], GROUPS[f"ssd{la}"]

                def project(g):
                    for j in range(2):
                        c, gg = c0 + 2 * g + j, g0 + 2 * g + j
                        take_chunk(pe, c, 0, 0)
                        take_banks(pe, gg, 0, 0)
                        for t in range(2):
                            Tc = T if (j, t) == (1, 1) else TT
                            for k in range(KT):
                                mm = pe.matmul(PB[:, gg % 2, t, 0:Tc], ring[:, c % SLOTS, k, t * P:(t + 1) * P],
                                               H[:, k, 0:Tc], start=(k == 0), stop=(k == KT - 1))
                        mm.then_inc(chunk_done, 1)

                def scan_group(g):
                    b = g % 2
                    tok = [t for t in range(4) if live(la, t)]
                    pe.wait_ge(sem("s_conv"), LAYER["s_conv"] * la + 4 * g + 4)
                    if g >= 1:
                        pe.wait_ge(sem("s_y"), LAYER["s_y"] * la + (2 if la == 0 else 1) * g)
                    for i, bank in enumerate((PA[0], PA[1], PS[:, 0])):
                        if i == 2 and g >= 1:
                            pe.wait_ge(sem("s_diff"), LAYER["s_diff"] * la + 8 * g)
                        for t in range(4):
                            mm = pe.transpose(bank[:, t * P:(t + 1) * P], CV[b][:, i, t * P:(t + 1) * P], ident)
                        mm.then_inc(sem("s_turns"), 1)
                    for t in tok:
                        mm = pe.matmul(PS[:, 1, t * P:(t + 1) * P], CV[b][:, 2, t * P:(t + 1) * P],
                                       CV[b][:, 3, t * P:(t + 1) * P], start=True, stop=True)
                    mm.then_inc(sem("s_cb"), 1)
                    pe.wait_ge(sem("s_turned"), LAYER["s_turned"] * la + 3 * g + 3)
                    for i in range(3):
                        for d, order in enumerate((F_ORDER, B_ORDER)):
                            n = 6 * g + 2 * i + d
                            pe.wait_ge(sem("s_xd"), LAYER["s_xd"] * la + n + 1)
                            pe.matmul(PA[0][:, 256 * d:256 * d + 256], BT[:, order[i], :], XD[d],
                                      start=True, stop=True).then_inc(sem("s_delta"), 1)
                        for d, order in enumerate((F_ORDER, B_ORDER)):
                            n = 6 * g + 2 * i + d
                            pe.wait_ge(sem("s_state"), LAYER["s_state"] * la + n + 1)
                            t = order[i + 1]
                            if live(la, t):
                                pe.matmul(PA[1][:, 256 * d:256 * d + 256], CV[b][:, 3, t * P:(t + 1) * P], HT[d],
                                          start=True, stop=True).then_inc(sem("s_inter"), 1)
                        if inter_count(la, g, i):
                            pe.wait_ge(sem("s_inter_read"), LAYER["s_inter_read"] * la + inter_count(la, g, i))

                    def decays(r):
                        n = 4 * g + r
                        for d, tri in enumerate((c_("tri_le"), c_("tri_ge"))):
                            if r == 0:
                                pe.wait_ge(sem("s_cbm"), LAYER["s_cbm"] * la + 2 * g + 2)
                            else:
                                pe.wait_ge(sem("s_diff"), LAYER["s_diff"] * la + 2 * (n - 1) + d + 1)
                            for t in tok:
                                hh = 32 * d + 4 * g + r
                                mm = pe.matmul(PS[:, d, t * P:(t + 1) * P], full(DTA[:, t, hh:hh + 1]), tri,
                                               start=True, stop=True)
                            mm.then_inc(sem("s_bc"), 1)

                    def within(r):
                        n = 4 * g + r
                        pe.wait_ge(sem("s_m"), LAYER["s_m"] * la + 2 * n + 2)
                        pe.wait_ge(sem("s_xc"), LAYER["s_xc"] * la + 2 * n + 2)
                        for t in tok:
                            for d in range(2):
                                mm = pe.matmul(PA[t // 2][:, 256 * (t % 2) + HD * r:256 * (t % 2) + HD * r + HD],
                                               MB[r % 2][:, d, t, :], XC[r % 2][:, d, t, :],
                                               start=(d == 0), stop=(d == 1))
                        mm.then_inc(sem("s_within"), 1)

                    decays(0)
                    for r in range(4):
                        if r < 3:
                            decays(r + 1)
                        within(r)

                project(0)
                for g in range(SSD_GROUPS):
                    if g + 1 < SSD_GROUPS:
                        project(g + 1)
                    scan_group(g)
                bar()
                pe_tokens(pe, f"z{la}", lambda k, t: H[:, k, t * P:(t + 1) * P], T // P)
                bar()
                for i in range(16):
                    if i >= 2:
                        pe.wait_ge(sem("yt_read"), LAYER["yt_read"] * la + i - 1)
                    for t in range(T // P):
                        mm = pe.transpose(PS[:, i % 2, t * P:(t + 1) * P], Y[:, t, i * P:(i + 1) * P], ident)
                    mm.then_inc(sem("yt"), 1)
                bar()
                pe_deep(pe, f"ssd_o{la}", lambda k: YT[:, k, 0:T], T, 2)
                pe_features(pe, f"gs{la}", hl, T)
                bar()
                pe_features(pe, f"out2{la}", lambda k: MRG[:, k, 0:T], T)
                bar()
                norm_pe(pe, f"m2{la}", T, ONE_D)
                pe.wait_ge(sem("mod_shifted"), past(f"m2{la}") + KT * (T // T1))
                pe_features(pe, f"mlp1{la}", hl, T)
                bar()
                pe_deep(pe, f"mlp2{la}", lambda k: HID2[:, k, 0:T], T, 4)
                bar()
            norm_pe(pe, "final", T1, ONE_D)

        @block.scalar
        def _(act):
            def bar():
                barrier(act, "act")

            copy = nc.scalar.activation

            act.wait_ge(loaded, 16 * 3)
            act.wait_ge(rows_in, 16 * 2)
            act.wait_ge(sem("consts"), 1)
            copy(CACT, p_("cvec", 0, 16).rearrange("p (c k) -> p k c", c=2), ACT.Silu).then_inc(sem("cact"), 1)
            act.wait_ge(sem("lam_dot"), 4)
            copy(LAMS[:, 0:4], LAMS[:, 0:4], ACT.Exp).then_inc(sem("lam_exp"), 1)
            for la in range(DEPTH_2):
                copy(r_(f"a_log{la}"), r_(f"a_log{la}"), ACT.Exp).then_inc(sem("a_exp"), 1)

            def x1(k):
                return X[:, k, 0:T1]

            norm_act(act, "n1", x1, T1)

            def qk_out(base, scaled):
                def op(bank, j, it):
                    return copy(A_QK[:, base + 2 * j + 1, :], bank[:, 0:T1], ACT.Copy,
                                scale=SCALE if j < scaled else 1.0)
                return op

            evac(act, 1, "a_qk", qk_out(0, 3))
            evac(act, 1, "a_v", lambda bank, j, it: copy(V1[:, 1, CHUNK * j:CHUNK * (j + 1)], bank[:, 0:CHUNK], ACT.Copy))
            evac(act, 1, "b_q", qk_out(12, 2))
            evac(act, 1, "b_kv", lambda bank, j, it: copy(V1[:, :, 768:896],
                                                          bank[:, 0:256].rearrange("p (t n) -> p t n", t=2), ACT.Copy))
            evac(act, 1, "c_qk", qk_out(17, 1))
            evac(act, 1, "c_v", lambda bank, j, it: copy(V1[:, 1, 896:1152], bank[:, 0:CHUNK], ACT.Copy))

            def gate_out(bank, j, it):
                return copy(one(GATE, 2 * j + 1, 2, it), bank[:, 0:T1], ACT.Sigmoid,
                            bias=par[:, span(PARAMS["b_gate"][0] + 2 * j + 1, 2, it)])

            evac(act, 1, "gates", gate_out)
            act.wait_ge(sem("gates_v"), 12)
            copy(GATE[:, 0:24:2, :], GATE[:, 0:24:2, :], ACT.Sigmoid)
            bar()

            def softmax1(u):
                br, h, qt, qi, ki, qh, kh, vi, o = unit1(u)
                nk = P * (qt + 1)
                n = len(qi) * nk
                b = u % 2
                if u >= 2:
                    act.wait_ge(sem("u_turns"), u - 1)
                if br == "c":
                    act.wait_ge(sem("u_scores"), u + 1)
                    if u > N_AB:
                        act.wait_ge(sem("u_probs"), u)
                    z = scores_bank(u)[:, 0, 0:nk]
                    copy(U_K[:, 0:nk], z, ACT.Sigmoid, scale=-1.0).then_inc(sem("u_keep"), 1)
                    copy(U_P[b][:, 0:nk], z, ACT.Sigmoid).then_inc(sem("u_read_a"), 1)
                    return
                act.wait_ge(sem("u_max"), u + 1)
                if br == "b":
                    copy(STAT[:, 8 + b:9 + b], STAT[:, b:b + 1], ACT.Exp, bias=r_("sinks", h, 1))\
                        .then_inc(sem("u_sink"), 1)
                copy(U_P[b][:, 0:n], U_L[b][:, 0:n], ACT.Exp, bias=STAT[:, b:b + 1],
                     accum_out=STAT[:, 4 + b:5 + b]).then_inc(sem("u_exp"), 1)

            def out1(u):
                br, h, qt, qi, ki, qh, kh, vi, o = unit1(u)
                act.wait_ge(sem("u_out"), u + 1)
                rows_ = slice(HD * qh, HD * qh + HD)
                copy(O1[rows_, o, qt * P:(qt + 1) * P], PB[rows_, 0, u % 2, 0:P], ACT.Copy)\
                    .then_inc(sem("u_out_read"), 1)

            for u in range(len(units1) + 1):
                if u < len(units1):
                    softmax1(u)
                if u >= 1:
                    out1(u - 1)
            bar()
            bar()
            evac(act, 1, "out", lambda bank, j, it: copy(HO1[:, 2 * j + 1, :], bank[:, 0:T1], ACT.Copy))
            bar()
            norm_act(act, "n2", lambda k: HO1[:, k, :], T1)
            bar()
            norm_act(act, "n3", x1, T1)

            c0, g0 = PLAN["up"][0], GROUPS["up"]
            W2, CB = PARAMS["conv_w"][0] + 2 * 64, PARAMS["conv_b"][0]

            def up(it):
                for i in range(2):
                    for v in range(2):
                        j = 2 * i + v
                        g = g0 + j
                        act.wait_ge(chunk_done, c0 + j + 1 + 4 * it)
                        if not isinstance(it, int) and v == 0:
                            act.wait_ge(sem("up_prod"), 2 * it + (i - 1))
                        for t in range(2):
                            tile = 32 * v + 2 * i + t
                            ins = copy(UP[:, i, v, t * T1:(t + 1) * T1], PB[:, g % 2, t, 0:T1], ACT.Identity,
                                       scale=par[:, span(W2 + tile, 4, it)], bias=par[:, span(CB + tile, 4, it)])
                        ins.then_inc(sem("up_mid"), 1)
                        if v == 0:
                            act.wait_ge(evacuated[g % 2], 2 * (g // 2) + 2 + 4 * it)
                            copy(UP[:, i, 0, :], UP[:, i, 0, :], ACT.Gelu_apprx_tanh).then_inc(sem("up_gelu"), 1)
            act.wait_ge(sem("n3_h"), KT)
            repeat(act, 8, up, True)
            bar()
            evac(act, 1, "down", lambda bank, j, it: copy(one(DN1, 2 * j + 1, 2, it), bank[:, 0:T1], ACT.Copy),
                 share=4)
            bar()
            norm_act(act, "n4", lambda k: DN1[:, k, :], T1)
            bar()

            for la in range(DEPTH_2):
                T = TT if la == 0 else T1
                halves = T // T1
                evac(act, 1, f"ada{la}", lambda bank, j, it: copy(ADA[0:2, span(2 * j + 1, 2, it, P)],
                                                                  bank[0:2, 0:P], ACT.Copy))
                bar()
                norm_act(act, f"m1{la}", lambda k: X[:, k, :], TT)

                def shift(tag, part, n_half):
                    for k in range(KT):
                        for s in range(n_half):
                            act.wait_ge(sem("mod_scaled"), past(tag) + n_half * k + s + 1)
                            cols = slice(s * T1, (s + 1) * T1)
                            copy(H[:, k, cols], H[:, k, cols], ACT.Identity, bias=mod_(la, part, k, s))\
                                .then_inc(sem("mod_shifted"), 1)

                shift(f"m1{la}", 0, 2)
                evac(act, 1, f"q{la}", lambda bank, j, it: copy(LQ[:, 2 * j + 1, 0:T], bank[:, 0:T], ACT.Copy, scale=SCALE))
                evac(act, 1, f"k{la}", lambda bank, j, it: copy(LK[:, 2 * j + 1, :], bank[:, 0:TT], ACT.Copy))
                evac(act, 1, f"v{la}", lambda bank, j, it: copy(
                    LV[:, 2:4, CHUNK * j:CHUNK * (j + 1)], bank.rearrange("p (t n) -> p t n", t=2), ACT.Copy))
                bar()
                bar()
                us = units2(la)

                def exps2(u):
                    h, qt, k0, nk = us[u]
                    b = u % 2
                    act.wait_ge(sem("w_max"), LAYER["w_max"] * la + u + 1)
                    if u >= 2:
                        act.wait_ge(sem("w_turns"), LAYER["w_turns"] * la + u - 1)
                    for cc in range(2):
                        copy(AT_P[b][:, cc, 0:nk], scores_bank(u)[:, cc, 0:nk], ACT.Exp,
                             bias=STAT[:, 2 * b + cc:2 * b + cc + 1],
                             accum_out=STAT[:, 4 + 2 * b + cc:5 + 2 * b + cc]).then_inc(sem("w_exp"), 1)

                def out2(u):
                    h, qt, k0, nk = us[u]
                    act.wait_ge(sem("w_out"), LAYER["w_out"] * la + u + 1)
                    copy(LQ[:, h, qt * P:(qt + 1) * P], PB[:, 0, u % 2, 0:P], ACT.Copy)\
                        .then_inc(sem("w_out_read"), 1)

                for u in range(len(us) + 1):
                    if u < len(us):
                        exps2(u)
                    if u >= 1:
                        out2(u - 1)
                bar()
                for h in range(8):
                    act.wait_ge(sem("sub_sum"), LAYER["sub_sum"] * la + h + 1)
                    if h >= 2:
                        act.wait_ge(sem("sub_out"), LAYER["sub_out"] * la + h - 1)
                    copy(SUB_R[h % 2][:, 0:T], PS[:, h % 2, 0:T], ACT.Sqrt, bias=EPS_C)\
                        .then_inc(sem("sub_root"), 1)
                bar()
                evac(act, 1, f"ga{la}", lambda bank, j, it: copy(MRG[:, 2 * j + 1, 0:T], bank[:, 0:T], ACT.Sigmoid))
                act.wait_ge(sem("ga_v"), LAYER["ga_v"] * la + 4)
                copy(MRG[:, 0:8:2, 0:T], MRG[:, 0:8:2, 0:T], ACT.Sigmoid)
                bar()
                bar()
                E1 = XD[0].rearrange("p (a b) -> p a b", a=4)
                E2 = XD[1].rearrange("p (a b) -> p a b", a=4)
                act.wait_ge(sem("dt_abs"), LAYER["dt_abs"] * la + 1)
                copy(E1, E1, ACT.Exp, scale=-1.0).then_inc(sem("dt_exp"), 1)
                act.wait_ge(sem("dt_one"), LAYER["dt_one"] * la + 1)
                copy(WD, E2, ACT.Ln).then_inc(sem("dt_ln"), 1)
                act.wait_ge(sem("dt_rest"), LAYER["dt_rest"] * la + 2)
                copy(ECS, CS, ACT.Exp)
                copy(WD, WD, ACT.Exp).then_inc(sem("dt_wd"), 1)
                copy(CHD, CHD, ACT.Exp)
                bar()

                (c0, _), g0 = PLAN[f"ssd{la}"], GROUPS[f"ssd{la}"]
                W0, CBs = PARAMS[f"sconv_w{la}"][0], PARAMS[f"sconv_b{la}"][0]

                def middle(g):
                    b = g % 2
                    for j in range(2):
                        gg = g0 + 2 * g + j
                        act.wait_ge(chunk_done, c0 + 2 * g + j + 1)
                        if g >= 2 and j == 0:
                            act.wait_ge(sem("s_within"), LAYER["s_within"] * la + 4 * (g - 1))
                        for t in range(2):
                            i = 2 * j + t
                            Tc = T if i == 3 else TT
                            ch = channels(g, i)
                            copy(CV[b][:, i, 0:Tc], PB[:, gg % 2, t, 0:Tc], ACT.Identity,
                                 scale=par[:, W0 + 2 * 32 + ch:W0 + 2 * 32 + ch + 1],
                                 bias=par[:, CBs + ch:CBs + ch + 1]).then_inc(sem("s_mid"), 1)

                def silus(g):
                    b = g % 2
                    for i in range(4):
                        Tc = T if i == 3 else TT
                        gg = g0 + 2 * g + i // 2
                        act.wait_ge(evacuated[gg % 2], 2 * (gg // 2) + i % 2 + 1)
                        copy(CV[b][:, i, 0:Tc], CV[b][:, i, 0:Tc], ACT.Silu).then_inc(sem("s_conv"), 1)

                def turned(g):
                    for i, bank in enumerate((PA[0], PA[1], PS[:, 0])):
                        act.wait_ge(sem("s_turns"), LAYER["s_turns"] * la + 3 * g + i + 1)
                        src = bank.rearrange("p (t n) -> p t n", t=4)
                        if i == 0 and g >= 1:
                            act.wait_ge(sem("s_y"), LAYER["s_y"] * la + (2 if la == 0 else 1) * g)
                            act.wait_ge(sem("s_yi"), LAYER["s_yi"] * la + g)
                            act.wait_ge(sem("s_xc"), LAYER["s_xc"] * la + 8 * g)
                        dst = BT[:, :, :] if i == 2 else XG[:, :, i * P:(i + 1) * P]
                        copy(dst, src, ACT.Copy).then_inc(sem("s_turned"), 1)

                def decay_exps(g):
                    tok = slice(0, 4 if la == 0 else 2)
                    for r in range(4):
                        for d in range(2):
                            n = 2 * (4 * g + r) + d
                            act.wait_ge(sem("s_diff"), LAYER["s_diff"] * la + n + 1)
                            copy(MB[r % 2][:, d, tok, :], MB[r % 2][:, d, tok, :], ACT.Exp)\
                                .then_inc(sem("s_exp"), 1)

                middle(0)
                silus(0)
                for g in range(SSD_GROUPS):
                    if g + 1 < SSD_GROUPS:
                        middle(g + 1)
                    turned(g)
                    if g + 1 < SSD_GROUPS:
                        silus(g + 1)
                    decay_exps(g)
                bar()
                (c0, n), g0 = PLAN[f"z{la}"], GROUPS[f"z{la}"]
                w = CHUNK * (T // P) // 2
                for j in range(n):
                    act.wait_ge(chunk_done, c0 + j + 1)
                    if j >= 2:
                        act.wait_ge(sem("z_used"), LAYER["z_used"] * la + j - 1)
                    for s in range(2):
                        copy(ZT[j % 2][:, s * w:(s + 1) * w], PB[:, (g0 + j) % 2, s, 0:w], ACT.Silu)\
                            .then_inc(evacuated[(g0 + j) % 2], 1)
                bar_z = T // P
                act.wait_ge(sem("z_used"), LAYER["z_used"] * la + n)
                for t in range(bar_z):
                    copy(YT[:, 0:4, :], Y[:, t, :].rearrange("p (a b) -> p a b", a=4), ACT.Square,
                         accum_out=STAT[:, t:t + 1]).then_inc(sem("z_sq"), 1)
                    act.wait_ge(sem("z_sq"), LAYER["z_sq"] * la + t + 1)
                copy(STAT[:, 4:4 + bar_z], STAT[:, 0:bar_z], ACT.Sqrt, scale=1.0 / SSD_INNER, bias=EPS_C)\
                    .then_inc(sem("z_root"), 1)
                bar()
                for i in range(1, 16, 2):
                    act.wait_ge(sem("yt"), LAYER["yt"] * la + i + 1)
                    if i >= 1:
                        act.wait_ge(sem("yt_read"), LAYER["yt_read"] * la + i)
                    copy(YT[:, i, 0:T], PS[:, i % 2, 0:T], ACT.Identity, scale=p_(f"ssd_g{la}", i))\
                        .then_inc(sem("yt_read"), 1)
                bar()
                evac(act, 1, f"ssd_o{la}", lambda bank, j, it: copy(one(MIX, 2 * j + 1, 2, it)[:, 0:T],
                                                                   bank[:, 0:T], ACT.Copy), share=2)
                evac(act, 1, f"gs{la}", lambda bank, j, it: copy(GS[:, 2 * j + 1, 0:T], bank[:, 0:T], ACT.Sigmoid))
                act.wait_ge(sem("gs_v"), LAYER["gs_v"] * la + 4)
                copy(GS[:, 0:8:2, 0:T], GS[:, 0:8:2, 0:T], ACT.Sigmoid).then_inc(sem("gs_done"), 1)
                bar()
                bar()
                norm_act(act, f"m2{la}", lambda k: X[:, k, 0:T], T)
                shift(f"m2{la}", 3, halves)
                evac(act, 1, f"mlp1{la}", lambda bank, j, it: copy(one(HID2, 2 * j + 1, 2, it)[:, 0:T],
                                                                  bank[:, 0:T], ACT.Relu))
                bar()
                bar()
            norm_act(act, "final", x1, T1)

        @block.vector
        def _(v):
            def bar():
                barrier(v, "dve")

            vec = nc.vector
            steps = [0]

            def then(ins):
                steps[0] += 1
                ins.then_inc(sem("dve_step"), 1)
                v.wait_ge(sem("dve_step"), steps[0])

            for col, value in ((ONE, 1.0), (ONE_D, 1.0 / D), (ONE_H, 1.0 / P), (EPS_C, EPS)):
                ins = vec.memset(col, value)
            ins.then_inc(sem("consts"), 1)
            v.wait_ge(loaded, 16 * 3)
            v.wait_ge(rows_in, 16 * 2)
            vec.tensor_scalar(NEG_SINK, r_("sinks"), -1.0, None, ALU.mult)
            for la in range(DEPTH_2):
                then(vec.tensor_tensor(r_(f"lam_q{la}"), r_(f"lam_q{la}"), r_(f"lam_k{la}"), ALU.mult))
                for i in range(2):
                    vec.reduce_sum(LAMS[:, 2 * la + i:2 * la + i + 1], r_(f"lam_q{la}", HD * i, HD), AX.X)\
                        .then_inc(sem("lam_dot"), 1)
                lam_init = 0.8 - 0.6 * math.exp(-0.3 * la)
                vec.tensor_scalar(p_(f"subln_g{la}"), p_(f"subln_g{la}"), 1.0 - lam_init, None, ALU.mult)
            v.wait_ge(sem("lam_exp"), 1)
            v.wait_ge(sem("a_exp"), DEPTH_2)
            for la in range(DEPTH_2):
                lam_init = 0.8 - 0.6 * math.exp(-0.3 * la)
                then(vec.tensor_tensor(NEG_LAM[:, la:la + 1], LAMS[:, 2 * la + 1:2 * la + 2],
                                       LAMS[:, 2 * la:2 * la + 1], ALU.subtract))
                vec.tensor_scalar(NEG_LAM[:, la:la + 1], NEG_LAM[:, la:la + 1], -lam_init, None, ALU.add)
                vec.tensor_scalar(r_(f"a_log{la}"), r_(f"a_log{la}"), -1.0, None, ALU.mult)
            v.wait_ge(sem("rev_sum"), 1)
            vec.tensor_copy(REV[0:N_BIAS, :], PA[1][0:N_BIAS, 0:N_REV]).then_inc(sem("rev"), 1)

            def x1(k):
                return X[:, k, 0:T1]

            def norm_scale(tag, src, dst, g, T, name):
                norm_dve(v, tag, src, T)
                for k in range(KT):
                    vec.scalar_tensor_tensor(dst(k), src(k), g(k), RSTD[:, 0:T], ALU.mult, ALU.mult)\
                        .then_inc(sem(f"{tag}_{name}"), 1)

            norm_scale("n1", x1, lambda k: H[:, k, 0:T1], lambda k: p_("pre_g", k), T1, "h")

            def qk_out(base, scaled):
                def op(bank, j, it):
                    return vec.tensor_scalar(A_QK[:, base + 2 * j, :], bank[:, 0:T1],
                                             SCALE if j < scaled else 1.0, None, ALU.mult)
                return op

            evac(v, 0, "a_qk", qk_out(0, 3))
            evac(v, 0, "a_v", lambda bank, j, it: vec.tensor_copy(V1[:, 0, CHUNK * j:CHUNK * (j + 1)], bank[:, 0:CHUNK]))
            evac(v, 0, "b_q", qk_out(12, 2))
            evac(v, 0, "b_kv", lambda bank, j, it: vec.tensor_copy(A_QK[:, 16, :], bank[:, 0:T1]))
            evac(v, 0, "c_qk", qk_out(17, 1))
            evac(v, 0, "c_v", lambda bank, j, it: vec.tensor_copy(V1[:, 0, 896:1152], bank[:, 0:CHUNK]))

            def gate_out(bank, j, it):
                return vec.tensor_scalar(one(GATE, 2 * j, 2, it), bank[:, 0:T1],
                                         par[:, span(PARAMS["b_gate"][0] + 2 * j, 2, it)], None, ALU.add)

            for i in range(N_BIAS // 2):
                v.wait_ge(sem("flip"), i + 1)
                vec.tensor_copy(BIAS[:, 2 * i:2 * i + 2, :], PS[:, i % 2, :].rearrange("p (a b) -> p a b", a=2))\
                    .then_inc(sem("flip_read"), 1)
            evac(v, 0, "gates", gate_out)
            v.drain().then_inc(sem("gates_v"), 12)
            bar()

            def rows1(u):
                br, h, qt, qi, ki, qh, kh, vi, o = unit1(u)
                nk = P * (qt + 1)
                off = 0 if qt == 1 else P
                b = u % 2
                if br == "c":
                    return
                S = scores_bank(u)
                v.wait_ge(sem("u_scores"), u + 1)
                L = U_L[b]
                if u >= 2:
                    v.wait_ge(sem("u_exp"), u - 1)
                if br == "a":
                    L2 = L[:, 0:2 * nk].rearrange("p (g n) -> p g n", g=2)
                    vec.tensor_tensor(L2, S[:, 0, 0:2 * nk].rearrange("p (g n) -> p g n", g=2),
                                      BIAS[:, h:h + 5:4, off:off + nk], ALU.add)
                    ins = vec.tensor_tensor(L[:, 2 * nk:3 * nk], S[:, 1, 0:nk], BIAS[:, 8 + h, off:off + nk], ALU.add)
                    n = 3 * nk
                else:
                    ins = vec.tensor_tensor(L[:, 0:nk], S[:, 0, 0:nk], BIAS[:, 12 + h, off:off + nk], ALU.add)
                    n = nk
                ins.then_inc(sem("u_read_v"), 1)
                v.wait_ge(sem("u_read_v"), u + 1)
                if br == "b":
                    then(vec.tensor_reduce(STAT[:, b:b + 1], L[:, 0:n], AX.X, ALU.max, negate=True))
                    vec.tensor_tensor(STAT[:, b:b + 1], STAT[:, b:b + 1], NEG_SINK[:, h:h + 1], ALU.min)\
                        .then_inc(sem("u_max"), 1)
                else:
                    vec.tensor_reduce(STAT[:, b:b + 1], L[:, 0:n], AX.X, ALU.max, negate=True)\
                        .then_inc(sem("u_max"), 1)

            def probs1(u):
                br, h, qt, qi, ki, qh, kh, vi, o = unit1(u)
                nk = P * (qt + 1)
                n = len(qi) * nk
                b = u % 2
                if br == "c":
                    v.wait_ge(sem("u_keep"), u - N_AB + 1)
                    off = 0 if qt == 1 else P
                    then(vec.tensor_tensor(U_K[:, 0:nk], U_K[:, 0:nk], c_("c_after", off, nk), ALU.max))
                    vec.memset(U_R[:, nk:nk + 1], 1.0)
                    then(vec.tensor_tensor_scan(U_R[:, 0:nk][:, ::-1], U_K[:, 0:nk][:, ::-1], U_K[:, 0:nk][:, ::-1],
                                                1.0, ALU.mult, ALU.bypass))
                    v.wait_ge(sem("u_read_a"), u - N_AB + 1)
                    then(vec.tensor_tensor(U_P[b][:, 0:nk], U_P[b][:, 0:nk], c_("c_before", off, nk), ALU.mult))
                    vec.tensor_tensor(U_P[b][:, 0:nk], U_P[b][:, 0:nk], U_R[:, 1:nk + 1], ALU.mult)\
                        .then_inc(sem("u_probs"), 1)
                else:
                    v.wait_ge(sem("u_exp"), u + 1)
                    if br == "b":
                        v.wait_ge(sem("u_sink"), u - 2 * A_HEADS + 1)
                        then(vec.tensor_tensor(STAT[:, 4 + b:5 + b], STAT[:, 4 + b:5 + b],
                                               STAT[:, 8 + b:9 + b], ALU.add))
                    then(vec.reciprocal(STAT[:, 12 + b:13 + b], STAT[:, 4 + b:5 + b]))
                    vec.tensor_scalar(U_P[b][:, 0:n], U_P[b][:, 0:n], STAT[:, 12 + b:13 + b], None, ALU.mult)\
                        .then_inc(sem("u_probs"), 1)
                nb = n // P
                v.wait_ge(sem("u_turns"), u + 1)
                if u >= 1:
                    v.wait_ge(sem("u_out"), u)
                if nb > 4:
                    vec.tensor_copy(U_T[:, 0:4, :], PA[0].rearrange("p (a b) -> p a b", a=4))
                    vec.tensor_copy(U_T[:, 4:6, :], PA[1][:, 0:256].rearrange("p (a b) -> p a b", a=2))\
                        .then_inc(sem("u_turned"), 1)
                else:
                    vec.tensor_copy(U_T[:, 0:nb, :], PA[0][:, 0:n].rearrange("p (a b) -> p a b", a=nb))\
                        .then_inc(sem("u_turned"), 1)

            for u in range(len(units1) + 1):
                if u < len(units1):
                    rows1(u)
                if u >= 1:
                    probs1(u - 1)
            bar()
            c0, g0 = PLAN["branches"][0], GROUPS["branches"]
            for j in range(4):
                g = g0 + j
                v.wait_ge(chunk_done, c0 + j + 1)
                for t in range(2):
                    k = 2 * j + t
                    vec.tensor_tensor(GATE[:, 16 + k, :], PS[:, g % 2, t * T1:(t + 1) * T1], GATE[:, 16 + k, :], ALU.mult)
                    vec.tensor_tensor(GATE[:, k, :], PB[:, g % 2, t, 0:T1], GATE[:, k, :], ALU.mult)
                    vec.tensor_tensor(GATE[:, 8 + k, :], PB[:, g % 2, t, T1:2 * T1], GATE[:, 8 + k, :], ALU.mult)\
                        .then_inc(evacuated[g % 2], 1)
            v.drain().then_inc(sem("branch_v"), 1)
            bar()
            evac(v, 0, "out", lambda bank, j, it: vec.tensor_copy(HO1[:, 2 * j, :], bank[:, 0:T1]))
            bar()

            def residual1(tag, src, g):
                norm_dve(v, tag, src, T1)
                for k in range(KT):
                    vec.scalar_tensor_tensor(src(k), src(k), p_(g, k), RSTD[:, 0:T1], ALU.mult, ALU.mult)\
                        .then_inc(sem(f"{tag}_part"), 1)
                for k in range(KT):
                    v.wait_ge(sem(f"{tag}_part"), k + 1)
                    vec.tensor_tensor(x1(k), x1(k), src(k), ALU.add)

            residual1("n2", lambda k: HO1[:, k, :], "post_g")
            bar()
            norm_scale("n3", x1, lambda k: H[:, k, 0:T1], lambda k: p_("ffn_pre_g", k), T1, "h")
            c0, g0 = PLAN["up"][0], GROUPS["up"]
            W0 = PARAMS["conv_w"][0]

            def up(it):
                for i in range(2):
                    for vv in range(2):
                        j = 2 * i + vv
                        g = g0 + j
                        v.wait_ge(sem("up_mid"), j + 1 + 4 * it)
                        for tap in (1, 0):
                            lag = 2 - tap
                            if tap == 0:
                                v.wait_ge(sem("up_tap"), j + 1 + 4 * it)
                            for t in range(2):
                                tile = 32 * vv + 2 * i + t
                                dst = UP[:, i, vv, t * T1 + lag:(t + 1) * T1]
                                ins = vec.scalar_tensor_tensor(
                                    dst, PB[:, g % 2, t, 0:T1 - lag], par[:, span(W0 + 64 * tap + tile, 4, it)],
                                    dst, ALU.mult, ALU.add)
                                if tap == 0:
                                    ins.then_inc(evacuated[g % 2], 1)
                            if tap == 1:
                                ins.then_inc(sem("up_tap"), 1)
            repeat(v, 8, up, True)
            bar()
            evac(v, 0, "down", lambda bank, j, it: vec.tensor_copy(one(DN1, 2 * j, 2, it), bank[:, 0:T1]), share=4)
            bar()
            residual1("n4", lambda k: DN1[:, k, :], "ffn_post_g")
            bar()

            for la in range(DEPTH_2):
                T = TT if la == 0 else T1
                halves = T // T1
                tok = slice(0, T // P)
                evac(v, 0, f"ada{la}", lambda bank, j, it: vec.tensor_copy(
                    ADA[0:2, span(2 * j, 2, it, P)], bank[0:2, 0:P]))
                bar()
                v.wait_ge(sem("mod_sum"), LAYER["mod_sum"] * la + 1)
                M = mod[:, la]
                then(vec.tensor_tensor(M, PA[1][:, 0:96].rearrange("p (n c) -> p n c", c=2),
                                       p_(f"ada_b{la}", 0, 48).unsqueeze(2).broadcast_to([P, 48, 2]), ALU.add))
                for part, g in ((1, f"mix_g{la}"), (4, f"mlp_g{la}")):
                    m = mod[:, la, part * KT:(part + 1) * KT, :]
                    then(vec.scalar_tensor_tensor(m, m, 1.0, p_(g, 0, KT).unsqueeze(2).broadcast_to([P, KT, 2]),
                                                  ALU.add, ALU.mult))

                def norm_mod(tag, part, n_half):
                    norm_dve(v, tag, lambda k: X[:, k, 0:n_half * T1], n_half * T1)
                    for k in range(KT):
                        for s_ in range(n_half):
                            cols = slice(s_ * T1, (s_ + 1) * T1)
                            vec.scalar_tensor_tensor(H[:, k, cols], X[:, k, cols], mod_(la, part, k, s_),
                                                     RSTD[:, cols], ALU.mult, ALU.mult)\
                                .then_inc(sem("mod_scaled"), 1)

                norm_mod(f"m1{la}", 1, 2)
                evac(v, 0, f"q{la}", lambda bank, j, it: vec.tensor_scalar(LQ[:, 2 * j, 0:T], bank[:, 0:T],
                                                                          SCALE, None, ALU.mult))
                evac(v, 0, f"k{la}", lambda bank, j, it: vec.tensor_copy(LK[:, 2 * j, :], bank[:, 0:TT]))
                evac(v, 0, f"v{la}", lambda bank, j, it: vec.tensor_copy(
                    LV[:, 0:2, CHUNK * j:CHUNK * (j + 1)], bank.rearrange("p (t n) -> p t n", t=2)))
                bar()
                for i in range(2 * KT):
                    v.wait_ge(sem("rot"), LAYER["rot"] * la + i + 1)
                    vec.tensor_tensor(ROT_T[i % 2], PS[:, i % 2, 0:T1], c_("sin"), ALU.mult)\
                        .then_inc(sem("rot_read"), 1)
                    v.wait_ge(sem("rot_read"), LAYER["rot_read"] * la + i + 1)
                    v.wait_ge(sem("rot_cos"), LAYER["rot_cos"] * la + i + 1)
                    x = (LQ if i < KT else LK)[:, i % KT, 0:T1]
                    vec.tensor_tensor(x, x, ROT_T[i % 2], ALU.add)
                bar()

                us = units2(la)

                def rows2(u):
                    h, qt, k0, nk = us[u]
                    b = u % 2
                    v.wait_ge(sem("w_scores"), LAYER["w_scores"] * la + u + 1)
                    if u >= 2:
                        v.wait_ge(sem("w_exp"), LAYER["w_exp"] * la + 2 * (u - 1))
                    vec.tensor_reduce(STAT[:, 2 * b:2 * b + 2], scores_bank(u)[:, :, 0:nk], AX.X, ALU.max, negate=True)\
                        .then_inc(sem("w_max"), 1)

                def probs2(u):
                    h, qt, k0, nk = us[u]
                    b = u % 2
                    n = nk // P
                    v.wait_ge(sem("w_exp"), LAYER["w_exp"] * la + 2 * u + 2)
                    r0, r1 = STAT[:, 8 + 2 * b:9 + 2 * b], STAT[:, 9 + 2 * b:10 + 2 * b]
                    then(vec.reciprocal(STAT[:, 8 + 2 * b:10 + 2 * b], STAT[:, 4 + 2 * b:6 + 2 * b]))
                    then(vec.tensor_tensor(r1, r1, NEG_LAM[:, la:la + 1], ALU.mult))
                    p0, p1 = AT_P[b][:, 0, 0:nk], AT_P[b][:, 1, 0:nk]
                    then(vec.tensor_scalar(p1, p1, r1, None, ALU.mult))
                    vec.scalar_tensor_tensor(p0, p0, r0, p1, ALU.mult, ALU.add).then_inc(sem("w_probs"), 1)
                    v.wait_ge(sem("w_turns"), LAYER["w_turns"] * la + u + 1)
                    if u >= 2:
                        v.wait_ge(sem("w_out"), LAYER["w_out"] * la + u - 1)
                    vec.tensor_copy(AT_T[b][:, 0:n, :], PA[b][:, 0:nk].rearrange("p (a b) -> p a b", a=n))\
                        .then_inc(sem("w_turned"), 1)

                for u in range(len(us) + 1):
                    if u < len(us):
                        rows2(u)
                    if u >= 1:
                        probs2(u - 1)
                bar()
                for h in range(8):
                    v.wait_ge(sem("sub_root"), LAYER["sub_root"] * la + h + 1)
                    r = SUB_R[h % 2][:, 0:T]
                    then(vec.reciprocal(r, r))
                    vec.scalar_tensor_tensor(LQ[:, h, 0:T], LQ[:, h, 0:T], p_(f"subln_g{la}"), r,
                                             ALU.mult, ALU.mult).then_inc(sem("sub_out"), 1)
                bar()
                evac(v, 0, f"ga{la}", lambda bank, j, it: vec.tensor_copy(MRG[:, 2 * j, 0:T], bank[:, 0:T]))
                v.drain().then_inc(sem("ga_v"), 4)
                bar()
                both(v, f"attn_o{la}", lambda bank, t, j, it: vec.tensor_tensor(
                    MRG[:, 2 * j + t, 0:T], bank[:, 0:T], MRG[:, 2 * j + t, 0:T], ALU.mult))
                bar()
                E1 = XD[0].rearrange("p (a b) -> p a b", a=4)
                E2 = XD[1].rearrange("p (a b) -> p a b", a=4)
                v.wait_ge(sem("dt_sum"), LAYER["dt_sum"] * la + 1)
                then(vec.tensor_tensor(DT, PS[:, 0, 0:256].rearrange("p (a b) -> p a b", a=4),
                                       r_(f"dt_bias{la}").unsqueeze(1).broadcast_to([P, 4, 64]), ALU.add))
                vec.scalar_tensor_tensor(E1, DT, -1.0, DT, ALU.mult, ALU.max).then_inc(sem("dt_abs"), 1)
                v.wait_ge(sem("dt_exp"), LAYER["dt_exp"] * la + 1)
                then(vec.tensor_scalar(DT, DT, 0.0, None, ALU.max))
                vec.tensor_scalar(E2, E1, 1.0, None, ALU.add).then_inc(sem("dt_one"), 1)
                v.wait_ge(sem("dt_one"), LAYER["dt_one"] * la + 1)
                then(vec.tensor_scalar(CS, E2, -1.0, None, ALU.add))
                then(vec.tensor_tensor(CS, E1, CS, ALU.subtract))
                then(vec.reciprocal(CHD, E2))
                then(vec.tensor_tensor(CS, CS, CHD, ALU.mult))
                v.wait_ge(sem("dt_ln"), LAYER["dt_ln"] * la + 1)
                then(vec.tensor_tensor(CS, CS, WD, ALU.add))
                then(vec.tensor_tensor(DT, DT, CS, ALU.add))
                vec.tensor_tensor(DTA, DT, r_(f"a_log{la}").unsqueeze(1).broadcast_to([P, 4, 64]), ALU.mult)\
                    .then_inc(sem("dt_a"), 1)
                v.wait_ge(sem("dt_cs"), LAYER["dt_cs"] * la + 1)
                vec.tensor_copy(CS, PS[:, 1, 0:256].rearrange("p (a b) -> p a b", a=4)).then_inc(sem("dt_rest"), 1)
                then(vec.tensor_copy(CHD, PS[:, 1, 256:512].rearrange("p (a b) -> p a b", a=4)))
                vec.tensor_tensor(WD, CHD, CS, ALU.subtract).then_inc(sem("dt_rest"), 1)
                v.wait_ge(sem("dt_wd"), LAYER["dt_wd"] * la + 1)
                vec.tensor_tensor(WD, WD, DT, ALU.mult)
                bar()

                (c0, _), g0 = PLAN[f"ssd{la}"], GROUPS[f"ssd{la}"]
                W0 = PARAMS[f"sconv_w{la}"][0]
                NY = 2 if la == 0 else 1

                def taps(g):
                    b = g % 2
                    for j in range(2):
                        gg = g0 + 2 * g + j
                        for t in range(2):
                            i = 2 * j + t
                            v.wait_ge(sem("s_mid"), LAYER["s_mid"] * la + 4 * g + i + 1)
                            n = (T if i == 3 else TT) // T1
                            ch = channels(g, i)
                            for tap in (0, 1, 3, 4):
                                s_ = tap - 2
                                lo, hi = max(0, -s_), T1 - max(0, s_)
                                dst = CV[b][:, i, 0:n * T1].rearrange("p (a b) -> p a b", a=n)[:, :, lo:hi]
                                src = PB[:, gg % 2, t, 0:n * T1].rearrange("p (a b) -> p a b", a=n)[:, :, lo + s_:hi + s_]
                                ins = vec.scalar_tensor_tensor(dst, src, par[:, W0 + 32 * tap + ch:W0 + 32 * tap + ch + 1],
                                                               dst, ALU.mult, ALU.add)
                                if tap == 4:
                                    ins.then_inc(evacuated[gg % 2], 1)
                                else:
                                    then(ins)

                def states(g):
                    v.wait_ge(sem("s_cb"), LAYER["s_cb"] * la + g + 1)
                    for d, tri in enumerate((c_("tri_le"), c_("tri_ge"))):
                        n = T // P
                        vec.tensor_tensor(CBM[:, d, tok, :], PS[:, 1, 0:T].rearrange("p (a b) -> p a b", a=n),
                                          tri.unsqueeze(1).broadcast_to([P, n, P]), ALU.mult)\
                            .then_inc(sem("s_cbm"), 1)
                    for i in range(3):
                        for d, order in enumerate((F_ORDER, B_ORDER)):
                            n = 6 * g + 2 * i + d
                            t = order[i]
                            heads = slice(32 * d + 4 * g, 32 * d + 4 * g + 4)
                            v.wait_ge(sem("s_delta"), LAYER["s_delta"] * la + 6 * g + 2 * i + 2)
                            if inter_count(la, g, i - 1) > 0:
                                v.wait_ge(sem("s_inter"), LAYER["s_inter"] * la + inter_count(la, g, i - 1))
                            delta = PA[0][:, 256 * d:256 * d + 256]
                            if i == 0:
                                vec.tensor_copy(HT[d], delta).then_inc(sem("s_state"), 1)
                            else:
                                hv = HT[d].rearrange("p (a b) -> p a b", a=4)
                                v.wait_ge(sem("s_state"), LAYER["s_state"] * la + n - 1)
                                then(vec.tensor_tensor(hv, hv, CHD[:, t, heads].unsqueeze(2).broadcast_to([P, 4, HD]),
                                                       ALU.mult))
                                vec.tensor_tensor(HT[d], HT[d], delta, ALU.add).then_inc(sem("s_state"), 1)
                        for d, order in enumerate((F_ORDER, B_ORDER)):
                            t = order[i + 1]
                            if not live(la, t):
                                continue
                            heads = slice(32 * d + 4 * g, 32 * d + 4 * g + 4)
                            v.wait_ge(sem("s_inter"), LAYER["s_inter"] * la + inter_count(la, g, i))
                            v.wait_ge(sem("s_yi"), LAYER["s_yi"] * la + g + 1)
                            then(vec.tensor_tensor(YT2[d].rearrange("p (a b) -> p a b", a=4),
                                                   PA[1][:, 256 * d:256 * d + 256].rearrange("p (a b) -> p a b", a=4),
                                                   ECS[:, t, heads].unsqueeze(2).broadcast_to([P, 4, HD]), ALU.mult))
                            vec.tensor_tensor(YI[:, t, :], YI[:, t, :], YT2[d], ALU.add)\
                                .then_inc(sem("s_inter_read"), 1)

                def diff(g, r):
                    n = 4 * g + r
                    if n >= 2:
                        v.wait_ge(sem("s_within"), LAYER["s_within"] * la + n - 1)
                    for d in range(2):
                        nt = T // P
                        hh = 32 * d + 4 * g + r
                        v.wait_ge(sem("s_bc"), LAYER["s_bc"] * la + 2 * n + d + 1)
                        for t in range(nt):
                            ins = vec.tensor_scalar(MB[r % 2][:, d, t, :], PS[:, d, t * P:(t + 1) * P],
                                                    CS[:, t, hh:hh + 1], 0.0, ALU.subtract, ALU.min)
                        ins.then_inc(sem("s_diff"), 1)

                def masked(g, r):
                    n = 4 * g + r
                    for d in range(2):
                        v.wait_ge(sem("s_exp"), LAYER["s_exp"] * la + 2 * n + d + 1)
                        if r == 0:
                            v.wait_ge(sem("s_cbm"), LAYER["s_cbm"] * la + 2 * g + d + 1)
                        m = MB[r % 2][:, d, tok, :]
                        vec.tensor_tensor(m, m, CBM[:, d, tok, :], ALU.mult)\
                            .then_inc(sem("s_m"), 1)

                def sum_y(g):
                    v.wait_ge(sem("s_within"), LAYER["s_within"] * la + 4 * g + 4)
                    v.wait_ge(sem("s_inter_read"), LAYER["s_inter_read"] * la + inter_count(la, g, 2))
                    for i in range(NY):
                        vec.tensor_tensor(Y[:, 2 * i:2 * i + 2, 256 * g:256 * g + 256],
                                          PA[i].rearrange("p (a b) -> p a b", a=2),
                                          YI[:, 2 * i:2 * i + 2, :], ALU.add).then_inc(sem("s_y"), 1)

                taps(0)
                for g in range(SSD_GROUPS):
                    if g + 1 < SSD_GROUPS:
                        taps(g + 1)
                    states(g)
                    diff(g, 0)
                    for r in range(4):
                        if r < 3:
                            diff(g, r + 1)
                        masked(g, r)
                    sum_y(g)
                bar()
                (c0, n), g0 = PLAN[f"z{la}"], GROUPS[f"z{la}"]
                nt = T // P
                for j in range(n):
                    gg = g0 + j
                    v.wait_ge(evacuated[gg % 2], 2 * (gg // 2) + 2)
                    y = Y[:, tok, CHUNK * j:CHUNK * (j + 1)]
                    vec.tensor_tensor(y, y, ZT[j % 2][:, 0:nt * CHUNK].rearrange("p (a b) -> p a b", a=nt), ALU.mult)\
                        .then_inc(sem("z_used"), 1)
                v.wait_ge(sem("z_root"), LAYER["z_root"] * la + 1)
                then(vec.reciprocal(STAT[:, 8:8 + nt], STAT[:, 4:4 + nt]))
                for t in range(nt):
                    vec.tensor_scalar(Y[:, t, :], Y[:, t, :], STAT[:, 8 + t:9 + t], None, ALU.mult)
                bar()
                for i in range(0, 16, 2):
                    v.wait_ge(sem("yt"), LAYER["yt"] * la + i + 1)
                    if i >= 1:
                        v.wait_ge(sem("yt_read"), LAYER["yt_read"] * la + i)
                    vec.tensor_scalar(YT[:, i, 0:T], PS[:, i % 2, 0:T], p_(f"ssd_g{la}", i), None, ALU.mult)\
                        .then_inc(sem("yt_read"), 1)
                bar()
                evac(v, 0, f"ssd_o{la}", lambda bank, j, it: vec.tensor_copy(one(MIX, 2 * j, 2, it)[:, 0:T],
                                                                           bank[:, 0:T]), share=2)
                evac(v, 0, f"gs{la}", lambda bank, j, it: vec.tensor_copy(GS[:, 2 * j, 0:T], bank[:, 0:T]))
                v.drain().then_inc(sem("gs_v"), 4)
                v.wait_ge(sem("gs_done"), LAYER["gs_done"] * la + 1)
                for g in range(4):
                    gg = GROUPS[f"gs{la}"] + g
                    v.wait_ge(evacuated[gg % 2], 2 * (gg // 2) + 2)
                for k in range(KT):
                    then(vec.tensor_tensor(MIX[:, k, 0:T], MIX[:, k, 0:T], GS[:, k, 0:T], ALU.mult))
                    vec.tensor_tensor(MRG[:, k, 0:T], MRG[:, k, 0:T], MIX[:, k, 0:T], ALU.add)
                bar()

                def add_to(part):
                    def op(bank, t, j, it):
                        for s_ in range(halves):
                            cols = slice(s_ * T1, (s_ + 1) * T1)
                            x = one(X, 2 * j + t, 2, it)[:, cols]
                            m = mod[:, la, span(part * KT + 2 * j + t, 2, it), s_:s_ + 1].rearrange("p a b -> p (a b)")
                            ins = vec.scalar_tensor_tensor(x, bank[:, cols], m, x, ALU.mult, ALU.add)
                        return ins
                    return op

                both(v, f"out2{la}", add_to(2))
                bar()
                norm_mod(f"m2{la}", 4, halves)
                evac(v, 0, f"mlp1{la}", lambda bank, j, it: vec.tensor_scalar(one(HID2, 2 * j, 2, it)[:, 0:T], bank[:, 0:T],
                                                                            0.0, None, ALU.max))
                bar()
                both(v, f"mlp2{la}", add_to(5), 4)
                bar()
            norm_scale("final", x1, lambda k: H[:, k, 0:T1], lambda k: p_("final_g", k), T1, "h")

        @block.gpsimd
        def _(pool):
            def bar():
                barrier(pool, "pool")

            gp = nc.gpsimd
            pool.dma_start(row[:, :], rows.broadcast_to([P, N_ROWS])).then_inc(rows_in, 16)
            pool.dma_start(wdt[:, :, :, :], w_dt).then_inc(rows_in, 16)
            pool.dma_start(REL[0:36, 0:N_BIAS], rel_bias).then_inc(sem("hot"), 16)
            pool.dma_start(HOT[0:36, :], rev_hot).then_inc(sem("hot"), 16)
            pool.wait_ge(loaded, 16 * 3)
            pool.wait_ge(sem("rev"), 1)
            pool.dma_start(scratch, REV[0:N_BIAS, :]).then_inc(sem("rev_out"), 16)
            pool.wait_ge(sem("rev_out"), 16)
            pool.dma_start(BIAS_UP, bass.AP(scratch.tensor, 0, [[1, P], [N_REV, N_BIAS], [1, 256]]))\
                .then_inc(sem("bias_in"), 16)
            pool.wait_ge(sem("bias_in"), 16)
            bar()
            bar()
            pool.wait_ge(sem("branch_v"), 1)
            for i in (8, 16):
                gp.tensor_tensor(GATE[:, 0:8, :], GATE[:, 0:8, :], GATE[:, i:i + 8, :], ALU.add)\
                    .then_inc(sem("merged"), 1)
                pool.wait_ge(sem("merged"), i // 8)
            bar()
            bar()
            bar()
            c0, g0 = PLAN["up"][0], GROUPS["up"]

            def up(it):
                for i in range(2):
                    g = g0 + 2 * i + 1
                    pool.wait_ge(sem("up_gelu"), 2 * it + i + 1)
                    pool.wait_ge(evacuated[g % 2], 2 * (g // 2) + 2 + 4 * it)
                    gp.tensor_tensor(one(HID1_PAIRS, i, 2, it), UP[:, i, 0, :], UP[:, i, 1, :], ALU.mult)\
                        .then_inc(sem("up_prod"), 1)
            repeat(pool, 8, up)
            bar()
            bar()
            bar()
            for la in range(DEPTH_2):
                T = TT if la == 0 else T1
                bar()
                bar()
                for i in range(2 * KT):
                    pool.wait_ge(sem("rot"), LAYER["rot"] * la + i + 1)
                    x = (LQ if i < KT else LK)[:, i % KT, 0:T1]
                    gp.tensor_tensor(x, x, c_("cos"), ALU.mult).then_inc(sem("rot_cos"), 1)
                bar()
                bar()
                for h in range(8):
                    if h >= 2:
                        pool.wait_ge(sem("sub_sum"), LAYER["sub_sum"] * la + h - 1)
                    gp.tensor_tensor(SUB_S[h % 2][:, 0:T], LQ[:, h, 0:T], LQ[:, h, 0:T], ALU.mult)\
                        .then_inc(sem("sub_sq"), 1)
                bar()
                bar()
                bar()
                bar()
                NY = 2 if la == 0 else 1

                for g in range(SSD_GROUPS):
                    pool.wait_ge(sem("s_turned"), LAYER["s_turned"] * la + 3 * g + 2)
                    if g >= 1:
                        pool.wait_ge(sem("s_y"), LAYER["s_y"] * la + NY * g)
                    gp.tensor_tensor(YI.rearrange("p t (r n) -> p t r n", r=4), XG.rearrange("p t (r n) -> p t r n", r=4),
                                     r_(f"ssd_d{la}", 4 * g, 4).unsqueeze(1).unsqueeze(3).broadcast_to([P, 4, 4, HD]),
                                     ALU.mult).then_inc(sem("s_yi"), 1)
                    for i in range(3):
                        for d, order in enumerate((F_ORDER, B_ORDER)):
                            n = 6 * g + 2 * i + d
                            t = order[i]
                            if n >= 2:
                                pool.wait_ge(sem("s_delta"), LAYER["s_delta"] * la + n - 1)
                            heads = slice(32 * d + 4 * g, 32 * d + 4 * g + 4)
                            gp.tensor_tensor(XD[d].rearrange("p (a b) -> p a b", a=4),
                                             XG[:, t, :].rearrange("p (a b) -> p a b", a=4),
                                             WD[:, t, heads].unsqueeze(2).broadcast_to([P, 4, HD]), ALU.mult)\
                                .then_inc(sem("s_xd"), 1)
                    for r in range(4):
                        n = 4 * g + r
                        if n >= 2:
                            pool.wait_ge(sem("s_within"), LAYER["s_within"] * la + n - 1)
                        for d in range(2):
                            hh = 32 * d + 4 * g + r
                            gp.tensor_tensor(XC[r % 2][:, d, :, :], XG[:, :, HD * r:HD * r + HD],
                                             DT[:, :, hh:hh + 1].broadcast_to([P, 4, HD]), ALU.mult)\
                                .then_inc(sem("s_xc"), 1)
                bar()
                bar()
                bar()
                bar()
                bar()
                (c0, n), g0 = PLAN[f"mlp1{la}"], GROUPS[f"mlp1{la}"]

                def square(it):
                    for j in range(4):
                        g = g0 + j
                        pool.wait_ge(evacuated[g % 2], 2 * (g // 2) + 2 + 4 * it)
                        hh = HID2[:, span2(j, 4, it), 0:T]
                        gp.tensor_tensor(hh, hh, hh, ALU.mult)
                repeat(pool, n // 4, square)
                bar()
                bar()


def _weights(w):
    K, N = w.shape
    return w.reshape(K // D, KT, P, N // CHUNK, CHUNK).transpose(3, 0, 2, 1, 4).reshape(-1, P, KT, CHUNK)


def _stream(a):
    w = a["w_in"][0]
    perm = [HD * h + i for t in range(4) for h in (t, t + 4) for i in range(HD)]
    c = {}
    c["a_qk"] = _weights(w[:, 0:1536])
    c["a_v"] = _weights(w[:, 1536:2304])
    c["b_q"] = _weights(w[:, 2304:2816][:, perm])
    c["b_kv"] = _weights(w[:, 2816:3072])
    c["c_qk"] = _weights(w[:, 3072:3584])
    c["c_v"] = _weights(w[:, 3584:3840])
    c["gates"] = _weights(w[:, 3840:6912])
    c["branches"] = _weights(np.concatenate([a["w_br_a"][0], a["w_br_b"][0][perm], a["w_br_c"][0]], 0))
    c["out"] = _weights(a["w_out"][0])
    up = _weights(a["w_up"][0])
    c["up"] = np.stack([up[:16], up[16:]], 1).reshape(32, P, KT, CHUNK)
    c["down"] = _weights(a["w_down"][0])
    for la in range(DEPTH_2):
        w = a["w_in_2"][la]
        c[f"ada{la}"] = _weights(a["ada_w_2"][la])
        c[f"q{la}"] = _weights(w[:, 0:1024])
        c[f"k{la}"] = _weights(w[:, 1024:2048])
        c[f"v{la}"] = _weights(w[:, 2048:3072])
        c[f"z{la}"] = _weights(w[:, 3072:5120])
        xs, b, cc = w[:, 5120:7168], w[:, 7168:8192], w[:, 8192:9216]
        parts = []
        for g in range(SSD_GROUPS):
            parts += [xs[:, 256 * g:256 * g + 256], b[:, P * g:P * g + P], cc[:, P * g:P * g + P]]
        c[f"ssd{la}"] = _weights(np.concatenate(parts, 1))
        c[f"ga{la}"] = _weights(w[:, 9280:10304])
        c[f"gs{la}"] = _weights(w[:, 10304:11328])
        c[f"attn_o{la}"] = _weights(a["w_attn_o_2"][la])
        c[f"ssd_o{la}"] = _weights(a["w_ssd_o_2"][la])
        c[f"out2{la}"] = _weights(a["w_out_2"][la])
        c[f"mlp1{la}"] = _weights(a["w_mlp1_2"][la])
        c[f"mlp2{la}"] = _weights(a["w_mlp2_2"][la])
    out = np.empty((N_CHUNKS, P, KT, CHUNK), np.float32)
    for name, (at, n) in PLAN.items():
        assert len(c[name]) == n, name
        out[at:at + n] = c[name]
    return out


def _columns(v):
    return np.ascontiguousarray(v).reshape(-1, P).T


def _params(a):
    c = {"pre_g": a["attn_pre_norm"], "post_g": a["attn_post_norm"], "ffn_pre_g": a["ffn_pre_norm"],
         "ffn_post_g": a["ffn_post_norm"], "b_gate": a["b_gate"], "conv_w": a["conv_w"], "conv_b": a["conv_b"],
         "final_g": a["final_norm_g_2"], "cvec": np.stack([a["c_2"][0], a["c_ctx_2"]])}
    for la in range(DEPTH_2):
        c |= {f"ada_b{la}": a["ada_b_2"][la], f"mix_g{la}": a["norm_mix_g_2"][la], f"sconv_w{la}": a["conv_w_2"][la],
              f"sconv_b{la}": a["conv_b_2"][la], f"subln_g{la}": a["attn_subln_g_2"][la],
              f"ssd_g{la}": a["ssd_norm_g_2"][la], f"mlp_g{la}": a["norm_mlp_g_2"][la]}
    return np.concatenate([_columns(c[name]) for name in PARAMS], 1)


def _rows(a):
    c = {"sinks": a["sinks"]}
    for la in range(DEPTH_2):
        c |= {f"dt_bias{la}": np.concatenate([a["dt_bias_f_2"][la], a["dt_bias_b_2"][la]]),
              f"a_log{la}": np.concatenate([a["a_log_f_2"][la], a["a_log_b_2"][la]]), f"ssd_d{la}": a["ssd_d_2"][la],
              f"lam_q{la}": np.concatenate([a["lambda_q1_2"][la], a["lambda_q2_2"][la]]),
              f"lam_k{la}": np.concatenate([a["lambda_k1_2"][la], a["lambda_k2_2"][la]])}
    return np.concatenate([c[name].reshape(1, -1) for name in ROWS], 1)


def _consts():
    i = np.arange(P)
    before = np.zeros((P, 2 * P), np.float32)
    before[:, :P] = 1
    before[:, P:] = i[None, :] < i[:, None]
    rot = np.zeros((P, P), np.float32)
    for m in range(P):
        if m % HD < HD // 2:
            rot[m + HD // 2, m] = -1
        else:
            rot[m - HD // 2, m] = 1
    t = np.arange(T1)
    inv = np.float32(10000.0) ** (-np.arange(HD // 4, dtype=np.float32) / (HD // 4))
    ang = np.concatenate([(t // GRID_W).astype(np.float32)[:, None] * inv,
                          (t % GRID_W).astype(np.float32)[:, None] * inv], 1)
    wide = lambda x: np.tile(x.T, (4, 1))
    c = {"ident": np.eye(P), "tri_le": i[:, None] <= i[None, :], "tri_ge": i[:, None] >= i[None, :], "rot": rot,
         "flip": np.eye(P)[::-1], "cos": wide(np.cos(ang)), "sin": wide(np.sin(ang)), "c_before": before, "c_after": 1 - before}
    return np.concatenate([np.asarray(c[name], np.float32) for name in CONSTS], 1)


def _hot():
    dist = (N_REV // 3 * 2 - 1) - np.arange(N_REV)
    far = np.maximum(dist, 1).astype(np.float32)
    large = 16 + (np.log(far / np.float32(16)) / np.float32(math.log(2048 / 16)) * np.float32(16)).astype(np.int32)
    bucket = np.where(dist < 16, np.maximum(dist, 0), np.minimum(large, 31))
    hot = np.zeros((36, N_REV), np.float32)
    hot[bucket, np.arange(N_REV)] = 1
    seen = [dist <= 128, dist % 4 == 0, dist % 16 == 0, dist <= 127]
    for i, s in enumerate(seen):
        hot[32 + i] = ~(s & (dist >= 0))
    return hot


def kernel(**inputs):
    import concourse.bacc as _bacc
    from concourse.bass_utils import run_bass_kernel_spmd as _run

    a = {k: np.asarray(v) for k, v in inputs.items()}
    x = np.concatenate([a["x"][0], a["ctx_2"][0]], 0)
    rel = np.zeros((36, N_BIAS), np.float32)
    rel[:32] = a["rel_bias"]
    for i in range(3):
        rel[32 + i, 4 * i:4 * i + 4] = NEG
    rel[35, 12:] = NEG
    w_dt = np.stack([w[:, 9216:9280].reshape(KT, P, 64).transpose(1, 0, 2) for w in a["w_in_2"]], 1)
    arrays = {
        "xT": x.T.reshape(KT, P, TT).transpose(1, 0, 2), "stream": _stream(a), "params": _params(a),
        "rows": _rows(a), "consts": _consts(), "rel_bias": rel, "rev_hot": _hot(), "w_dt": w_dt,
    }
    arrays = {k: np.ascontiguousarray(v, dtype=np.float32) for k, v in arrays.items()}
    nc = _bacc.Bacc("TRN2", target_bir_lowering=False, num_devices=1)
    args = [nc.dram_tensor(k, v.shape, F32, kind="ExternalInput").ap() for k, v in arrays.items()]
    args.append(nc.dram_tensor("scratch", (N_BIAS, N_REV), F32).ap())
    args.append(nc.dram_tensor("out", (P, KT, T1), F32, kind="ExternalOutput").ap())
    program(nc, *args)
    r = _run(nc, [arrays], core_ids=[0])
    y = np.asarray(r.results[0]["out"])
    return y.transpose(2, 1, 0).reshape(1, T1, D)
```

```python
import math
from contextlib import ExitStack

import numpy as np

import concourse.bass as bass
from concourse import mybir

P = 128
D = 1024
KT = D // P
T1 = 256
TT = 512
DEPTH_2 = 2
CHUNK = 256
SLOTS = 4
FF = 4 * D
NEG = -1.0e30
HD = 64
A_HEADS, A_GROUPS, B_HEADS, C_HEADS = 4, 3, 8, 4
SSD_HEADS, SSD_GROUPS, SSD_INNER = 32, 8, 2048
SCALE = HD ** -0.5
EPS = 1e-6
GRID_W = 64

ALU = mybir.AluOpType
ACT = mybir.ActivationFunctionType
AX = mybir.AxisListType
F32 = mybir.dt.float32


def columns_of(parts):
    at, out = 0, {}
    for name, n in parts:
        out[name] = (at, n)
        at += n
    return out, at


def param_parts():
    parts = [("pre_g", KT), ("post_g", KT), ("ffn_pre_g", KT), ("ffn_post_g", KT), ("b_gate", 3 * KT),
             ("conv_w", 3 * 2 * FF // P), ("conv_b", 2 * FF // P), ("final_g", KT), ("cvec", 2 * KT)]
    for la in range(DEPTH_2):
        parts += [(f"ada_b{la}", 6 * KT), (f"mix_g{la}", KT), (f"sconv_w{la}", 5 * 32), (f"sconv_b{la}", 32),
                  (f"subln_g{la}", 1), (f"ssd_g{la}", 16), (f"mlp_g{la}", KT)]
    return parts


def row_parts():
    parts = [("sinks", B_HEADS)]
    for la in range(DEPTH_2):
        parts += [(f"dt_bias{la}", 64), (f"a_log{la}", 64), (f"ssd_d{la}", SSD_HEADS),
                  (f"lam_q{la}", 128), (f"lam_k{la}", 128)]
    return parts


def const_parts():
    return [("ident", P), ("tri_le", P), ("tri_ge", P), ("rot", P), ("flip", P), ("sel", 2), ("cos", T1), ("sin", T1),
            ("c_before", 2 * P), ("c_after", 2 * P)]


PARAMS, N_PARAMS = columns_of(param_parts())
ROWS, N_ROWS = columns_of(row_parts())
CONSTS, N_CONSTS = columns_of(const_parts())
N_REV = 384
N_BIAS = A_GROUPS * A_HEADS + B_HEADS


A_UNITS = 2 * (A_HEADS + B_HEADS + C_HEADS)
GATE_AT = [i for i in range(A_UNITS) if i % 8 in (1, 4, 6)]
ADA_CHUNKS = 6 * D // CHUNK


def attention_fill(la):
    if la == -1:
        return [([("gates", GATE_AT.index(u))] if u in GATE_AT else [])
                + ([("ada0", u)] if u < ADA_CHUNKS else []) for u in range(A_UNITS)]
    units = 32 if la == 0 else 16
    every = units // 4
    return [([(f"ga{la}", u // every)] if u % every == every // 2 else [])
            + ([(f"ada{la + 1}", u)] if la == 0 and u < ADA_CHUNKS else []) for u in range(units)]


def chunk_order():
    order = []

    def whole(*sections):
        for name, n in sections:
            order.extend((name, j) for j in range(n))

    whole(("a_qk", 6), ("a_v", 3), ("b_q", 2), ("b_kv", 1), ("c_qk", 2), ("c_v", 1))
    order.extend(x for unit in attention_fill(-1) for x in unit)
    whole(("branches", 4), ("out", 4), ("up", 32), ("down", 16))
    for la in range(DEPTH_2):
        whole((f"q{la}", 4), (f"k{la}", 4), (f"v{la}", 4))
        order.extend(x for unit in attention_fill(la) for x in unit)
        whole((f"ssd{la}", 2), (f"attn_o{la}", 4))
        for g in range(SSD_GROUPS):
            if g + 1 < SSD_GROUPS:
                order.extend([(f"ssd{la}", 2 * g + 2), (f"ssd{la}", 2 * g + 3)])
            order.append((f"z{la}", g))
        whole((f"gs{la}", 4), (f"ssd_o{la}", 8), (f"out2{la}", 4), (f"mlp1{la}", 16), (f"mlp2{la}", 16))
    return order


ORDER = chunk_order()
N_CHUNKS = len(ORDER)
CHUNKS = {}
for _at, (_name, _j) in enumerate(ORDER):
    CHUNKS.setdefault(_name, []).append(_at)
    assert len(CHUNKS[_name]) == _j + 1


def bank_plan():
    turn, used, plan = 0, [0, 0], {}
    for name, j in ORDER:
        share = 4 if name == "down" or name.startswith("mlp2") else 2 if name.startswith("ssd_o") else 1
        if j % share:
            continue
        pair = 0 if name.startswith(("gates", "ada", "ga")) else turn
        if pair == turn:
            turn = 1 - turn
        plan.setdefault(name, []).append((pair, used[pair]))
        used[pair] += 1
    return plan


GROUPS = bank_plan()

B1_BIAS = 0
B1_QK = B1_BIAS + N_BIAS * 256
B1_V = B1_QK + 21 * 256
B1_GATE = B1_V + 2 * 1152
B1_O = B1_GATE + 24 * 256
B1_TMP = B1_O + 8 * 256
L_Q, L_K, L_V, L_TMP = 0, 4096, 8192, 16384
L_Y, L_MRG, L_SSD = 0, 8192, 12288
ARENA = 27136


def program(nc, xT, stream, params, rows, consts, rel_bias, rev_hot, w_dt, scratch, out):
    ctx = ExitStack()
    with ctx:
        def sb(name, shape):
            return ctx.enter_context(nc.sbuf_tensor(name, shape, F32))

        made = {}

        def sem(name):
            if name not in made:
                made[name] = ctx.enter_context(nc.semaphore(name))
            return made[name]

        ring = sb("ring", [P, SLOTS, KT, CHUNK])
        X = sb("X", [P, KT, TT])
        H = sb("H", [P, KT, TT])
        par = sb("par", [P, N_PARAMS])
        row = sb("row", [P, N_ROWS])
        con = sb("con", [P, N_CONSTS])
        wdt = sb("wdt", [P, DEPTH_2, KT, 64])
        mod = sb("mod", [P, DEPTH_2, 6 * KT, 2])
        small = sb("small", [P, 512])
        work = sb("work", [P, ARENA])
        PB = ctx.enter_context(nc.psum_tensor("PB", [P, 2, 2, 512], F32))
        PA = [ctx.enter_context(nc.psum_tensor(f"PA{i}", [P, 512], F32))[:, :] for i in range(2)]
        PS = ctx.enter_context(nc.psum_tensor("PS", [P, 2, 512], F32))

        def area(at, *shape):
            n = int(np.prod(shape))
            assert at + n <= ARENA, (at, n)
            v = work[:, at:at + n]
            names = "abcd"[:len(shape)]
            if len(shape) == 1:
                return v
            return v.rearrange(f"p ({' '.join(names)}) -> p {' '.join(names)}",
                               **{k: s for k, s in zip(names, shape)})

        def p_(name, i=0, n=1):
            at, _ = PARAMS[name]
            return par[:, at + i:at + i + n]

        def r_(name, i=0, n=None):
            at, m = ROWS[name]
            return row[:, at + i:at + i + (m if n is None else n)]

        def c_(name, i=0, n=None):
            at, m = CONSTS[name]
            return con[:, at + i:at + i + (m if n is None else n)]

        ident = c_("ident")
        ONE, ONE_D, ONE_H, ONE_I = (small[:, 0:1], small[:, 1:2], small[:, 2:3], small[:, 3:4])
        EPS_C = small[:, 4:5]
        LAM = small[:, 8:16]

        def full(col):
            return col.broadcast_to([P, P])

        landed = [sem(f"weights_landed{i}") for i in range(SLOTS)]
        chunk_done = sem("chunk_done")
        evacuated = [sem("evacuated0"), sem("evacuated1")]
        stage_end = sem("stage_end")
        loaded, loaded_late, rows_in, wdt_in = sem("loaded"), sem("loaded_late"), sem("rows_in"), sem("wdt_in")

        LAYER = {
            "mod_sum": 1, "rot_read": 16, "rot": 16, "rot_cos": 16, "w_exp": 64, "w_scores": 32,
            "w_probs": 32, "w_turned": 32, "w_turns": 32, "w_out_read": 32, "w_out": 32, "w_max": 32,
            "sub_sq": 8, "sub_root": 8, "sub_sum": 8, "sub_out": 8, "dt_sum": 1,
            "dt_a": 1, "dt_cs": 1, "dt_abs": 1, "dt_exp": 1, "dt_one": 1, "dt_ln": 1,
            "dt_rest": 2, "dt_wd": 1, "dt_exps": 1, "dt_ready": 1, "s_conv": 32, "s_y": 16, "s_diff": 64, "s_turns": 24,
            "s_cb": 8, "s_turned": 24, "s_xd": 48, "s_delta": 48, "s_state": 48, "s_inter": 48,
            "s_inter_read": 48, "s_cbm": 16, "s_bc": 64, "s_exp": 64, "s_m": 64, "s_xc": 64,
            "s_within": 32, "s_mid": 32, "s_yi": 8, "yt_read": 8, "yt": 16, "z_used": 8,
            "z_sq": 4, "z_root": 1, "z_scaled": 4, "mixed": 8,
        }
        NORMS = ["n1", "n2", "n3", "n4", "m10", "m20", "m11", "m21", "final"]

        def past(tag):
            return {"m10": 0, "m20": 2 * KT, "m11": 4 * KT, "m21": 6 * KT}[tag]

        barriers = {}

        def barrier(eng, who):
            barriers[who] = barriers.get(who, 0) + 1
            eng.drain().then_inc(stage_end, 1)
            eng.wait_ge(stage_end, 4 * barriers[who])

        def repeat(eng, n, body, first=False):
            if first:
                body(0)
            if n == 1:
                body(0)
            else:
                with eng.Fori(1 if first else 0, n) as i:
                    body(i)

        def mod_(la, part, k, c):
            i = part * KT + k
            return mod[:, la, i:i + 1, c:c + 1].rearrange("p a b -> p (a b)")

        def span(base, step, it, size=1):
            if isinstance(it, int):
                return slice((base + step * it) * size, (base + step * it + 1) * size)
            return bass.ds(it * (step * size) + base * size, size)

        def span2(j, step, it):
            if isinstance(it, int):
                return slice(2 * (j + step * it), 2 * (j + step * it) + 2)
            return bass.ds(it * (2 * step) + 2 * j, 2)

        def one(buf, base, step, it):
            if isinstance(it, int):
                return buf[:, base + step * it, :]
            return buf[:, span(base, step, it), :].rearrange("p o n -> p (o n)")

        def take_chunk(pe, c, it, step):
            pe.wait_ge(landed[c % SLOTS], 16 * (c // SLOTS + 1) + 16 * (step // SLOTS) * it)

        def take_banks(pe, group, it, step):
            pair, before = group
            if before:
                pe.wait_ge(evacuated[pair], 2 * before + step * it)

        def pe_features(pe, name, rhs, T, per=4, ready=None):
            c0, n = CHUNKS[name][0], len(CHUNKS[name])
            per = min(per, n)
            loops = n // per if n % per == 0 and per % SLOTS == 0 else 1
            per = n // loops

            def body(it):
                for j in range(per):
                    c, (pair, before) = c0 + j, GROUPS[name][j]
                    take_chunk(pe, c, it, per)
                    take_banks(pe, (pair, before), it, per)
                    for t in range(2):
                        for k in range(KT):
                            if ready and j == 0 and t == 0:
                                ready(k)
                            mm = pe.matmul(PB[:, pair, t, 0:T], ring[:, c % SLOTS, k, t * P:(t + 1) * P],
                                           rhs(k), start=(k == 0), stop=(k == KT - 1))
                    mm.then_inc(chunk_done, 1)
            repeat(pe, loops, body)

        def pe_tokens(pe, name, lhs, n_tok, per=4):
            c0, n = CHUNKS[name][0], len(CHUNKS[name])
            loops = n // per if n % per == 0 else 1
            per = n // loops

            def body(it):
                for j in range(per):
                    c, (pair, before) = c0 + j, GROUPS[name][j]
                    take_chunk(pe, c, it, per)
                    take_banks(pe, (pair, before), it, per)
                    for t in range(n_tok):
                        half = t // (n_tok // 2)
                        col = CHUNK * (t % (n_tok // 2))
                        for k in range(KT):
                            mm = pe.matmul(PB[:, pair, half, col:col + CHUNK], lhs(k, t),
                                           ring[:, c % SLOTS, k, :], start=(k == 0), stop=(k == KT - 1))
                    mm.then_inc(chunk_done, 1)
            repeat(pe, loops, body)

        def pe_deep(pe, name, rhs, T, share):
            c0, n = CHUNKS[name][0], len(CHUNKS[name])
            per = 2 * share
            loops = n // per if per % SLOTS == 0 else 1
            per = n // loops

            def body(it):
                for j in range(per):
                    c, (pair, before), part = c0 + j, GROUPS[name][j // share], j % share
                    take_chunk(pe, c, it, per)
                    if part == 0:
                        take_banks(pe, (pair, before), it, per // share)
                    for t in range(2):
                        for k in range(KT):
                            mm = pe.matmul(PB[:, pair, t, 0:T], ring[:, c % SLOTS, k, t * P:(t + 1) * P],
                                           rhs(KT * part + k), start=(part == 0 and k == 0),
                                           stop=(part == share - 1 and k == KT - 1))
                    mm.then_inc(chunk_done, 1)
            repeat(pe, loops, body)

        def evac(eng, half, name, op, share=1, per=4):
            c0, n = CHUNKS[name][0], len(CHUNKS[name])
            groups = n // share
            per_g = min(per, groups) if share == 1 else 2
            if groups % per_g or (per_g * share) % SLOTS or per_g % 2:
                per_g = groups
            loops = groups // per_g

            def body(it):
                for j in range(per_g):
                    pair, _ = GROUPS[name][j]
                    eng.wait_ge(chunk_done, c0 + share * (j + 1) + per_g * share * it)
                    op(PB[:, pair, half, :], j, it * per_g if loops > 1 else 0).then_inc(evacuated[pair], 1)
            repeat(eng, loops, body)

        def both(eng, name, op, share=1):
            c0, n = CHUNKS[name][0], len(CHUNKS[name])
            groups = n // share
            per_g = min(4, groups) if share == 1 else 2
            loops = groups // per_g

            def body(it):
                for j in range(per_g):
                    pair, _ = GROUPS[name][j]
                    eng.wait_ge(chunk_done, c0 + share * (j + 1) + per_g * share * it)
                    for t in range(2):
                        op(PB[:, pair, t, :], t, j, it * per_g if loops > 1 else 0).then_inc(evacuated[pair], 1)
            repeat(eng, loops, body)

        SQ = area(ARENA - 4096, KT, TT)
        RSTD = sb("rstd", [P, TT])

        def norm_pe(pe, tag, T, ones, n=KT):
            for k in range(n):
                if k % 2 == 0:
                    pe.wait_ge(sem("norm_sq_v"), 4 * NORMS.index(tag) + k // 2 + 1)
                else:
                    pe.wait_ge(sem("norm_sq_a"), 4 * NORMS.index(tag) + k // 2 + 1)
                mm = pe.matmul(PA[0][:, 0:T], full(ones), SQ[:, k, 0:T], start=(k == 0), stop=(k == n - 1))
            mm.then_inc(sem("norm_sum"), 1)

        def norm_act(act, tag, src, T):
            for k in range(1, KT, 2):
                nc.scalar.activation(SQ[:, k, 0:T], src(k), ACT.Square).then_inc(sem("norm_sq_a"), 1)
            act.wait_ge(sem("norm_sum"), NORMS.index(tag) + 1)
            nc.scalar.activation(RSTD[:, 0:T], PA[0][:, 0:T], ACT.Sqrt, bias=EPS_C).then_inc(sem("norm_root"), 1)

        def norm_dve(v, tag, src, T):
            for k in range(0, KT, 2):
                nc.vector.tensor_tensor(SQ[:, k, 0:T], src(k), src(k), ALU.mult).then_inc(sem("norm_sq_v"), 1)
            v.wait_ge(sem("norm_root"), NORMS.index(tag) + 1)
            nc.vector.reciprocal(RSTD[:, 0:T], RSTD[:, 0:T]).then_inc(sem("norm_rstd"), 1)
            v.wait_ge(sem("norm_rstd"), NORMS.index(tag) + 1)

        A_QK = area(B1_QK, 21, T1)
        V1 = area(B1_V, 2, 1152)
        GATE = area(B1_GATE, 24, T1)
        O1 = area(B1_O, 8, T1)
        BIAS = area(B1_BIAS, N_BIAS, 256)
        BIAS_UP = area(B1_GATE, N_BIAS, 256)
        REL = area(B1_O, 32)
        HOT = area(B1_O + 32, N_REV)
        REV = area(B1_O + 512, N_REV)
        HO1 = area(B1_QK, 8, T1)
        HID1 = area(0, 32, T1)
        DN1 = area(B1_GATE, 8, T1)
        UP = area(B1_QK + 4096, 2, 2, 2 * T1)

        U_L = [area(B1_TMP + 768 * i, 768) for i in range(2)]
        U_P = [area(B1_TMP + 1536 + 768 * i, 768) for i in range(2)]
        U_T = area(B1_TMP + 3072, 6, P)
        U_R = area(B1_TMP + 3840, 260)
        U_K = area(B1_TMP + 4104, 256)
        STAT = small[:, 64:96]
        CACT = small[:, 128:384].rearrange("p (k c) -> p k c", c=32)
        NEG_SINK = small[:, 32:40]
        NEG_LAM = small[:, 40:42]
        LAMS = small[:, 48:56]

        LQ, LK, LV = area(L_Q, KT, TT), area(L_K, KT, TT), area(L_V, 4, D)
        MRG = area(L_MRG, KT, TT)
        GA = area(ARENA - 4096, KT, TT)
        AT_P = [area(L_TMP + 1024 * i, 2, TT) for i in range(2)]
        AT_T = [area(L_TMP + 2048 + 512 * i, 4, P) for i in range(2)]
        ADA = [RSTD[:, CHUNK * i:CHUNK * (i + 1)] for i in range(2)]
        ROT_T = [area(L_TMP + 4096 + 256 * i, T1) for i in range(2)]
        SUB_R = [area(L_TMP + 512 * i, TT) for i in range(2)]
        SUB_S = [area(L_TMP + 1024 + 512 * i, TT) for i in range(2)]

        Y = area(L_Y, 4, SSD_INNER)
        at = L_SSD
        CV = [area(at + 2048 * i, 4, TT) for i in range(2)]
        at += 4096
        XG = area(at, 4, 256)
        at += 1024
        BT = area(at, 4, P)
        at += 512
        CBM = area(at, 2, 4, P)
        at += 1024
        MB = [area(at + 1024 * i, 2, 4, P) for i in range(2)]
        at += 2048
        XC = [area(at + 512 * i, 2, 4, HD) for i in range(2)]
        at += 1024
        XD = [area(at + 256 * i, 256) for i in range(2)]
        at += 512
        HT = [area(at + 256 * i, 256) for i in range(2)]
        at += 512
        YI = area(at, 4, 256)
        at += 1024
        YT2 = [area(at + 256 * i, 256) for i in range(2)]
        at += 512
        DT, DTA, CS, ECS, WD, CHD = (area(at + 256 * i, 4, 64) for i in range(6))
        at += 1536
        ZT = area(at, 1024)
        at += 1024
        assert at <= ARENA, at
        YT = area(L_SSD, 16, TT)
        GS = area(L_SSD + 8192, KT, TT)
        MIX = [area(L_SSD + 8192 + 4096 + 512 * i, TT) for i in range(2)]
        HID2 = area(0, 32, TT)
        HID1_PAIRS = area(0, 16, 2 * T1)

        units1 = [("a", h, qt) for h in range(A_HEADS) for qt in range(2)]
        units1 += [("b", h, qt) for h in range(B_HEADS) for qt in range(2)]
        units1 += [("c", h, qt) for h in range(C_HEADS) for qt in range(2)]
        N_AB = 2 * (A_HEADS + B_HEADS)

        def unit1(u):
            br, h, qt = units1[u]
            if br == "a":
                q, k = [2 * g + h // 2 for g in range(3)], [6 + 2 * g + h // 2 for g in range(3)]
                return br, h, qt, q, k, h % 2, h % 2, [(g * A_HEADS + h) * HD for g in range(3)], h // 2
            if br == "b":
                half = h // (B_HEADS // 2)
                return br, h, qt, [12 + h % 4], [16], half, half, [768 + half * HD], 2 + h % 4
            return br, h, qt, [17 + h // 2], [19 + h // 2], h % 2, h % 2, [896 + h * HD], 6 + h // 2

        def yt_bank(i):
            return (PS[:, 0], PS[:, 1], PA[0], PA[1])[i % 4]

        def scores_bank(u):
            return PS if u % 2 == 0 else PB[:, 1]

        def units2(la):
            lat = [(h, qt, 0, TT) for h in range(8) for qt in range(2)]
            own = [(h, 2 + qt, T1, T1) for h in range(8) for qt in range(2)]
            return lat + (own if la == 0 else [])

        F_ORDER, B_ORDER = (2, 3, 0, 1), (3, 2, 1, 0)

        def channels(g, i):
            return (2 * g, 2 * g + 1, 16 + g, 24 + g)[i]

        def inter_count(la, g, i):
            a_group = 6 if la == 0 else 4
            return a_group * g + max(0, 2 * (i + 1) - (0 if la == 0 else 2))

        def live(la, tt):
            return la == 0 or tt < 2

        def ada_index(name, j):
            return ADA_CHUNKS * int(name[3:]) + j

        class Beside:

            def __init__(self):
                self.pending = None

            def finish(self, second):
                if self.pending:
                    second(*self.pending)
                    self.pending = None

        block = ctx.enter_context(nc.Block())

        @block.sync
        def _(sp):
            sp.dma_start(X[:, :, 0:T1], xT[:, :, 0:T1]).then_inc(loaded, 16)
            sp.dma_start(par[:, :], params).then_inc(loaded, 16)
            for c in range(SLOTS):
                sp.dma_start(ring[:, c, :, :], stream[c]).then_inc(landed[c], 16)
            sp.dma_start(con[:, :], consts).then_inc(loaded_late, 16)
            sp.dma_start(X[:, :, T1:TT], xT[:, :, T1:TT]).then_inc(loaded_late, 16)
            with sp.Fori(1, N_CHUNKS // SLOTS) as it:
                for j in range(SLOTS):
                    sp.wait_ge(chunk_done, SLOTS * it + (j + 1 - SLOTS))
                    sp.dma_start(ring[:, j, :, :],
                                 stream[bass.ds(SLOTS * it + j, 1)].rearrange("o p k n -> (o p) k n"))\
                        .then_inc(landed[j], 16)
            for c in range(N_CHUNKS // SLOTS * SLOTS, N_CHUNKS):
                sp.wait_ge(chunk_done, c - SLOTS + 1)
                sp.dma_start(ring[:, c % SLOTS, :, :], stream[c]).then_inc(landed[c % SLOTS], 16)
            sp.wait_ge(sem("final_h"), KT)
            sp.dma_start(out, H[:, :, 0:T1]).then_inc(sem("stored"), 16)
            sp.wait_ge(sem("stored"), 16)

        @block.tensor
        def _(pe):
            def bar():
                barrier(pe, "pe")

            pe.wait_ge(loaded, 16 * 2)
            pe.wait_ge(rows_in, 16)
            pe.wait_ge(sem("consts"), 1)
            pe.wait_ge(sem("hot"), 32)
            pe.matmul(PA[1][0:N_BIAS, 0:N_REV], REL[0:36, 0:N_BIAS], HOT[0:36, :], start=True, stop=True)\
                .then_inc(sem("rev_sum"), 1)

            def x1(k):
                return X[:, k, 0:T1]

            def h1(k):
                return H[:, k, 0:T1]

            def h1_tok(k, t):
                return H[:, k, t * P:(t + 1) * P]

            norm_pe(pe, "n1", T1, ONE_D)
            pe_features(pe, "a_qk", h1, T1, ready=lambda k: pe.wait_ge(sem("n1_h"), k + 1))
            pe_tokens(pe, "a_v", h1_tok, 2)
            pe_features(pe, "b_q", h1, T1)
            c, (pair, before) = CHUNKS["b_kv"][0], GROUPS["b_kv"][0]
            take_chunk(pe, c, 0, 0)
            take_banks(pe, (pair, before), 0, 0)
            for k in range(KT):
                pe.matmul(PB[:, pair, 0, 0:T1], ring[:, c % SLOTS, k, 0:P], h1(k),
                          start=(k == 0), stop=(k == KT - 1))
            for t in range(2):
                for k in range(KT):
                    mm = pe.matmul(PB[:, pair, 1, t * P:(t + 1) * P], h1_tok(k, t),
                                   ring[:, c % SLOTS, k, P:2 * P], start=(k == 0), stop=(k == KT - 1))
            mm.then_inc(chunk_done, 1)
            pe_features(pe, "c_qk", h1, T1)
            pe_tokens(pe, "c_v", h1_tok, 2)
            pe.wait_ge(loaded_late, 16 * 2)
            pe.wait_ge(wdt_in, 16)
            pe.wait_ge(sem("bias_in"), 16)
            for i in range(N_BIAS // 2):
                if i >= 2:
                    pe.wait_ge(sem("flip_read"), i - 1)
                pe.matmul(PS[:, i % 2, :], c_("flip"), BIAS_UP[:, 2 * i:2 * i + 2, :].rearrange("p a b -> p (a b)"),
                          start=True, stop=True).then_inc(sem("flip"), 1)
            bar()

            held = Beside()

            def ada_second(name, j):
                pair, before = GROUPS[name][j]
                pe.wait_ge(evacuated[pair], 2 * before + 1)
                for t in range(2):
                    mm = pe.matmul(PB[:, pair, 1, 2 * t:2 * t + 2], ADA[j % 2][:, t * P:(t + 1) * P], c_("sel"),
                                   start=True, stop=True)
                mm.then_inc(sem("ada_turned"), 1)

            def beside(items, T, t):
                if t == 0:
                    held.finish(ada_second)
                for name, j in items:
                    modulation = name.startswith("ada")
                    if modulation and t == 0:
                        continue
                    c, (pair, before) = CHUNKS[name][j], GROUPS[name][j]
                    if modulation or t == 0:
                        take_chunk(pe, c, 0, 0)
                        take_banks(pe, (pair, before), 0, 0)
                    if modulation:
                        for k in range(KT):
                            q = 32 * (k % 4)
                            mm = pe.matmul(PB[q:q + 32, pair, 0, 0:CHUNK], CACT[:, k, :], ring[:, c % SLOTS, k, :],
                                           start=(k < 4), stop=(k >= 4))
                        held.pending = (name, j)
                    else:
                        for k in range(KT):
                            mm = pe.matmul(PB[:, pair, t, 0:T], ring[:, c % SLOTS, k, t * P:(t + 1) * P],
                                           H[:, k, 0:T], start=(k == 0), stop=(k == KT - 1))
                        if t == 0:
                            continue
                    mm.then_inc(chunk_done, 1)

            def scores1(u):
                br, h, qt, qi, ki, qh, kh, vi, o = unit1(u)
                nk = P * (qt + 1)
                if u >= 2:
                    if u - 2 < N_AB:
                        pe.wait_ge(sem("u_read_v"), u - 1)
                    else:
                        pe.wait_ge(sem("u_read_a"), u - 1 - N_AB)
                S = scores_bank(u)
                for i, (a, b) in enumerate(zip(qi, ki)):
                    r = slice(HD * qh, HD * qh + HD)
                    mm = pe.matmul(S[:, i // 2, (i % 2) * nk:(i % 2) * nk + nk], A_QK[r, a, qt * P:(qt + 1) * P],
                                   A_QK[r, b, 0:nk], start=True, stop=True)
                mm.then_inc(sem("u_scores"), 1)

            def turn1(u):
                br, h, qt, qi, ki, qh, kh, vi, o = unit1(u)
                n = len(qi) * (qt + 1)
                pe.wait_ge(sem("u_probs"), u + 1)
                if u >= 1:
                    pe.wait_ge(sem("u_out_read"), u)
                for i in range(n):
                    mm = pe.transpose(PA[i // 4][:, (i % 4) * P:(i % 4 + 1) * P],
                                      U_P[u % 2][:, i * P:(i + 1) * P], ident)
                mm.then_inc(sem("u_turns"), 1)

            def values1(u):
                br, h, qt, qi, ki, qh, kh, vi, o = unit1(u)
                n = len(qi) * (qt + 1)
                pe.wait_ge(sem("u_turned"), u + 1)
                for i in range(n):
                    col = vi[i // (qt + 1)]
                    mm = pe.matmul(PA[0][HD * qh:HD * qh + HD, 0:P],
                                   V1[:, i % (qt + 1), col:col + HD], U_T[:, i, :],
                                   start=(i == 0), stop=(i == n - 1))
                mm.then_inc(sem("u_out"), 1)

            for u in range(len(units1) + 1):
                if u < len(units1):
                    scores1(u)
                    beside(attention_fill(-1)[u], T1, 0)
                if u >= 1:
                    turn1(u - 1)
                if u < len(units1):
                    beside(attention_fill(-1)[u], T1, 1)
                if u >= 1:
                    values1(u - 1)
            held.finish(ada_second)
            bar()
            bar()

            for j in range(4):
                c, (pair, before) = CHUNKS["branches"][j], GROUPS["branches"][j]
                take_chunk(pe, c, 0, 0)
                take_banks(pe, (pair, before), 0, 0)
                for t in range(2):
                    for i, (k0, k1) in enumerate(((0, 2), (2, 6), (6, 8))):
                        dst = PS[:, pair, t * T1:(t + 1) * T1] if i == 2 \
                            else PB[:, pair, t, i * T1:(i + 1) * T1]
                        for k in range(k0, k1):
                            mm = pe.matmul(dst, ring[:, c % SLOTS, k, t * P:(t + 1) * P], O1[:, k, :],
                                           start=(k == k0), stop=(k == k1 - 1))
                mm.then_inc(chunk_done, 1)
            bar()
            pe_features(pe, "out", lambda k: GATE[:, k, :], T1)
            bar()
            norm_pe(pe, "n2", T1, ONE_D)
            bar()
            norm_pe(pe, "n3", T1, ONE_D)
            pe_features(pe, "up", h1, T1, ready=lambda k: pe.wait_ge(sem("n3_h"), k + 1))
            bar()
            pe_deep(pe, "down", lambda k: HID1[:, k, :], T1, 4)
            bar()
            norm_pe(pe, "n4", T1, ONE_D)
            bar()

            for la in range(DEPTH_2):
                T = TT if la == 0 else T1
                norm_pe(pe, f"m1{la}", TT, ONE_D)

                def hl(k):
                    return H[:, k, 0:T]

                def hall(k):
                    return H[:, k, :]

                pe_features(pe, f"q{la}", hl, T,
                            ready=lambda k: pe.wait_ge(sem("mod_shifted"), past(f"m1{la}") + 2 * (k + 1)))
                pe_features(pe, f"k{la}", hall, TT)
                for j in range(4):
                    c, (pair, before) = CHUNKS[f"v{la}"][j], GROUPS[f"v{la}"][j]
                    take_chunk(pe, c, 0, 0)
                    take_banks(pe, (pair, before), 0, 0)
                    for t in range(4):
                        for k in range(KT):
                            mm = pe.matmul(PB[:, pair, t // 2, CHUNK * (t % 2):CHUNK * (t % 2 + 1)],
                                           H[:, k, t * P:(t + 1) * P], ring[:, c % SLOTS, k, :],
                                           start=(k == 0), stop=(k == KT - 1))
                        if t == 3:
                            mm.then_inc(chunk_done, 1)
                        i = 4 * j + t
                        qk_pair, qk_before = GROUPS[f"q{la}" if i < KT else f"k{la}"][i % KT // 2]
                        pe.wait_ge(evacuated[qk_pair], 2 * qk_before + 2)
                        if i >= 2:
                            pe.wait_ge(sem("rot_read"), LAYER["rot_read"] * la + i - 1)
                        pe.matmul(PS[:, i % 2, 0:T1], c_("rot"), (LQ if i < KT else LK)[:, i % KT, 0:T1],
                                  start=True, stop=True).then_inc(sem("rot"), 1)
                bar()

                us = units2(la)

                def scores2(u):
                    h, qt, k0, nk = us[u]
                    if u >= 2:
                        pe.wait_ge(sem("w_exp"), LAYER["w_exp"] * la + 2 * (u - 1))
                    S = scores_bank(u)
                    for cc in range(2):
                        rows_ = slice(HD * cc, HD * cc + HD)
                        mm = pe.matmul(S[:, cc, 0:nk], LQ[rows_, h, qt * P:(qt + 1) * P],
                                       LK[rows_, h, k0:k0 + nk], start=True, stop=True)
                    mm.then_inc(sem("w_scores"), 1)

                def turn2(u):
                    h, qt, k0, nk = us[u]
                    n = nk // P
                    pe.wait_ge(sem("w_probs"), LAYER["w_probs"] * la + u + 1)
                    if u >= 2:
                        pe.wait_ge(sem("w_out_read"), LAYER["w_out_read"] * la + u - 1)
                    for i in range(n):
                        mm = pe.transpose(PA[u % 2][:, i * P:(i + 1) * P],
                                          AT_P[u % 2][:, 0, i * P:(i + 1) * P], ident)
                    mm.then_inc(sem("w_turns"), 1)

                def values2(u):
                    h, qt, k0, nk = us[u]
                    n = nk // P
                    pe.wait_ge(sem("w_turned"), LAYER["w_turned"] * la + u + 1)
                    for i in range(n):
                        mm = pe.matmul(PA[u % 2][:, 0:P], LV[:, k0 // P + i, h * P:(h + 1) * P],
                                       AT_T[u % 2][:, i, :], start=(i == 0), stop=(i == n - 1))
                    mm.then_inc(sem("w_out"), 1)

                for u in range(len(us) + 2):
                    if u < len(us):
                        scores2(u)
                        beside(attention_fill(la)[u], T, 0)
                    if 1 <= u <= len(us):
                        turn2(u - 1)
                    if u < len(us):
                        beside(attention_fill(la)[u], T, 1)
                    if u >= 2:
                        values2(u - 2)
                held.finish(ada_second)
                bar()
                def project_z(g, tiles):
                    c, (pair, before) = CHUNKS[f"z{la}"][g], GROUPS[f"z{la}"][g]
                    per = T // P // 2
                    for t in tiles:
                        if t == 0:
                            take_chunk(pe, c, 0, 0)
                            take_banks(pe, (pair, before), 0, 0)
                        col = CHUNK * (t % per)
                        for k in range(KT):
                            mm = pe.matmul(PB[:, pair, t // per, col:col + CHUNK], H[:, k, t * P:(t + 1) * P],
                                           ring[:, c % SLOTS, k, :], start=(k == 0), stop=(k == KT - 1))
                        if t == T // P - 1:
                            mm.then_inc(chunk_done, 1)

                def project(g, halves_):
                    if g == SSD_GROUPS:
                        return
                    for n in halves_:
                        i, s_ = n // 2, n % 2
                        j, t = i // 2, i % 2
                        c, (pair, before) = CHUNKS[f"ssd{la}"][2 * g + j], GROUPS[f"ssd{la}"][2 * g + j]
                        if n % 4 == 0:
                            take_chunk(pe, c, 0, 0)
                            take_banks(pe, (pair, before), 0, 0)
                        Tc = T if i == 3 else TT
                        for k in range(4 * s_, 4 * s_ + 4):
                            mm = pe.matmul(PB[:, pair, t, 0:Tc], ring[:, c % SLOTS, k, t * P:(t + 1) * P],
                                           H[:, k, 0:Tc], start=(k == 0), stop=(k == KT - 1))
                        if n % 4 == 3:
                            mm.then_inc(chunk_done, 1)

                def scan_group(g):
                    b = g % 2
                    tok = [t for t in range(4) if live(la, t)]
                    if g >= 1:
                        pe.wait_ge(sem("s_y"), LAYER["s_y"] * la + (2 if la == 0 else 1) * g)
                    for i, bank in enumerate((PA[0], PA[1], PS[:, 0])):
                        if i == 2 and g >= 1:
                            pe.wait_ge(sem("s_diff"), LAYER["s_diff"] * la + 8 * g)
                        pe.wait_ge(sem("s_conv"), LAYER["s_conv"] * la + 4 * g + i + 1)
                        for t in range(4):
                            mm = pe.transpose(bank[:, t * P:(t + 1) * P], CV[b][:, i, t * P:(t + 1) * P], ident)
                        mm.then_inc(sem("s_turns"), 1)
                    pe.wait_ge(sem("s_conv"), LAYER["s_conv"] * la + 4 * g + 4)
                    if g == 0:
                        pe.wait_ge(sem("dt_rest"), LAYER["dt_rest"] * la + 2)
                    for t in tok:
                        mm = pe.matmul(PS[:, 1, t * P:(t + 1) * P], CV[b][:, 2, t * P:(t + 1) * P],
                                       CV[b][:, 3, t * P:(t + 1) * P], start=True, stop=True)
                    mm.then_inc(sem("s_cb"), 1)
                    project(g + 1, (0,))
                    if g + 1 == SSD_GROUPS:
                        project_z(g, (0,))
                    pe.wait_ge(sem("s_turned"), LAYER["s_turned"] * la + 3 * g + 3)
                    for i in range(3):
                        for d, order in enumerate((F_ORDER, B_ORDER)):
                            n = 6 * g + 2 * i + d
                            pe.wait_ge(sem("s_xd"), LAYER["s_xd"] * la + n + 1)
                            pe.matmul(PA[0][:, 256 * d:256 * d + 256], BT[:, order[i], :], XD[d],
                                      start=True, stop=True).then_inc(sem("s_delta"), 1)
                        project(g + 1, ((1,), (2, 3), (4,))[i])
                        if g + 1 == SSD_GROUPS and i + 1 < T // P:
                            project_z(g, (i + 1,))
                        if i and inter_count(la, g, i - 1):
                            pe.wait_ge(sem("s_inter_read"), LAYER["s_inter_read"] * la + inter_count(la, g, i - 1))
                        for d, order in enumerate((F_ORDER, B_ORDER)):
                            n = 6 * g + 2 * i + d
                            pe.wait_ge(sem("s_state"), LAYER["s_state"] * la + n + 1)
                            t = order[i + 1]
                            if live(la, t):
                                pe.matmul(PA[1][:, 256 * d:256 * d + 256], CV[b][:, 3, t * P:(t + 1) * P], HT[d],
                                          start=True, stop=True).then_inc(sem("s_inter"), 1)
                    def decays(r):
                        n = 4 * g + r
                        for d, tri in enumerate((c_("tri_le"), c_("tri_ge"))):
                            if r == 0:
                                pe.wait_ge(sem("s_cbm"), LAYER["s_cbm"] * la + 2 * g + 2)
                            else:
                                pe.wait_ge(sem("s_diff"), LAYER["s_diff"] * la + 2 * (n - 1) + d + 1)
                            for t in tok:
                                hh = 32 * d + 4 * g + r
                                mm = pe.matmul(PS[:, d, t * P:(t + 1) * P], full(DTA[:, t, hh:hh + 1]), tri,
                                               start=True, stop=True)
                            mm.then_inc(sem("s_bc"), 1)

                    def within(r):
                        n = 4 * g + r
                        if r == 0:
                            pe.wait_ge(sem("s_inter_read"), LAYER["s_inter_read"] * la + inter_count(la, g, 2))
                        pe.wait_ge(sem("s_m"), LAYER["s_m"] * la + 2 * n + 2)
                        pe.wait_ge(sem("s_xc"), LAYER["s_xc"] * la + 2 * n + 2)
                        for t in tok:
                            for d in range(2):
                                mm = pe.matmul(PA[t // 2][:, 256 * (t % 2) + HD * r:256 * (t % 2) + HD * r + HD],
                                               MB[r % 2][:, d, t, :], XC[r % 2][:, d, t, :],
                                               start=(d == 0), stop=(d == 1))
                        mm.then_inc(sem("s_within"), 1)

                    decays(0)
                    z_tiles = ((), (), (0,), (1, 2), (3,)) if la == 0 else ((), (), (0,), (), (1,))
                    if g + 1 == SSD_GROUPS:
                        z_tiles = ((),) * 5
                    for r in range(4):
                        project(g + 1, ((5,), (6, 7), (), ())[r])
                        project_z(g, z_tiles[r])
                        if r < 3:
                            decays(r + 1)
                        within(r)
                    project_z(g, z_tiles[4])

                for t in range(4):
                    for k in range(KT):
                        mm = pe.matmul(PS[:, 0, 64 * t:64 * t + 64], H[:, k, t * P:(t + 1) * P],
                                       wdt[:, la, k, :], start=(k == 0), stop=(k == KT - 1))
                mm.then_inc(sem("dt_sum"), 1)
                for h in range(8):
                    pe.wait_ge(sem("sub_sq"), LAYER["sub_sq"] * la + h + 1)
                    if h >= 2:
                        pe.wait_ge(sem("sub_root"), LAYER["sub_root"] * la + h - 1)
                    pe.matmul(PA[h % 2][:, 0:T], full(ONE_H), SUB_S[h % 2][:, 0:T], start=True, stop=True)\
                        .then_inc(sem("sub_sum"), 1)
                    project(0, (h,))
                pe.wait_ge(sem("dt_a"), LAYER["dt_a"] * la + 1)
                for t in range(4):
                    for d, tri in enumerate((c_("tri_le"), c_("tri_ge"))):
                        pe.matmul(PS[:, 1, 64 * t + 32 * d:64 * t + 32 * d + 32], tri,
                                  DTA[:, t, 32 * d:32 * d + 32], start=True, stop=True)
                pe.matmul(PS[:, 1, 256:512], full(ONE), DTA.rearrange("p a b -> p (a b)"),
                          start=True, stop=True).then_inc(sem("dt_cs"), 1)
                pe_features(pe, f"attn_o{la}", lambda k: LQ[:, k, 0:T], T,
                            ready=lambda k: pe.wait_ge(sem("sub_out"), LAYER["sub_out"] * la + k + 1))
                for g in range(SSD_GROUPS):
                    scan_group(g)
                bar()
                for i in range(16):
                    if i % 4 == 0:
                        c, (pair, before) = CHUNKS[f"gs{la}"][i // 4], GROUPS[f"gs{la}"][i // 4]
                        take_chunk(pe, c, 0, 0)
                        take_banks(pe, (pair, before), 0, 0)
                        for t in range(2):
                            for k in range(KT):
                                mm = pe.matmul(PB[:, pair, t, 0:T], ring[:, c % SLOTS, k, t * P:(t + 1) * P],
                                               H[:, k, 0:T], start=(k == 0), stop=(k == KT - 1))
                        mm.then_inc(chunk_done, 1)
                    if i == 0:
                        pe.wait_ge(sem("z_scaled"), LAYER["z_scaled"] * la + T // P)
                    if i >= 4:
                        pe.wait_ge(sem(f"yt_read{i % 2}"), LAYER["yt_read"] * la + (i - 4) // 2 + 1)
                    for t in range(T // P):
                        mm = pe.transpose(yt_bank(i)[:, t * P:(t + 1) * P], Y[:, t, i * P:(i + 1) * P], ident)
                    mm.then_inc(sem("yt"), 1)
                for i in range(2):
                    pe.wait_ge(sem(f"yt_read{i}"), LAYER["yt_read"] * la + 8)
                pe_deep(pe, f"ssd_o{la}", lambda k: YT[:, k, 0:T], T, 2)
                pe_features(pe, f"out2{la}", lambda k: MRG[:, k, 0:T], T,
                            ready=lambda k: pe.wait_ge(sem("mixed"), LAYER["mixed"] * la + k + 1))
                bar()
                norm_pe(pe, f"m2{la}", T, ONE_D)
                pe_features(pe, f"mlp1{la}", hl, T,
                            ready=lambda k: pe.wait_ge(sem("mod_shifted"), past(f"m2{la}") + (k + 1) * (T // T1)))
                bar()
                pe_deep(pe, f"mlp2{la}", lambda k: HID2[:, k, 0:T], T, 4)
                bar()
            norm_pe(pe, "final", T1, ONE_D)

        @block.scalar
        def _(act):
            def bar():
                barrier(act, "act")

            copy = nc.scalar.activation

            act.wait_ge(loaded, 16 * 2)
            act.wait_ge(rows_in, 16)
            act.wait_ge(sem("consts"), 1)
            copy(CACT[:, :, 0:2], p_("cvec", 0, 16).rearrange("p (c k) -> p k c", c=2), ACT.Silu).then_inc(sem("cact"), 1)
            act.wait_ge(sem("lam_dot"), 4)
            copy(LAMS[:, 0:4], LAMS[:, 0:4], ACT.Exp).then_inc(sem("lam_exp"), 1)
            for la in range(DEPTH_2):
                copy(r_(f"a_log{la}"), r_(f"a_log{la}"), ACT.Exp).then_inc(sem("a_exp"), 1)

            def x1(k):
                return X[:, k, 0:T1]

            norm_act(act, "n1", x1, T1)

            def qk_out(base, scaled):
                def op(bank, j, it):
                    return copy(A_QK[:, base + 2 * j + 1, :], bank[:, 0:T1], ACT.Copy,
                                scale=SCALE if j < scaled else 1.0)
                return op

            evac(act, 1, "a_qk", qk_out(0, 3))
            evac(act, 1, "a_v", lambda bank, j, it: copy(V1[:, 1, CHUNK * j:CHUNK * (j + 1)], bank[:, 0:CHUNK], ACT.Copy))
            evac(act, 1, "b_q", qk_out(12, 2))
            evac(act, 1, "b_kv", lambda bank, j, it: copy(V1[:, :, 768:896],
                                                          bank[:, 0:256].rearrange("p (t n) -> p t n", t=2), ACT.Copy))
            evac(act, 1, "c_qk", qk_out(17, 1))
            evac(act, 1, "c_v", lambda bank, j, it: copy(V1[:, 1, 896:1152], bank[:, 0:CHUNK], ACT.Copy))

            def gate_out(bank, j, it):
                return copy(one(GATE, 2 * j + 1, 2, it), bank[:, 0:T1], ACT.Identity,
                            bias=par[:, span(PARAMS["b_gate"][0] + 2 * j + 1, 2, it)])

            bar()
            held = Beside()

            def ada_second(name, j):
                pair, before = GROUPS[name][j]
                act.wait_ge(sem("ada_turned"), ada_index(name, j) + 1)
                copy(mod[:, int(name[3:]), 2 * j:2 * j + 2, :], PB[:, pair, 1, 0:4].rearrange("p (n c) -> p n c", c=2),
                     ACT.Copy).then_inc(evacuated[pair], 1)

            def beside(items, op):
                for name, j in items:
                    if name.startswith("ada"):
                        held.pending = (name, j)
                        continue
                    pair, before = GROUPS[name][j]
                    act.wait_ge(chunk_done, CHUNKS[name][j] + 1)
                    op(PB[:, pair, 1, :], j, 0).then_inc(evacuated[pair], 1)

            def softmax1(u):
                br, h, qt, qi, ki, qh, kh, vi, o = unit1(u)
                nk = P * (qt + 1)
                n = len(qi) * nk
                b = u % 2
                if u >= 2:
                    act.wait_ge(sem("u_turns"), u - 1)
                if br == "c":
                    act.wait_ge(sem("u_scores"), u + 1)
                    if u > N_AB:
                        act.wait_ge(sem("u_probs"), u)
                    z = scores_bank(u)[:, 0, 0:nk]
                    copy(U_K[:, 0:nk], z, ACT.Sigmoid, scale=-1.0).then_inc(sem("u_keep"), 1)
                    copy(U_P[b][:, 0:nk], z, ACT.Sigmoid).then_inc(sem("u_read_a"), 1)
                    return
                act.wait_ge(sem("u_max"), u + 1)
                if br == "b":
                    copy(STAT[:, 8 + b:9 + b], STAT[:, b:b + 1], ACT.Exp, bias=r_("sinks", h, 1))\
                        .then_inc(sem("u_sink"), 1)
                copy(U_P[b][:, 0:n], U_L[b][:, 0:n], ACT.Exp, bias=STAT[:, b:b + 1],
                     accum_out=STAT[:, 4 + b:5 + b]).then_inc(sem("u_exp"), 1)

            def out1(u):
                br, h, qt, qi, ki, qh, kh, vi, o = unit1(u)
                act.wait_ge(sem("u_out"), u + 1)
                rows_ = slice(HD * qh, HD * qh + HD)
                copy(O1[rows_, o, qt * P:(qt + 1) * P], PA[0][rows_, 0:P], ACT.Copy)\
                    .then_inc(sem("u_out_read"), 1)

            for u in range(len(units1) + 1):
                held.finish(ada_second)
                if u < len(units1):
                    softmax1(u)
                    beside(attention_fill(-1)[u], gate_out)
                if u >= 1:
                    out1(u - 1)
            held.finish(ada_second)
            bar()
            copy(GATE, GATE, ACT.Sigmoid)
            bar()
            bar()
            evac(act, 1, "out", lambda bank, j, it: copy(HO1[:, 2 * j + 1, :], bank[:, 0:T1], ACT.Copy))
            bar()
            norm_act(act, "n2", lambda k: HO1[:, k, :], T1)
            bar()
            norm_act(act, "n3", x1, T1)

            c0 = CHUNKS["up"][0]
            W2, CB = PARAMS["conv_w"][0] + 2 * 64, PARAMS["conv_b"][0]

            def up(it):
                for i in range(2):
                    for v in range(2):
                        j = 2 * i + v
                        pair, before = GROUPS["up"][j]
                        act.wait_ge(chunk_done, c0 + j + 1 + 4 * it)
                        if not isinstance(it, int) and v == 0:
                            act.wait_ge(sem("up_prod"), 2 * it + (i - 1))
                        for t in range(2):
                            tile = 32 * v + 2 * i + t
                            ins = copy(UP[:, i, v, t * T1:(t + 1) * T1], PB[:, pair, t, 0:T1], ACT.Identity,
                                       scale=par[:, span(W2 + tile, 4, it)], bias=par[:, span(CB + tile, 4, it)])
                        ins.then_inc(sem("up_mid"), 1)
                        if v == 0:
                            act.wait_ge(evacuated[pair], 2 * before + 2 + 4 * it)
                            copy(UP[:, i, 0, :], UP[:, i, 0, :], ACT.Gelu_apprx_tanh).then_inc(sem("up_gelu"), 1)
            act.wait_ge(sem("n3_h"), KT)
            repeat(act, 8, up, True)
            bar()
            evac(act, 1, "down", lambda bank, j, it: copy(one(DN1, 2 * j + 1, 2, it), bank[:, 0:T1], ACT.Copy),
                 share=4)
            bar()
            norm_act(act, "n4", lambda k: DN1[:, k, :], T1)
            bar()

            for la in range(DEPTH_2):
                T = TT if la == 0 else T1
                halves = T // T1
                norm_act(act, f"m1{la}", lambda k: X[:, k, :], TT)

                def shift(tag, part, n_half):
                    for k in range(KT):
                        for s in range(n_half):
                            act.wait_ge(sem("mod_scaled"), past(tag) + n_half * k + s + 1)
                            cols = slice(s * T1, (s + 1) * T1)
                            copy(H[:, k, cols], H[:, k, cols], ACT.Identity, bias=mod_(la, part, k, s))\
                                .then_inc(sem("mod_shifted"), 1)

                shift(f"m1{la}", 0, 2)
                evac(act, 1, f"q{la}", lambda bank, j, it: copy(LQ[:, 2 * j + 1, 0:T], bank[:, 0:T], ACT.Copy, scale=SCALE))
                evac(act, 1, f"k{la}", lambda bank, j, it: copy(LK[:, 2 * j + 1, :], bank[:, 0:TT], ACT.Copy))
                evac(act, 1, f"v{la}", lambda bank, j, it: copy(
                    LV[:, 2:4, CHUNK * j:CHUNK * (j + 1)], bank.rearrange("p (t n) -> p t n", t=2), ACT.Copy))
                bar()
                us = units2(la)

                def ga_out(bank, j, it):
                    return copy(GA[:, 2 * j + 1, 0:T], bank[:, 0:T], ACT.Copy)

                def exps2(u):
                    h, qt, k0, nk = us[u]
                    b = u % 2
                    act.wait_ge(sem("w_max"), LAYER["w_max"] * la + u + 1)
                    if u >= 2:
                        act.wait_ge(sem("w_turns"), LAYER["w_turns"] * la + u - 1)
                    for cc in range(2):
                        copy(AT_P[b][:, cc, 0:nk], scores_bank(u)[:, cc, 0:nk], ACT.Exp,
                             bias=STAT[:, 2 * b + cc:2 * b + cc + 1],
                             accum_out=STAT[:, 4 + 2 * b + cc:5 + 2 * b + cc]).then_inc(sem("w_exp"), 1)

                def out2(u):
                    h, qt, k0, nk = us[u]
                    act.wait_ge(sem("w_out"), LAYER["w_out"] * la + u + 1)
                    copy(LQ[:, h, qt * P:(qt + 1) * P], PA[u % 2][:, 0:P], ACT.Copy)\
                        .then_inc(sem("w_out_read"), 1)

                for u in range(len(us) + 2):
                    held.finish(ada_second)
                    if u < len(us):
                        exps2(u)
                        beside(attention_fill(la)[u], ga_out)
                    if u >= 2:
                        out2(u - 2)
                held.finish(ada_second)
                bar()
                copy(MRG[:, :, 0:T], GA[:, :, 0:T], ACT.Sigmoid).then_inc(sem("gate_open"), 1)
                E1 = XD[0].rearrange("p (a b) -> p a b", a=4)
                E2 = XD[1].rearrange("p (a b) -> p a b", a=4)
                act.wait_ge(sem("dt_abs"), LAYER["dt_abs"] * la + 1)
                copy(E1, E1, ACT.Exp, scale=-1.0).then_inc(sem("dt_exp"), 1)
                act.wait_ge(sem("dt_one"), LAYER["dt_one"] * la + 1)
                copy(WD, E2, ACT.Ln).then_inc(sem("dt_ln"), 1)
                W0, CBs = PARAMS[f"sconv_w{la}"][0], PARAMS[f"sconv_b{la}"][0]

                def middle(g, chunks):
                    b = g % 2
                    for j in chunks if g < SSD_GROUPS else ():
                        pair, _ = GROUPS[f"ssd{la}"][2 * g + j]
                        act.wait_ge(chunk_done, CHUNKS[f"ssd{la}"][2 * g + j] + 1)
                        if g >= 2 and j == 0:
                            act.wait_ge(sem("s_within"), LAYER["s_within"] * la + 4 * (g - 1))
                        for t in range(2):
                            i = 2 * j + t
                            Tc = T if i == 3 else TT
                            ch = channels(g, i)
                            copy(CV[b][:, i, 0:Tc], PB[:, pair, t, 0:Tc], ACT.Identity,
                                 scale=par[:, W0 + 2 * 32 + ch:W0 + 2 * 32 + ch + 1],
                                 bias=par[:, CBs + ch:CBs + ch + 1]).then_inc(sem("s_mid"), 1)

                def silus(g):
                    b = g % 2
                    for i in range(4):
                        Tc = T if i == 3 else TT
                        pair, before = GROUPS[f"ssd{la}"][2 * g + i // 2]
                        act.wait_ge(evacuated[pair], 2 * before + i % 2 + 1)
                        copy(CV[b][:, i, 0:Tc], CV[b][:, i, 0:Tc], ACT.Silu).then_inc(sem("s_conv"), 1)

                def turned(g):
                    for i, bank in enumerate((PA[0], PA[1], PS[:, 0])):
                        act.wait_ge(sem("s_turns"), LAYER["s_turns"] * la + 3 * g + i + 1)
                        src = bank.rearrange("p (t n) -> p t n", t=4)
                        if i == 0 and g >= 1:
                            act.wait_ge(sem("s_y"), LAYER["s_y"] * la + (2 if la == 0 else 1) * g)
                            act.wait_ge(sem("s_yi"), LAYER["s_yi"] * la + g)
                            act.wait_ge(sem("s_xc"), LAYER["s_xc"] * la + 8 * g)
                        dst = BT[:, :, :] if i == 2 else XG[:, :, i * P:(i + 1) * P]
                        copy(dst, src, ACT.Copy).then_inc(sem("s_turned"), 1)

                def decay_exps(g, heads):
                    tok = slice(0, 4 if la == 0 else 2)
                    for r in heads:
                        for d in range(2):
                            n = 2 * (4 * g + r) + d
                            act.wait_ge(sem("s_diff"), LAYER["s_diff"] * la + n + 1)
                            copy(MB[r % 2][:, d, tok, :], MB[r % 2][:, d, tok, :], ACT.Exp)\
                                .then_inc(sem("s_exp"), 1)

                def silu_z(g):
                    pair, _ = GROUPS[f"z{la}"][g]
                    act.wait_ge(chunk_done, CHUNKS[f"z{la}"][g] + 1)
                    if g >= 1:
                        act.wait_ge(sem("z_used"), LAYER["z_used"] * la + g)
                    w = CHUNK * (T // P) // 2
                    for i in range(2):
                        copy(ZT[:, i * w:(i + 1) * w], PB[:, pair, i, 0:w], ACT.Silu).then_inc(evacuated[pair], 1)

                for h in range(8):
                    act.wait_ge(sem("sub_sum"), LAYER["sub_sum"] * la + h + 1)
                    if h >= 2:
                        act.wait_ge(sem("sub_out"), LAYER["sub_out"] * la + h - 1)
                    copy(SUB_R[h % 2][:, 0:T], PA[h % 2][:, 0:T], ACT.Sqrt, bias=EPS_C)\
                        .then_inc(sem("sub_root"), 1)
                    if h == 4:
                        middle(0, (0,))
                middle(0, (1,))
                silus(0)
                act.wait_ge(sem("dt_rest"), LAYER["dt_rest"] * la + 2)
                copy(ECS, CS, ACT.Exp)
                copy(WD, WD, ACT.Exp).then_inc(sem("dt_wd"), 1)
                copy(CHD, CHD, ACT.Exp).then_inc(sem("dt_exps"), 1)
                for g in range(SSD_GROUPS):
                    turned(g)
                    middle(g + 1, (0,))
                    decay_exps(g, (0, 1))
                    middle(g + 1, (1,))
                    decay_exps(g, (2, 3))
                    if g + 1 < SSD_GROUPS:
                        silus(g + 1)
                    silu_z(g)
                bar()
                for t in range(T // P):
                    copy(YT[:, 0:4, :], Y[:, t, :].rearrange("p (a b) -> p a b", a=4), ACT.Square,
                         accum_out=STAT[:, t:t + 1]).then_inc(sem("z_sq"), 1)
                    act.wait_ge(sem("z_sq"), LAYER["z_sq"] * la + t + 1)
                copy(STAT[:, 4:4 + T // P], STAT[:, 0:T // P], ACT.Sqrt, scale=1.0 / SSD_INNER, bias=EPS_C)\
                    .then_inc(sem("z_root"), 1)
                for j in range(4):
                    pair, _ = GROUPS[f"gs{la}"][j]
                    act.wait_ge(chunk_done, CHUNKS[f"gs{la}"][j] + 1)
                    for t in range(2):
                        copy(GS[:, 2 * j + t, 0:T], PB[:, pair, t, 0:T], ACT.Sigmoid).then_inc(evacuated[pair], 1)
                    for i in (4 * j + 1, 4 * j + 3):
                        act.wait_ge(sem("yt"), LAYER["yt"] * la + i + 1)
                        copy(YT[:, i, 0:T], yt_bank(i)[:, 0:T], ACT.Identity, scale=p_(f"ssd_g{la}", i))\
                            .then_inc(sem("yt_read1"), 1)
                bar()
                norm_act(act, f"m2{la}", lambda k: X[:, k, 0:T], T)
                shift(f"m2{la}", 3, halves)
                evac(act, 1, f"mlp1{la}", lambda bank, j, it: copy(one(HID2, 2 * j + 1, 2, it)[:, 0:T],
                                                                  bank[:, 0:T], ACT.Relu))
                bar()
                bar()
            norm_act(act, "final", x1, T1)

        @block.vector
        def _(v):
            def bar():
                barrier(v, "dve")

            vec = nc.vector
            steps = [0]

            def then(ins):
                steps[0] += 1
                ins.then_inc(sem("dve_step"), 1)
                v.wait_ge(sem("dve_step"), steps[0])

            for col, value in ((ONE, 1.0), (ONE_D, 1.0 / D), (ONE_H, 1.0 / P), (EPS_C, EPS), (CACT, 0.0)):
                ins = vec.memset(col, value)
            ins.then_inc(sem("consts"), 1)
            v.wait_ge(loaded, 16 * 2)
            v.wait_ge(rows_in, 16)
            vec.tensor_scalar(NEG_SINK, r_("sinks"), -1.0, None, ALU.mult)
            for la in range(DEPTH_2):
                then(vec.tensor_tensor(r_(f"lam_q{la}"), r_(f"lam_q{la}"), r_(f"lam_k{la}"), ALU.mult))
                for i in range(2):
                    vec.reduce_sum(LAMS[:, 2 * la + i:2 * la + i + 1], r_(f"lam_q{la}", HD * i, HD), AX.X)\
                        .then_inc(sem("lam_dot"), 1)
                lam_init = 0.8 - 0.6 * math.exp(-0.3 * la)
                vec.tensor_scalar(p_(f"subln_g{la}"), p_(f"subln_g{la}"), 1.0 - lam_init, None, ALU.mult)
            v.wait_ge(sem("lam_exp"), 1)
            v.wait_ge(sem("a_exp"), DEPTH_2)
            for la in range(DEPTH_2):
                lam_init = 0.8 - 0.6 * math.exp(-0.3 * la)
                then(vec.tensor_tensor(NEG_LAM[:, la:la + 1], LAMS[:, 2 * la + 1:2 * la + 2],
                                       LAMS[:, 2 * la:2 * la + 1], ALU.subtract))
                vec.tensor_scalar(NEG_LAM[:, la:la + 1], NEG_LAM[:, la:la + 1], -lam_init, None, ALU.add)
                vec.tensor_scalar(r_(f"a_log{la}"), r_(f"a_log{la}"), -1.0, None, ALU.mult)
            v.wait_ge(sem("rev_sum"), 1)
            vec.tensor_copy(REV[0:N_BIAS, :], PA[1][0:N_BIAS, 0:N_REV]).then_inc(sem("rev"), 1)

            def x1(k):
                return X[:, k, 0:T1]

            def norm_scale(tag, src, dst, g, T, name):
                norm_dve(v, tag, src, T)
                for k in range(KT):
                    vec.scalar_tensor_tensor(dst(k), src(k), g(k), RSTD[:, 0:T], ALU.mult, ALU.mult)\
                        .then_inc(sem(f"{tag}_{name}"), 1)

            norm_scale("n1", x1, lambda k: H[:, k, 0:T1], lambda k: p_("pre_g", k), T1, "h")

            def qk_out(base, scaled):
                def op(bank, j, it):
                    return vec.tensor_scalar(A_QK[:, base + 2 * j, :], bank[:, 0:T1],
                                             SCALE if j < scaled else 1.0, None, ALU.mult)
                return op

            evac(v, 0, "a_qk", qk_out(0, 3))
            evac(v, 0, "a_v", lambda bank, j, it: vec.tensor_copy(V1[:, 0, CHUNK * j:CHUNK * (j + 1)], bank[:, 0:CHUNK]))
            evac(v, 0, "b_q", qk_out(12, 2))
            evac(v, 0, "b_kv", lambda bank, j, it: vec.tensor_copy(A_QK[:, 16, :], bank[:, 0:T1]))
            evac(v, 0, "c_qk", qk_out(17, 1))
            evac(v, 0, "c_v", lambda bank, j, it: vec.tensor_copy(V1[:, 0, 896:1152], bank[:, 0:CHUNK]))

            def gate_out(bank, j, it):
                return vec.tensor_scalar(one(GATE, 2 * j, 2, it), bank[:, 0:T1],
                                         par[:, span(PARAMS["b_gate"][0] + 2 * j, 2, it)], None, ALU.add)

            for i in range(N_BIAS // 2):
                v.wait_ge(sem("flip"), i + 1)
                vec.tensor_copy(BIAS[:, 2 * i:2 * i + 2, :], PS[:, i % 2, :].rearrange("p (a b) -> p a b", a=2))\
                    .then_inc(sem("flip_read"), 1)
            bar()

            def beside(items, op):
                for name, j in items:
                    pair, before = GROUPS[name][j]
                    v.wait_ge(chunk_done, CHUNKS[name][j] + 1)
                    if name.startswith("ada"):
                        if ada_index(name, j) >= 2:
                            v.wait_ge(sem("ada_turned"), ada_index(name, j) - 1)
                        vec.tensor_copy(ADA[j % 2], PB[:, pair, 0, 0:CHUNK]).then_inc(evacuated[pair], 1)
                    else:
                        op(PB[:, pair, 0, :], j, 0).then_inc(evacuated[pair], 1)

            def rows1(u):
                br, h, qt, qi, ki, qh, kh, vi, o = unit1(u)
                nk = P * (qt + 1)
                off = 0 if qt == 1 else P
                b = u % 2
                if br == "c":
                    return
                S = scores_bank(u)
                v.wait_ge(sem("u_scores"), u + 1)
                L = U_L[b]
                if u >= 2:
                    v.wait_ge(sem("u_exp"), u - 1)
                if br == "a":
                    L2 = L[:, 0:2 * nk].rearrange("p (g n) -> p g n", g=2)
                    vec.tensor_tensor(L2, S[:, 0, 0:2 * nk].rearrange("p (g n) -> p g n", g=2),
                                      BIAS[:, h:h + 5:4, off:off + nk], ALU.add)
                    ins = vec.tensor_tensor(L[:, 2 * nk:3 * nk], S[:, 1, 0:nk], BIAS[:, 8 + h, off:off + nk], ALU.add)
                    n = 3 * nk
                else:
                    ins = vec.tensor_tensor(L[:, 0:nk], S[:, 0, 0:nk], BIAS[:, 12 + h, off:off + nk], ALU.add)
                    n = nk
                ins.then_inc(sem("u_read_v"), 1)
                v.wait_ge(sem("u_read_v"), u + 1)
                if br == "b":
                    then(vec.tensor_reduce(STAT[:, b:b + 1], L[:, 0:n], AX.X, ALU.max, negate=True))
                    vec.tensor_tensor(STAT[:, b:b + 1], STAT[:, b:b + 1], NEG_SINK[:, h:h + 1], ALU.min)\
                        .then_inc(sem("u_max"), 1)
                else:
                    vec.tensor_reduce(STAT[:, b:b + 1], L[:, 0:n], AX.X, ALU.max, negate=True)\
                        .then_inc(sem("u_max"), 1)

            def probs1(u):
                br, h, qt, qi, ki, qh, kh, vi, o = unit1(u)
                nk = P * (qt + 1)
                n = len(qi) * nk
                b = u % 2
                if br == "c":
                    v.wait_ge(sem("u_keep"), u - N_AB + 1)
                    off = 0 if qt == 1 else P
                    then(vec.tensor_tensor(U_K[:, 0:nk], U_K[:, 0:nk], c_("c_after", off, nk), ALU.max))
                    vec.memset(U_R[:, nk:nk + 1], 1.0)
                    then(vec.tensor_tensor_scan(U_R[:, 0:nk][:, ::-1], U_K[:, 0:nk][:, ::-1], U_K[:, 0:nk][:, ::-1],
                                                1.0, ALU.mult, ALU.bypass))
                    v.wait_ge(sem("u_read_a"), u - N_AB + 1)
                    then(vec.tensor_tensor(U_P[b][:, 0:nk], U_P[b][:, 0:nk], c_("c_before", off, nk), ALU.mult))
                    vec.tensor_tensor(U_P[b][:, 0:nk], U_P[b][:, 0:nk], U_R[:, 1:nk + 1], ALU.mult)\
                        .then_inc(sem("u_probs"), 1)
                else:
                    v.wait_ge(sem("u_exp"), u + 1)
                    if br == "b":
                        v.wait_ge(sem("u_sink"), u - 2 * A_HEADS + 1)
                        then(vec.tensor_tensor(STAT[:, 4 + b:5 + b], STAT[:, 4 + b:5 + b],
                                               STAT[:, 8 + b:9 + b], ALU.add))
                    then(vec.reciprocal(STAT[:, 12 + b:13 + b], STAT[:, 4 + b:5 + b]))
                    vec.tensor_scalar(U_P[b][:, 0:n], U_P[b][:, 0:n], STAT[:, 12 + b:13 + b], None, ALU.mult)\
                        .then_inc(sem("u_probs"), 1)

            def turned1(u):
                n = len(unit1(u)[3]) * P * (unit1(u)[2] + 1)
                nb = n // P
                v.wait_ge(sem("u_turns"), u + 1)
                if u >= 1:
                    v.wait_ge(sem("u_out"), u)
                if nb > 4:
                    vec.tensor_copy(U_T[:, 0:4, :], PA[0].rearrange("p (a b) -> p a b", a=4))
                    vec.tensor_copy(U_T[:, 4:6, :], PA[1][:, 0:256].rearrange("p (a b) -> p a b", a=2))\
                        .then_inc(sem("u_turned"), 1)
                else:
                    vec.tensor_copy(U_T[:, 0:nb, :], PA[0][:, 0:n].rearrange("p (a b) -> p a b", a=nb))\
                        .then_inc(sem("u_turned"), 1)

            for u in range(len(units1) + 1):
                if u >= 1:
                    probs1(u - 1)
                if u < len(units1):
                    rows1(u)
                if u >= 1:
                    turned1(u - 1)
                if u < len(units1):
                    beside(attention_fill(-1)[u], gate_out)
            bar()
            bar()
            for j in range(4):
                pair, _ = GROUPS["branches"][j]
                v.wait_ge(chunk_done, CHUNKS["branches"][j] + 1)
                for t in range(2):
                    k = 2 * j + t
                    vec.tensor_tensor(GATE[:, 16 + k, :], PS[:, pair, t * T1:(t + 1) * T1], GATE[:, 16 + k, :], ALU.mult)
                    vec.tensor_tensor(GATE[:, k, :], PB[:, pair, t, 0:T1], GATE[:, k, :], ALU.mult)
                    vec.tensor_tensor(GATE[:, 8 + k, :], PB[:, pair, t, T1:2 * T1], GATE[:, 8 + k, :], ALU.mult)\
                        .then_inc(evacuated[pair], 1)
            bar()
            evac(v, 0, "out", lambda bank, j, it: vec.tensor_copy(HO1[:, 2 * j, :], bank[:, 0:T1]))
            bar()

            def residual1(tag, src, g):
                norm_dve(v, tag, src, T1)
                for k in range(KT):
                    vec.scalar_tensor_tensor(src(k), src(k), p_(g, k), RSTD[:, 0:T1], ALU.mult, ALU.mult)\
                        .then_inc(sem(f"{tag}_part"), 1)
                for k in range(KT):
                    v.wait_ge(sem(f"{tag}_part"), k + 1)
                    vec.tensor_tensor(x1(k), x1(k), src(k), ALU.add)

            residual1("n2", lambda k: HO1[:, k, :], "post_g")
            bar()
            norm_scale("n3", x1, lambda k: H[:, k, 0:T1], lambda k: p_("ffn_pre_g", k), T1, "h")
            c0 = CHUNKS["up"][0]
            W0 = PARAMS["conv_w"][0]

            def up(it):
                for i in range(2):
                    for vv in range(2):
                        j = 2 * i + vv
                        pair, _ = GROUPS["up"][j]
                        v.wait_ge(sem("up_mid"), j + 1 + 4 * it)
                        for tap in (1, 0):
                            lag = 2 - tap
                            if tap == 0:
                                v.wait_ge(sem("up_tap"), j + 1 + 4 * it)
                            for t in range(2):
                                tile = 32 * vv + 2 * i + t
                                dst = UP[:, i, vv, t * T1 + lag:(t + 1) * T1]
                                ins = vec.scalar_tensor_tensor(
                                    dst, PB[:, pair, t, 0:T1 - lag], par[:, span(W0 + 64 * tap + tile, 4, it)],
                                    dst, ALU.mult, ALU.add)
                                if tap == 0:
                                    ins.then_inc(evacuated[pair], 1)
                            if tap == 1:
                                ins.then_inc(sem("up_tap"), 1)
            repeat(v, 8, up, True)
            bar()
            evac(v, 0, "down", lambda bank, j, it: vec.tensor_copy(one(DN1, 2 * j, 2, it), bank[:, 0:T1]), share=4)
            bar()
            residual1("n4", lambda k: DN1[:, k, :], "ffn_post_g")
            bar()

            for la in range(DEPTH_2):
                T = TT if la == 0 else T1
                halves = T // T1
                tok = slice(0, T // P)
                M = mod[:, la]
                then(vec.tensor_tensor(M, M,
                                       p_(f"ada_b{la}", 0, 48).unsqueeze(2).broadcast_to([P, 48, 2]), ALU.add))
                for part, g in ((1, f"mix_g{la}"), (4, f"mlp_g{la}")):
                    m = mod[:, la, part * KT:(part + 1) * KT, :]
                    then(vec.scalar_tensor_tensor(m, m, 1.0, p_(g, 0, KT).unsqueeze(2).broadcast_to([P, KT, 2]),
                                                  ALU.add, ALU.mult))

                def norm_mod(tag, part, n_half):
                    norm_dve(v, tag, lambda k: X[:, k, 0:n_half * T1], n_half * T1)
                    for k in range(KT):
                        for s_ in range(n_half):
                            cols = slice(s_ * T1, (s_ + 1) * T1)
                            vec.scalar_tensor_tensor(H[:, k, cols], X[:, k, cols], mod_(la, part, k, s_),
                                                     RSTD[:, cols], ALU.mult, ALU.mult)\
                                .then_inc(sem("mod_scaled"), 1)

                norm_mod(f"m1{la}", 1, 2)
                evac(v, 0, f"q{la}", lambda bank, j, it: vec.tensor_scalar(LQ[:, 2 * j, 0:T], bank[:, 0:T],
                                                                          SCALE, None, ALU.mult))
                evac(v, 0, f"k{la}", lambda bank, j, it: vec.tensor_copy(LK[:, 2 * j, :], bank[:, 0:TT]))
                for i in range(2 * KT):
                    v.wait_ge(sem("rot"), LAYER["rot"] * la + i + 1)
                    vec.tensor_tensor(ROT_T[i % 2], PS[:, i % 2, 0:T1], c_("sin"), ALU.mult)\
                        .then_inc(sem("rot_read"), 1)
                    v.wait_ge(sem("rot_read"), LAYER["rot_read"] * la + i + 1)
                    v.wait_ge(sem("rot_cos"), LAYER["rot_cos"] * la + i + 1)
                    x = (LQ if i < KT else LK)[:, i % KT, 0:T1]
                    vec.tensor_tensor(x, x, ROT_T[i % 2], ALU.add)
                    if i % 4 == 2:
                        j = i // 4
                        pair, _ = GROUPS[f"v{la}"][j]
                        v.wait_ge(chunk_done, CHUNKS[f"v{la}"][j] + 1)
                        vec.tensor_copy(LV[:, 0:2, CHUNK * j:CHUNK * (j + 1)],
                                        PB[:, pair, 0, :].rearrange("p (t n) -> p t n", t=2))\
                            .then_inc(evacuated[pair], 1)
                bar()

                us = units2(la)

                def ga_out(bank, j, it):
                    return vec.tensor_copy(GA[:, 2 * j, 0:T], bank[:, 0:T])

                def rows2(u):
                    h, qt, k0, nk = us[u]
                    b = u % 2
                    v.wait_ge(sem("w_scores"), LAYER["w_scores"] * la + u + 1)
                    if u >= 2:
                        v.wait_ge(sem("w_exp"), LAYER["w_exp"] * la + 2 * (u - 1))
                    vec.tensor_reduce(STAT[:, 2 * b:2 * b + 2], scores_bank(u)[:, :, 0:nk], AX.X, ALU.max, negate=True)\
                        .then_inc(sem("w_max"), 1)

                def probs2(u):
                    h, qt, k0, nk = us[u]
                    b = u % 2
                    v.wait_ge(sem("w_exp"), LAYER["w_exp"] * la + 2 * u + 2)
                    r0, r1 = STAT[:, 8 + 2 * b:9 + 2 * b], STAT[:, 9 + 2 * b:10 + 2 * b]
                    then(vec.reciprocal(STAT[:, 8 + 2 * b:10 + 2 * b], STAT[:, 4 + 2 * b:6 + 2 * b]))
                    then(vec.tensor_tensor(r1, r1, NEG_LAM[:, la:la + 1], ALU.mult))
                    p0, p1 = AT_P[b][:, 0, 0:nk], AT_P[b][:, 1, 0:nk]
                    then(vec.tensor_scalar(p1, p1, r1, None, ALU.mult))
                    vec.scalar_tensor_tensor(p0, p0, r0, p1, ALU.mult, ALU.add).then_inc(sem("w_probs"), 1)

                def turned2(u):
                    h, qt, k0, nk = us[u]
                    b = u % 2
                    n = nk // P
                    v.wait_ge(sem("w_turns"), LAYER["w_turns"] * la + u + 1)
                    if u >= 2:
                        v.wait_ge(sem("w_out"), LAYER["w_out"] * la + u - 1)
                    vec.tensor_copy(AT_T[b][:, 0:n, :], PA[b][:, 0:nk].rearrange("p (a b) -> p a b", a=n))\
                        .then_inc(sem("w_turned"), 1)

                for u in range(len(us) + 1):
                    if u >= 1:
                        probs2(u - 1)
                    if u < len(us):
                        rows2(u)
                    if u >= 1:
                        turned2(u - 1)
                    if u < len(us):
                        beside(attention_fill(la)[u], ga_out)
                bar()
                v.wait_ge(sem("gate_open"), la + 1)
                E1 = XD[0].rearrange("p (a b) -> p a b", a=4)
                E2 = XD[1].rearrange("p (a b) -> p a b", a=4)
                v.wait_ge(sem("dt_sum"), LAYER["dt_sum"] * la + 1)
                then(vec.tensor_tensor(DT, PS[:, 0, 0:256].rearrange("p (a b) -> p a b", a=4),
                                       r_(f"dt_bias{la}").unsqueeze(1).broadcast_to([P, 4, 64]), ALU.add))
                vec.scalar_tensor_tensor(E1, DT, -1.0, DT, ALU.mult, ALU.max).then_inc(sem("dt_abs"), 1)
                v.wait_ge(sem("dt_exp"), LAYER["dt_exp"] * la + 1)
                then(vec.tensor_scalar(DT, DT, 0.0, None, ALU.max))
                vec.tensor_scalar(E2, E1, 1.0, None, ALU.add).then_inc(sem("dt_one"), 1)
                v.wait_ge(sem("dt_one"), LAYER["dt_one"] * la + 1)
                then(vec.tensor_scalar(CS, E2, -1.0, None, ALU.add))
                then(vec.tensor_tensor(CS, E1, CS, ALU.subtract))
                then(vec.reciprocal(CHD, E2))
                then(vec.tensor_tensor(CS, CS, CHD, ALU.mult))
                v.wait_ge(sem("dt_ln"), LAYER["dt_ln"] * la + 1)
                then(vec.tensor_tensor(CS, CS, WD, ALU.add))
                then(vec.tensor_tensor(DT, DT, CS, ALU.add))
                vec.tensor_tensor(DTA, DT, r_(f"a_log{la}").unsqueeze(1).broadcast_to([P, 4, 64]), ALU.mult)\
                    .then_inc(sem("dt_a"), 1)
                W0 = PARAMS[f"sconv_w{la}"][0]
                NY = 2 if la == 0 else 1

                def taps(g, tiles):
                    b = g % 2
                    if g < SSD_GROUPS:
                        for i in tiles:
                            t = i % 2
                            pair, _ = GROUPS[f"ssd{la}"][2 * g + i // 2]
                            v.wait_ge(sem("s_mid"), LAYER["s_mid"] * la + 4 * g + i + 1)
                            n = (T if i == 3 else TT) // T1
                            ch = channels(g, i)
                            for tap in (0, 1, 3, 4):
                                s_ = tap - 2
                                lo, hi = max(0, -s_), T1 - max(0, s_)
                                dst = CV[b][:, i, 0:n * T1].rearrange("p (a b) -> p a b", a=n)[:, :, lo:hi]
                                src = PB[:, pair, t, 0:n * T1].rearrange("p (a b) -> p a b", a=n)[:, :, lo + s_:hi + s_]
                                ins = vec.scalar_tensor_tensor(dst, src, par[:, W0 + 32 * tap + ch:W0 + 32 * tap + ch + 1],
                                                               dst, ALU.mult, ALU.add)
                                if tap == 4:
                                    ins.then_inc(evacuated[pair], 1)
                                else:
                                    then(ins)

                def states(g):
                    v.wait_ge(sem("s_cb"), LAYER["s_cb"] * la + g + 1)
                    for d, tri in enumerate((c_("tri_le"), c_("tri_ge"))):
                        n = T // P
                        vec.tensor_tensor(CBM[:, d, tok, :], PS[:, 1, 0:T].rearrange("p (a b) -> p a b", a=n),
                                          tri.unsqueeze(1).broadcast_to([P, n, P]), ALU.mult)\
                            .then_inc(sem("s_cbm"), 1)
                    if g >= 1:
                        times_z(g - 1)
                    for i in range(3):
                        for d, order in enumerate((F_ORDER, B_ORDER)):
                            n = 6 * g + 2 * i + d
                            t = order[i]
                            heads = slice(32 * d + 4 * g, 32 * d + 4 * g + 4)
                            v.wait_ge(sem("s_delta"), LAYER["s_delta"] * la + 6 * g + 2 * i + 2)
                            if inter_count(la, g, i - 1) > 0:
                                v.wait_ge(sem("s_inter"), LAYER["s_inter"] * la + inter_count(la, g, i - 1))
                            delta = PA[0][:, 256 * d:256 * d + 256]
                            if i == 0:
                                vec.tensor_copy(HT[d], delta).then_inc(sem("s_state"), 1)
                            else:
                                hv = HT[d].rearrange("p (a b) -> p a b", a=4)
                                v.wait_ge(sem("s_state"), LAYER["s_state"] * la + n - 1)
                                then(vec.tensor_tensor(hv, hv, CHD[:, t, heads].unsqueeze(2).broadcast_to([P, 4, HD]),
                                                       ALU.mult))
                                vec.tensor_tensor(HT[d], HT[d], delta, ALU.add).then_inc(sem("s_state"), 1)
                        for d, order in enumerate((F_ORDER, B_ORDER)):
                            t = order[i + 1]
                            if not live(la, t):
                                continue
                            heads = slice(32 * d + 4 * g, 32 * d + 4 * g + 4)
                            v.wait_ge(sem("s_inter"), LAYER["s_inter"] * la + inter_count(la, g, i))
                            v.wait_ge(sem("s_yi"), LAYER["s_yi"] * la + g + 1)
                            then(vec.tensor_tensor(YT2[d].rearrange("p (a b) -> p a b", a=4),
                                                   PA[1][:, 256 * d:256 * d + 256].rearrange("p (a b) -> p a b", a=4),
                                                   ECS[:, t, heads].unsqueeze(2).broadcast_to([P, 4, HD]), ALU.mult))
                            vec.tensor_tensor(YI[:, t, :], YI[:, t, :], YT2[d], ALU.add)\
                                .then_inc(sem("s_inter_read"), 1)

                def diff(g, r):
                    n = 4 * g + r
                    if n >= 2:
                        v.wait_ge(sem("s_within"), LAYER["s_within"] * la + n - 1)
                    for d in range(2):
                        nt = T // P
                        hh = 32 * d + 4 * g + r
                        v.wait_ge(sem("s_bc"), LAYER["s_bc"] * la + 2 * n + d + 1)
                        for t in range(nt):
                            ins = vec.tensor_scalar(MB[r % 2][:, d, t, :], PS[:, d, t * P:(t + 1) * P],
                                                    CS[:, t, hh:hh + 1], 0.0, ALU.subtract, ALU.min)
                        ins.then_inc(sem("s_diff"), 1)

                def masked(g, r):
                    n = 4 * g + r
                    for d in range(2):
                        v.wait_ge(sem("s_exp"), LAYER["s_exp"] * la + 2 * n + d + 1)
                        if r == 0:
                            v.wait_ge(sem("s_cbm"), LAYER["s_cbm"] * la + 2 * g + d + 1)
                        m = MB[r % 2][:, d, tok, :]
                        vec.tensor_tensor(m, m, CBM[:, d, tok, :], ALU.mult)\
                            .then_inc(sem("s_m"), 1)

                def sum_y(g):
                    v.wait_ge(sem("s_within"), LAYER["s_within"] * la + 4 * g + 4)
                    v.wait_ge(sem("s_inter_read"), LAYER["s_inter_read"] * la + inter_count(la, g, 2))
                    for i in range(NY):
                        vec.tensor_tensor(Y[:, 2 * i:2 * i + 2, 256 * g:256 * g + 256],
                                          PA[i].rearrange("p (a b) -> p a b", a=2),
                                          YI[:, 2 * i:2 * i + 2, :], ALU.add).then_inc(sem("s_y"), 1)

                def times_z(g):
                    v.wait_ge(sem("s_y"), LAYER["s_y"] * la + NY * (g + 1))
                    pair, before = GROUPS[f"z{la}"][g]
                    v.wait_ge(evacuated[pair], 2 * before + 2)
                    y = Y[:, tok, CHUNK * g:CHUNK * (g + 1)]
                    vec.tensor_tensor(y, y, ZT[:, 0:T // P * CHUNK].rearrange("p (a b) -> p a b", a=T // P), ALU.mult)\
                        .then_inc(sem("z_used"), 1)

                for h in range(8):
                    v.wait_ge(sem("sub_root"), LAYER["sub_root"] * la + h + 1)
                    r = SUB_R[h % 2][:, 0:T]
                    then(vec.reciprocal(r, r))
                    vec.scalar_tensor_tensor(LQ[:, h, 0:T], LQ[:, h, 0:T], p_(f"subln_g{la}"), r,
                                             ALU.mult, ALU.mult).then_inc(sem("sub_out"), 1)
                    if h == 5:
                        taps(0, (0, 1))
                taps(0, (2, 3))
                v.wait_ge(sem("dt_cs"), LAYER["dt_cs"] * la + 1)
                vec.tensor_copy(CS, PS[:, 1, 0:256].rearrange("p (a b) -> p a b", a=4)).then_inc(sem("dt_rest"), 1)
                then(vec.tensor_copy(CHD, PS[:, 1, 256:512].rearrange("p (a b) -> p a b", a=4)))
                vec.tensor_tensor(WD, CHD, CS, ALU.subtract).then_inc(sem("dt_rest"), 1)
                v.wait_ge(sem("dt_wd"), LAYER["dt_wd"] * la + 1)
                vec.tensor_tensor(WD, WD, DT, ALU.mult).then_inc(sem("dt_ready"), 1)
                v.wait_ge(sem("dt_exps"), LAYER["dt_exps"] * la + 1)
                both(v, f"attn_o{la}", lambda bank, t, j, it: vec.tensor_tensor(
                    MRG[:, 2 * j + t, 0:T], bank[:, 0:T], MRG[:, 2 * j + t, 0:T], ALU.mult))
                for g in range(SSD_GROUPS):
                    states(g)
                    taps(g + 1, (0,))
                    diff(g, 0)
                    for r in range(4):
                        masked(g, r)
                        if r < 3:
                            diff(g, r + 1)
                            taps(g + 1, (r + 1,))
                    sum_y(g)
                times_z(SSD_GROUPS - 1)
                bar()
                nt = T // P
                v.wait_ge(sem("z_root"), LAYER["z_root"] * la + 1)
                then(vec.reciprocal(STAT[:, 8:8 + nt], STAT[:, 4:4 + nt]))
                for t in range(nt):
                    vec.tensor_scalar(Y[:, t, :], Y[:, t, :], STAT[:, 8 + t:9 + t], None, ALU.mult)\
                        .then_inc(sem("z_scaled"), 1)
                for i in range(0, 16, 2):
                    v.wait_ge(sem("yt"), LAYER["yt"] * la + i + 1)
                    vec.tensor_scalar(YT[:, i, 0:T], yt_bank(i)[:, 0:T], p_(f"ssd_g{la}", i), None, ALU.mult)\
                        .then_inc(sem("yt_read0"), 1)
                for pair, before in GROUPS[f"gs{la}"]:
                    v.wait_ge(evacuated[pair], 2 * before + 2)
                for j in range(4):
                    pair, before = GROUPS[f"ssd_o{la}"][j]
                    v.wait_ge(chunk_done, CHUNKS[f"ssd_o{la}"][2 * j + 1] + 1)
                    if j:
                        v.wait_ge(sem("mixed"), LAYER["mixed"] * la + 2 * j)
                    for t in range(2):
                        vec.tensor_tensor(MIX[t][:, 0:T], PB[:, pair, t, 0:T], GS[:, 2 * j + t, 0:T], ALU.mult)\
                            .then_inc(evacuated[pair], 1)
                    for t in range(2):
                        v.wait_ge(evacuated[pair], 2 * before + t + 1)
                        m = MRG[:, 2 * j + t, 0:T]
                        vec.tensor_tensor(m, m, MIX[t][:, 0:T], ALU.add).then_inc(sem("mixed"), 1)

                def add_to(part):
                    def op(bank, t, j, it):
                        for s_ in range(halves):
                            cols = slice(s_ * T1, (s_ + 1) * T1)
                            x = one(X, 2 * j + t, 2, it)[:, cols]
                            m = mod[:, la, span(part * KT + 2 * j + t, 2, it), s_:s_ + 1].rearrange("p a b -> p (a b)")
                            ins = vec.scalar_tensor_tensor(x, bank[:, cols], m, x, ALU.mult, ALU.add)
                        return ins
                    return op

                both(v, f"out2{la}", add_to(2))
                bar()
                norm_mod(f"m2{la}", 4, halves)
                evac(v, 0, f"mlp1{la}", lambda bank, j, it: vec.tensor_scalar(one(HID2, 2 * j, 2, it)[:, 0:T], bank[:, 0:T],
                                                                            0.0, None, ALU.max))
                bar()
                both(v, f"mlp2{la}", add_to(5), 4)
                bar()
            norm_scale("final", x1, lambda k: H[:, k, 0:T1], lambda k: p_("final_g", k), T1, "h")

        @block.gpsimd
        def _(pool):
            def bar():
                barrier(pool, "pool")

            gp = nc.gpsimd
            pool.dma_start(row[:, :], rows.broadcast_to([P, N_ROWS])).then_inc(rows_in, 16)
            pool.dma_start(REL[0:36, 0:N_BIAS], rel_bias).then_inc(sem("hot"), 16)
            pool.dma_start(HOT[0:36, :], rev_hot).then_inc(sem("hot"), 16)
            pool.dma_start(wdt[:, :, :, :], w_dt).then_inc(wdt_in, 16)
            pool.wait_ge(loaded, 16 * 2)
            pool.wait_ge(sem("rev"), 1)
            pool.dma_start(scratch, REV[0:N_BIAS, :]).then_inc(sem("rev_out"), 16)
            pool.wait_ge(sem("rev_out"), 16)
            pool.dma_start(BIAS_UP, bass.AP(scratch.tensor, 0, [[1, P], [N_REV, N_BIAS], [1, 256]]))\
                .then_inc(sem("bias_in"), 16)
            pool.wait_ge(sem("bias_in"), 16)
            bar()
            bar()
            bar()
            for j in range(4):
                pair, before = GROUPS["branches"][j]
                pool.wait_ge(evacuated[pair], 2 * before + 2)
                to = GATE[:, 2 * j:2 * j + 2, :]
                for i in (1, 2):
                    gp.tensor_tensor(to, to, GATE[:, 8 * i + 2 * j:8 * i + 2 * j + 2, :], ALU.add)\
                        .then_inc(sem("merged"), 1)
                    pool.wait_ge(sem("merged"), 2 * j + i)
            bar()
            bar()
            bar()
            c0 = CHUNKS["up"][0]

            def up(it):
                for i in range(2):
                    pair, before = GROUPS["up"][2 * i + 1]
                    pool.wait_ge(sem("up_gelu"), 2 * it + i + 1)
                    pool.wait_ge(evacuated[pair], 2 * before + 2 + 4 * it)
                    gp.tensor_tensor(one(HID1_PAIRS, i, 2, it), UP[:, i, 0, :], UP[:, i, 1, :], ALU.mult)\
                        .then_inc(sem("up_prod"), 1)
            repeat(pool, 8, up)
            bar()
            bar()
            bar()
            for la in range(DEPTH_2):
                T = TT if la == 0 else T1
                for i in range(2 * KT):
                    pool.wait_ge(sem("rot"), LAYER["rot"] * la + i + 1)
                    x = (LQ if i < KT else LK)[:, i % KT, 0:T1]
                    gp.tensor_tensor(x, x, c_("cos"), ALU.mult).then_inc(sem("rot_cos"), 1)
                bar()
                bar()
                for h in range(8):
                    if h >= 2:
                        pool.wait_ge(sem("sub_sum"), LAYER["sub_sum"] * la + h - 1)
                    gp.tensor_tensor(SUB_S[h % 2][:, 0:T], LQ[:, h, 0:T], LQ[:, h, 0:T], ALU.mult)\
                        .then_inc(sem("sub_sq"), 1)
                NY = 2 if la == 0 else 1
                pool.wait_ge(sem("dt_ready"), LAYER["dt_ready"] * la + 1)

                for g in range(SSD_GROUPS):
                    pool.wait_ge(sem("s_turned"), LAYER["s_turned"] * la + 3 * g + 2)
                    for i in range(3):
                        for d, order in enumerate((F_ORDER, B_ORDER)):
                            n = 6 * g + 2 * i + d
                            t = order[i]
                            if n >= 2:
                                pool.wait_ge(sem("s_delta"), LAYER["s_delta"] * la + n - 1)
                            heads = slice(32 * d + 4 * g, 32 * d + 4 * g + 4)
                            gp.tensor_tensor(XD[d].rearrange("p (a b) -> p a b", a=4),
                                             XG[:, t, :].rearrange("p (a b) -> p a b", a=4),
                                             WD[:, t, heads].unsqueeze(2).broadcast_to([P, 4, HD]), ALU.mult)\
                                .then_inc(sem("s_xd"), 1)
                        if i == 0:
                            if g >= 1:
                                pool.wait_ge(sem("s_y"), LAYER["s_y"] * la + NY * g)
                            gp.tensor_tensor(YI.rearrange("p t (r n) -> p t r n", r=4), XG.rearrange("p t (r n) -> p t r n", r=4),
                                             r_(f"ssd_d{la}", 4 * g, 4).unsqueeze(1).unsqueeze(3).broadcast_to([P, 4, 4, HD]),
                                             ALU.mult).then_inc(sem("s_yi"), 1)
                    for r in range(4):
                        n = 4 * g + r
                        if n >= 2:
                            pool.wait_ge(sem("s_within"), LAYER["s_within"] * la + n - 1)
                        for d in range(2):
                            hh = 32 * d + 4 * g + r
                            gp.tensor_tensor(XC[r % 2][:, d, :, :], XG[:, :, HD * r:HD * r + HD],
                                             DT[:, :, hh:hh + 1].broadcast_to([P, 4, HD]), ALU.mult)\
                                .then_inc(sem("s_xc"), 1)
                bar()
                bar()
                n = len(CHUNKS[f"mlp1{la}"])

                def square(it):
                    for j in range(4):
                        pair, before = GROUPS[f"mlp1{la}"][j]
                        pool.wait_ge(evacuated[pair], 2 * before + 2 + 4 * it)
                        hh = HID2[:, span2(j, 4, it), 0:T]
                        gp.tensor_tensor(hh, hh, hh, ALU.mult)
                repeat(pool, n // 4, square)
                bar()
                bar()


def _weights(w):
    K, N = w.shape
    return w.reshape(K // D, KT, P, N // CHUNK, CHUNK).transpose(3, 0, 2, 1, 4).reshape(-1, P, KT, CHUNK)


def _stream(a):
    w = a["w_in"][0]
    perm = [HD * h + i for t in range(4) for h in (t, t + 4) for i in range(HD)]
    c = {}
    c["a_qk"] = _weights(w[:, 0:1536])
    c["a_v"] = _weights(w[:, 1536:2304])
    c["b_q"] = _weights(w[:, 2304:2816][:, perm])
    c["b_kv"] = _weights(w[:, 2816:3072])
    c["c_qk"] = _weights(w[:, 3072:3584])
    c["c_v"] = _weights(w[:, 3584:3840])
    c["gates"] = _weights(w[:, 3840:6912])
    c["branches"] = _weights(np.concatenate([a["w_br_a"][0], a["w_br_b"][0][perm], a["w_br_c"][0]], 0))
    c["out"] = _weights(a["w_out"][0])
    up = _weights(a["w_up"][0])
    c["up"] = np.stack([up[:16], up[16:]], 1).reshape(32, P, KT, CHUNK)
    c["down"] = _weights(a["w_down"][0])
    for la in range(DEPTH_2):
        w = a["w_in_2"][la]
        c[f"ada{la}"] = _weights(a["ada_w_2"][la])
        c[f"q{la}"] = _weights(w[:, 0:1024])
        c[f"k{la}"] = _weights(w[:, 1024:2048])
        c[f"v{la}"] = _weights(w[:, 2048:3072])
        c[f"z{la}"] = _weights(w[:, 3072:5120])
        xs, b, cc = w[:, 5120:7168], w[:, 7168:8192], w[:, 8192:9216]
        parts = []
        for g in range(SSD_GROUPS):
            parts += [xs[:, 256 * g:256 * g + 256], b[:, P * g:P * g + P], cc[:, P * g:P * g + P]]
        c[f"ssd{la}"] = _weights(np.concatenate(parts, 1))
        c[f"ga{la}"] = _weights(w[:, 9280:10304])
        c[f"gs{la}"] = _weights(w[:, 10304:11328])
        c[f"attn_o{la}"] = _weights(a["w_attn_o_2"][la])
        c[f"ssd_o{la}"] = _weights(a["w_ssd_o_2"][la])
        c[f"out2{la}"] = _weights(a["w_out_2"][la])
        c[f"mlp1{la}"] = _weights(a["w_mlp1_2"][la])
        c[f"mlp2{la}"] = _weights(a["w_mlp2_2"][la])
    out = np.empty((N_CHUNKS, P, KT, CHUNK), np.float32)
    for name, at in CHUNKS.items():
        assert len(c[name]) == len(at), name
        out[at] = c[name]
    return out


def _columns(v):
    return np.ascontiguousarray(v).reshape(-1, P).T


def _params(a):
    c = {"pre_g": a["attn_pre_norm"], "post_g": a["attn_post_norm"], "ffn_pre_g": a["ffn_pre_norm"],
         "ffn_post_g": a["ffn_post_norm"], "b_gate": a["b_gate"], "conv_w": a["conv_w"], "conv_b": a["conv_b"],
         "final_g": a["final_norm_g_2"], "cvec": np.stack([a["c_2"][0], a["c_ctx_2"]])}
    for la in range(DEPTH_2):
        c |= {f"ada_b{la}": a["ada_b_2"][la], f"mix_g{la}": a["norm_mix_g_2"][la], f"sconv_w{la}": a["conv_w_2"][la],
              f"sconv_b{la}": a["conv_b_2"][la], f"subln_g{la}": a["attn_subln_g_2"][la],
              f"ssd_g{la}": a["ssd_norm_g_2"][la], f"mlp_g{la}": a["norm_mlp_g_2"][la]}
    return np.concatenate([_columns(c[name]) for name in PARAMS], 1)


def _rows(a):
    c = {"sinks": a["sinks"]}
    for la in range(DEPTH_2):
        c |= {f"dt_bias{la}": np.concatenate([a["dt_bias_f_2"][la], a["dt_bias_b_2"][la]]),
              f"a_log{la}": np.concatenate([a["a_log_f_2"][la], a["a_log_b_2"][la]]), f"ssd_d{la}": a["ssd_d_2"][la],
              f"lam_q{la}": np.concatenate([a["lambda_q1_2"][la], a["lambda_q2_2"][la]]),
              f"lam_k{la}": np.concatenate([a["lambda_k1_2"][la], a["lambda_k2_2"][la]])}
    return np.concatenate([c[name].reshape(1, -1) for name in ROWS], 1)


def _consts():
    i = np.arange(P)
    before = np.zeros((P, 2 * P), np.float32)
    before[:, :P] = 1
    before[:, P:] = i[None, :] < i[:, None]
    rot = np.zeros((P, P), np.float32)
    for m in range(P):
        if m % HD < HD // 2:
            rot[m + HD // 2, m] = -1
        else:
            rot[m - HD // 2, m] = 1
    t = np.arange(T1)
    inv = np.float32(10000.0) ** (-np.arange(HD // 4, dtype=np.float32) / (HD // 4))
    ang = np.concatenate([(t // GRID_W).astype(np.float32)[:, None] * inv,
                          (t % GRID_W).astype(np.float32)[:, None] * inv], 1)
    wide = lambda x: np.tile(x.T, (4, 1))
    c = {"ident": np.eye(P), "tri_le": i[:, None] <= i[None, :], "tri_ge": i[:, None] >= i[None, :], "rot": rot,
         "flip": np.eye(P)[::-1], "sel": (i[:, None] % 32) == np.arange(2)[None, :],
         "cos": wide(np.cos(ang)), "sin": wide(np.sin(ang)), "c_before": before, "c_after": 1 - before}
    return np.concatenate([np.asarray(c[name], np.float32) for name in CONSTS], 1)


def _hot():
    dist = (N_REV // 3 * 2 - 1) - np.arange(N_REV)
    far = np.maximum(dist, 1).astype(np.float32)
    large = 16 + (np.log(far / np.float32(16)) / np.float32(math.log(2048 / 16)) * np.float32(16)).astype(np.int32)
    bucket = np.where(dist < 16, np.maximum(dist, 0), np.minimum(large, 31))
    hot = np.zeros((36, N_REV), np.float32)
    hot[bucket, np.arange(N_REV)] = 1
    seen = [dist <= 128, dist % 4 == 0, dist % 16 == 0, dist <= 127]
    for i, s in enumerate(seen):
        hot[32 + i] = ~(s & (dist >= 0))
    return hot


def kernel(**inputs):
    import concourse.bacc as _bacc
    from concourse.bass_utils import run_bass_kernel_spmd as _run

    a = {k: np.asarray(v) for k, v in inputs.items()}
    x = np.concatenate([a["x"][0], a["ctx_2"][0]], 0)
    rel = np.zeros((36, N_BIAS), np.float32)
    rel[:32] = a["rel_bias"]
    for i in range(3):
        rel[32 + i, 4 * i:4 * i + 4] = NEG
    rel[35, 12:] = NEG
    w_dt = np.stack([w[:, 9216:9280].reshape(KT, P, 64).transpose(1, 0, 2) for w in a["w_in_2"]], 1)
    arrays = {
        "xT": x.T.reshape(KT, P, TT).transpose(1, 0, 2), "stream": _stream(a), "params": _params(a),
        "rows": _rows(a), "consts": _consts(), "rel_bias": rel, "rev_hot": _hot(), "w_dt": w_dt,
    }
    arrays = {k: np.ascontiguousarray(v, dtype=np.float32) for k, v in arrays.items()}
    nc = _bacc.Bacc("TRN2", target_bir_lowering=False, num_devices=1)
    args = [nc.dram_tensor(k, v.shape, F32, kind="ExternalInput").ap() for k, v in arrays.items()]
    args.append(nc.dram_tensor("scratch", (N_BIAS, N_REV), F32).ap())
    args.append(nc.dram_tensor("out", (P, KT, T1), F32, kind="ExternalOutput").ap())
    program(nc, *args)
    r = _run(nc, [arrays], core_ids=[0])
    y = np.asarray(r.results[0]["out"])
    return y.transpose(2, 1, 0).reshape(1, T1, D)
```
